# Optimizing a Trainium2 kernel written in Bass

```python
import math
import jax, jax.numpy as jnp
from jax import lax
import numpy as np

D_MODEL = 1024
BATCH = 1
SEQ = 512
DEPTH = 1

HEAD_DIM = 128
HEADS_PER_GROUP = 4
ATTN_GROUPS = ((128, 1), (512, 4), (2048, 16))
N_ATTN_GROUPS = len(ATTN_GROUPS)
ATTN_HEADS = HEADS_PER_GROUP * N_ATTN_GROUPS
ATTN_QK_WIDTH = ATTN_HEADS * HEAD_DIM
ATTN_OUT_WIDTH = HEADS_PER_GROUP * HEAD_DIM
BLOCK = 128
ROPE_THETA = 500000.0
ROPE_DIM = HEAD_DIM // 4
SSM_WIDTH = 512
SSM_GROUP = 16
SSM_GROUPS = SSM_WIDTH // SSM_GROUP
SSM_STATE = 64
DT_MIN = 0.001
DT_MAX = 0.1
D_FF = -(-8 * D_MODEL // (3 * 256)) * 256
PLE_DIM = 256
EPS = 1e-6
IN_WIDTH = 3 * ATTN_QK_WIDTH + SSM_WIDTH + 2 * D_MODEL


def rmsnorm(x, g):
    xf = x.astype(jnp.float32)
    y = xf * lax.rsqrt(jnp.mean(xf * xf, axis=-1, keepdims=True) + EPS)
    return (y * g.astype(jnp.float32)).astype(x.dtype)

def partial_rotary(x, positions):
    half = ROPE_DIM // 2
    inv_freq = ROPE_THETA ** (-jnp.arange(half, dtype=jnp.float32) * 2.0 / ROPE_DIM)
    ang = positions.astype(jnp.float32)[..., None] * inv_freq
    cos = jnp.cos(ang)[:, :, None, :]
    sin = jnp.sin(ang)[:, :, None, :]
    xr = x[..., :ROPE_DIM].astype(jnp.float32)
    x1, x2 = xr[..., :half], xr[..., half:]
    rot = jnp.concatenate([x1 * cos - x2 * sin, x2 * cos + x1 * sin], axis=-1).astype(x.dtype)
    return jnp.concatenate([rot, x[..., ROPE_DIM:]], axis=-1)

def dilated_band_attention(q, k, v, dilation, band):
    B, S, H, Dh = q.shape
    L = S // dilation
    Lp = -(-L // BLOCK) * BLOCK
    nb = Lp // BLOCK

    def to_sub(t):
        t = jnp.moveaxis(t.reshape(B, L, dilation, H, Dh), 2, 1)
        t = jnp.pad(t, ((0, 0), (0, 0), (0, Lp - L), (0, 0), (0, 0)))
        return t.reshape(B, dilation, nb, BLOCK, H, Dh)

    def with_prev(t):
        prev = jnp.pad(t, ((0, 0), (0, 0), (1, 0), (0, 0), (0, 0), (0, 0)))[:, :, :-1]
        return jnp.concatenate([prev, t], axis=3)

    def from_sub(t):
        rest = t.shape[4:]
        t = t.reshape((B, dilation, Lp) + rest)[:, :, :L]
        return jnp.moveaxis(t, 1, 2).reshape((B, S) + rest)

    qb = to_sub(q)
    kk = with_prev(to_sub(k))
    vv = with_prev(to_sub(v))
    scale = 1.0 / math.sqrt(Dh)
    s = jnp.einsum('brnqhd,brnkhd->brnhqk', qb, kk,
                   preferred_element_type=jnp.float32) * scale
    qi = jnp.arange(BLOCK)[:, None]
    kj = jnp.arange(2 * BLOCK)[None, :]
    rel = BLOCK + qi - kj
    in_band = (rel >= 0) & (rel <= band)
    not_first = (jnp.arange(nb) > 0)[:, None, None]
    valid = in_band[None] & (not_first | (kj >= BLOCK)[None])
    s = jnp.where(valid[None, None, :, None], s, -jnp.inf)
    m = jnp.max(s, axis=-1, keepdims=True)
    pexp = jnp.exp(s - m)
    den = jnp.sum(pexp, axis=-1, keepdims=True)
    o = jnp.einsum('brnhqk,brnkhd->brnqhd', pexp, vv.astype(jnp.float32))
    o = o / jnp.swapaxes(den[..., 0], -1, -2)[..., None]
    lse = jnp.swapaxes(m[..., 0] + jnp.log(den[..., 0]), -1, -2)
    return from_sub(o), from_sub(lse)

def _complex_affine_combine(e1, e2):
    a1r, a1i, b1r, b1i = e1
    a2r, a2i, b2r, b2i = e2
    ar = a1r * a2r - a1i * a2i
    ai = a1r * a2i + a1i * a2r
    br = a2r * b1r - a2i * b1i + b2r
    bi = a2r * b1i + a2i * b1r + b2i
    return (ar, ai, br, bi)

def s5_ssm(u, a_re, a_im, log_dt, b_re, b_im, c_re, c_im, d_skip):
    B, S, _ = u.shape
    uf = u.astype(jnp.float32).reshape(B, S, SSM_GROUPS, SSM_GROUP)
    dt = jnp.exp(log_dt.astype(jnp.float32))[:, None]
    lr = a_re.astype(jnp.float32)
    li = a_im.astype(jnp.float32)
    mag = jnp.exp(lr * dt)
    bar_re = mag * jnp.cos(li * dt)
    bar_im = mag * jnp.sin(li * dt)
    nr = bar_re - 1.0
    ni = bar_im
    den = lr * lr + li * li
    z_re = (nr * lr + ni * li) / den
    z_im = (ni * lr - nr * li) / den
    br_ = b_re.astype(jnp.float32)
    bi_ = b_im.astype(jnp.float32)
    bb_re = z_re[..., None] * br_ - z_im[..., None] * bi_
    bb_im = z_re[..., None] * bi_ + z_im[..., None] * br_
    bu_re = jnp.einsum('bsgc,gpc->bsgp', uf, bb_re)
    bu_im = jnp.einsum('bsgc,gpc->bsgp', uf, bb_im)
    ar = jnp.broadcast_to(bar_re, bu_re.shape)
    ai = jnp.broadcast_to(bar_im, bu_im.shape)
    _, _, h_re, h_im = lax.associative_scan(_complex_affine_combine, (ar, ai, bu_re, bu_im), axis=1)
    y = (jnp.einsum('bsgp,gcp->bsgc', h_re, c_re.astype(jnp.float32))
         - jnp.einsum('bsgp,gcp->bsgc', h_im, c_im.astype(jnp.float32))
         + d_skip.astype(jnp.float32) * uf)
    return y.reshape(B, S, SSM_WIDTH).astype(u.dtype)

def hybrid_layer(h, p_l, positions, g_mix, w_in, a_re, a_im, log_dt, b_re, b_im, c_re, c_im,
                 d_skip, w_attn_proj, w_glu_a, w_glu_b, w_out, g_ffn, w_ffn_gate, w_ffn_up,
                 w_ffn_down, w_ple_gate, w_ple_proj):
    B, S, _ = h.shape
    n = rmsnorm(h, g_mix)
    z = n @ w_in
    o0 = ATTN_QK_WIDTH
    q = z[..., 0:o0].reshape(B, S, ATTN_HEADS, HEAD_DIM)
    k = z[..., o0:2 * o0].reshape(B, S, ATTN_HEADS, HEAD_DIM)
    v = z[..., 2 * o0:3 * o0].reshape(B, S, ATTN_HEADS, HEAD_DIM)
    o1 = 3 * o0
    u = z[..., o1:o1 + SSM_WIDTH]
    o2 = o1 + SSM_WIDTH
    gate_attn = jax.nn.sigmoid(z[..., o2:o2 + D_MODEL])
    gate_ssm = jax.nn.sigmoid(z[..., o2 + D_MODEL:o2 + 2 * D_MODEL])

    q = partial_rotary(q, positions)
    k = partial_rotary(k, positions)
    outs = []
    lses = []
    for gi, (window, dilation) in enumerate(ATTN_GROUPS):
        hs = slice(gi * HEADS_PER_GROUP, (gi + 1) * HEADS_PER_GROUP)
        o_g, l_g = dilated_band_attention(q[:, :, hs], k[:, :, hs], v[:, :, hs],
                                          dilation, window // dilation)
        outs.append(o_g)
        lses.append(l_g)
    wts = jax.nn.softmax(jnp.stack(lses, axis=0), axis=0)
    attn = jnp.sum(wts[..., None] * jnp.stack(outs, axis=0), axis=0)
    attn_d = attn.reshape(B, S, ATTN_OUT_WIDTH).astype(h.dtype) @ w_attn_proj

    y = jax.nn.gelu(s5_ssm(u, a_re, a_im, log_dt, b_re, b_im, c_re, c_im, d_skip))
    ssm_d = (y @ w_glu_a) * jax.nn.sigmoid(y @ w_glu_b)

    h = h + (gate_attn * attn_d + gate_ssm * ssm_d) @ w_out

    n2 = rmsnorm(h, g_ffn)
    h = h + (jax.nn.silu(n2 @ w_ffn_gate) * (n2 @ w_ffn_up)) @ w_ffn_down

    h = h + jax.nn.sigmoid(h @ w_ple_gate) * (p_l.astype(h.dtype) @ w_ple_proj)
    return h

def first_inputs(seed: int = 0) -> dict:
    key = jax.random.key(seed)
    ks = jax.random.split(key, 26)
    f32 = jnp.float32

    def nrm(k, shape, fan_in):
        return jax.random.normal(k, shape, f32) * (fan_in ** -0.5)

    x = jax.random.normal(ks[0], (BATCH, SEQ, D_MODEL), f32)
    p = jax.random.normal(ks[1], (DEPTH, BATCH, SEQ, PLE_DIM), f32)
    positions = jnp.broadcast_to(jnp.arange(SEQ, dtype=jnp.int32)[None, :], (BATCH, SEQ))
    g_mix = 1.0 + 0.05 * jax.random.normal(ks[2], (DEPTH, D_MODEL), f32)
    w_in = nrm(ks[3], (DEPTH, D_MODEL, IN_WIDTH), D_MODEL)
    a_re = -0.5 + 0.01 * jax.random.normal(ks[4], (DEPTH, SSM_GROUPS, SSM_STATE), f32)
    a_im = (jnp.pi * jnp.arange(SSM_STATE, dtype=f32)[None, None, :]
            + 0.01 * jax.random.normal(ks[5], (DEPTH, SSM_GROUPS, SSM_STATE), f32))
    log_dt = jax.random.uniform(ks[6], (DEPTH, SSM_GROUPS), f32,
                                minval=math.log(DT_MIN), maxval=math.log(DT_MAX))
    b_re = nrm(ks[7], (DEPTH, SSM_GROUPS, SSM_STATE, SSM_GROUP), 2 * SSM_GROUP)
    b_im = nrm(ks[8], (DEPTH, SSM_GROUPS, SSM_STATE, SSM_GROUP), 2 * SSM_GROUP)
    c_re = nrm(ks[9], (DEPTH, SSM_GROUPS, SSM_GROUP, SSM_STATE), SSM_STATE)
    c_im = nrm(ks[10], (DEPTH, SSM_GROUPS, SSM_GROUP, SSM_STATE), SSM_STATE)
    d_skip = jax.random.normal(ks[11], (DEPTH, SSM_GROUPS, SSM_GROUP), f32)
    w_attn_proj = nrm(ks[12], (DEPTH, ATTN_OUT_WIDTH, D_MODEL), ATTN_OUT_WIDTH)
    w_glu_a = nrm(ks[13], (DEPTH, SSM_WIDTH, D_MODEL), SSM_WIDTH)
    w_glu_b = nrm(ks[14], (DEPTH, SSM_WIDTH, D_MODEL), SSM_WIDTH)
    w_out = nrm(ks[15], (DEPTH, D_MODEL, D_MODEL), D_MODEL)
    g_ffn = 1.0 + 0.05 * jax.random.normal(ks[16], (DEPTH, D_MODEL), f32)
    w_ffn_gate = nrm(ks[17], (DEPTH, D_MODEL, D_FF), D_MODEL)
    w_ffn_up = nrm(ks[18], (DEPTH, D_MODEL, D_FF), D_MODEL)
    w_ffn_down = nrm(ks[19], (DEPTH, D_FF, D_MODEL), D_FF)
    w_ple_gate = nrm(ks[20], (DEPTH, D_MODEL, D_MODEL), D_MODEL)
    w_ple_proj = nrm(ks[21], (DEPTH, PLE_DIM, D_MODEL), PLE_DIM)
    g_final = 1.0 + 0.05 * jax.random.normal(ks[22], (D_MODEL,), f32)
    return {"x": x, "p": p, "positions": positions, "g_mix": g_mix, "w_in": w_in,
            "a_re": a_re, "a_im": a_im, "log_dt": log_dt, "b_re": b_re, "b_im": b_im,
            "c_re": c_re, "c_im": c_im, "d_skip": d_skip, "w_attn_proj": w_attn_proj,
            "w_glu_a": w_glu_a, "w_glu_b": w_glu_b, "w_out": w_out, "g_ffn": g_ffn,
            "w_ffn_gate": w_ffn_gate, "w_ffn_up": w_ffn_up, "w_ffn_down": w_ffn_down,
            "w_ple_gate": w_ple_gate, "w_ple_proj": w_ple_proj, "g_final": g_final}

def first_block(x, p, positions, g_mix, w_in, a_re, a_im, log_dt, b_re, b_im, c_re, c_im, d_skip,
              w_attn_proj, w_glu_a, w_glu_b, w_out, g_ffn, w_ffn_gate, w_ffn_up, w_ffn_down,
              w_ple_gate, w_ple_proj, g_final):
    h = x
    for i in range(DEPTH):
        h = hybrid_layer(h, p[i], positions, g_mix[i], w_in[i], a_re[i], a_im[i], log_dt[i],
                         b_re[i], b_im[i], c_re[i], c_im[i], d_skip[i], w_attn_proj[i],
                         w_glu_a[i], w_glu_b[i], w_out[i], g_ffn[i], w_ffn_gate[i], w_ffn_up[i],
                         w_ffn_down[i], w_ple_gate[i], w_ple_proj[i])
    return rmsnorm(h, g_final)


D_RNN = 1280
RNN_BLOCK = 64
N_RNN_BLOCKS = D_RNN // RNN_BLOCK
CONV_WIDTH = 4
LRU_C = 8.0
N_HEADS_MLA = 16
QK_NOPE = 64
QK_ROPE = 32
V_HEAD = 64
Q_LORA = 384
KV_LORA = 256
ROPE_THETA_2 = 10000.0
Q_BLOCK = 128
D_FF_2 = 2816
FFN_CONV = 3
D_IN = D_RNN + Q_LORA + KV_LORA + QK_ROPE + 2 * D_MODEL


def rmsnorm_2(x, g):
    xf = x.astype(jnp.float32)
    y = xf * lax.rsqrt(jnp.mean(xf * xf, axis=-1, keepdims=True) + EPS)
    return (y * g.astype(jnp.float32)).astype(x.dtype)

def causal_dwconv(x, w, b):
    K = w.shape[0]
    S = x.shape[1]
    xp = jnp.pad(x, ((0, 0), (K - 1, 0), (0, 0)))
    y = xp[:, 0:S] * w[0]
    for k in range(1, K):
        y = y + xp[:, k:k + S] * w[k]
    return y + b

def rotary(x, positions):
    half = QK_ROPE // 2
    inv_freq = ROPE_THETA_2 ** (-jnp.arange(half, dtype=jnp.float32) / half)
    ang = positions.astype(jnp.float32)[..., None] * inv_freq
    ang = ang.reshape(ang.shape[:2] + (1,) * (x.ndim - 3) + (half,))
    cos, sin = jnp.cos(ang), jnp.sin(ang)
    xf = x.astype(jnp.float32)
    x1, x2 = xf[..., :half], xf[..., half:]
    out = jnp.concatenate([x1 * cos - x2 * sin, x2 * cos + x1 * sin], axis=-1)
    return out.astype(x.dtype)

def rg_lru(xc, positions, w_a, b_a, w_x, b_x, lru_param):
    B, S, W = xc.shape
    xb = xc.reshape(B, S, N_RNN_BLOCKS, RNN_BLOCK)
    r = jax.nn.sigmoid(jnp.einsum('bsnd,nde->bsne', xb, w_a).reshape(B, S, W) + b_a)
    i = jax.nn.sigmoid(jnp.einsum('bsnd,nde->bsne', xb, w_x).reshape(B, S, W) + b_x)
    log_a = -LRU_C * r.astype(jnp.float32) * jax.nn.softplus(-lru_param.astype(jnp.float32))
    a = jnp.exp(log_a)
    mult = jnp.sqrt(-jnp.expm1(2.0 * log_a))
    reset = (positions == 0)[..., None]
    a = jnp.where(reset, 0.0, a)
    mult = jnp.where(reset, 1.0, mult)
    bterm = mult * (i * xc).astype(jnp.float32)

    def combine(lhs, rhs):
        a1, b1 = lhs
        a2, b2 = rhs
        return a1 * a2, a2 * b1 + b2

    _, h = lax.associative_scan(combine, (a, bterm), axis=1)
    return h.astype(xc.dtype)

def causal_block_attention(q, k, v):
    B, S, H, Dk = q.shape
    Dv = v.shape[-1]
    nb = S // Q_BLOCK
    scale = 1.0 / math.sqrt(Dk)
    qb = q.reshape(B, nb, Q_BLOCK, H, Dk).transpose(1, 0, 2, 3, 4)
    kpos = jnp.arange(S)

    def one_block(args):
        qi, blk = args
        s = jnp.einsum('bqhd,bkhd->bhqk', qi, k).astype(jnp.float32) * scale
        qpos = blk * Q_BLOCK + jnp.arange(Q_BLOCK)
        mask = kpos[None, :] <= qpos[:, None]
        s = jnp.where(mask[None, None], s, -jnp.inf)
        p = jax.nn.softmax(s, axis=-1).astype(v.dtype)
        return jnp.einsum('bhqk,bkhd->bqhd', p, v)

    o = lax.map(one_block, (qb, jnp.arange(nb)))
    return o.transpose(1, 0, 2, 3, 4).reshape(B, S, H * Dv)

def second_inputs(seed: int = 0) -> dict:
    key = jax.random.key(seed)
    ks = jax.random.split(key, 32)

    def nrm(k, shape, fan_in, mult=1.0):
        return jax.random.normal(k, shape, jnp.float32) * (mult * fan_in ** -0.5)

    def gain(k, shape):
        return 1.0 + 0.02 * jax.random.normal(k, shape, jnp.float32)

    def bias(k, shape):
        return 0.01 * jax.random.normal(k, shape, jnp.float32)

    L = DEPTH
    a0 = jax.random.uniform(ks[10], (L, D_RNN), jnp.float32, 0.9, 0.999)
    s0 = a0 ** (1.0 / LRU_C)
    lru_param = jnp.log(s0) - jnp.log1p(-s0)
    positions = (jnp.arange(SEQ, dtype=jnp.int32)[None, :]
                 + jax.random.randint(ks[31], (BATCH, 1), 0, SEQ, dtype=jnp.int32))
    return {
        "x": jax.random.normal(ks[0], (BATCH, SEQ, D_MODEL), jnp.float32),
        "c": jax.random.normal(ks[1], (BATCH, D_MODEL), jnp.float32),
        "positions": positions,
        "w_ada": nrm(ks[2], (L, D_MODEL, 6 * D_MODEL), D_MODEL, 0.5),
        "b_ada": bias(ks[3], (L, 6 * D_MODEL)),
        "norm1_g": gain(ks[4], (L, D_MODEL)),
        "w_in": nrm(ks[5], (L, D_MODEL, D_IN), D_MODEL),
        "conv_w": nrm(ks[6], (L, CONV_WIDTH, D_RNN), CONV_WIDTH),
        "conv_b": bias(ks[7], (L, D_RNN)),
        "w_gate_a": nrm(ks[8], (L, N_RNN_BLOCKS, RNN_BLOCK, RNN_BLOCK), RNN_BLOCK),
        "b_gate_a": bias(ks[9], (L, D_RNN)),
        "w_gate_x": nrm(ks[11], (L, N_RNN_BLOCKS, RNN_BLOCK, RNN_BLOCK), RNN_BLOCK),
        "b_gate_x": bias(ks[12], (L, D_RNN)),
        "lru_param": lru_param,
        "q_norm_g": gain(ks[13], (L, Q_LORA)),
        "w_uq": nrm(ks[14], (L, Q_LORA, N_HEADS_MLA * (QK_NOPE + QK_ROPE)), Q_LORA),
        "kv_norm_g": gain(ks[15], (L, KV_LORA)),
        "w_ukv": nrm(ks[16], (L, KV_LORA, N_HEADS_MLA * (QK_NOPE + V_HEAD)), KV_LORA),
        "w_proj_rnn": nrm(ks[17], (L, D_RNN, D_MODEL), D_RNN),
        "w_proj_mla": nrm(ks[18], (L, N_HEADS_MLA * V_HEAD, D_MODEL), N_HEADS_MLA * V_HEAD),
        "w_out": nrm(ks[19], (L, D_MODEL, D_MODEL), D_MODEL),
        "norm2_g": gain(ks[20], (L, D_MODEL)),
        "w_up": nrm(ks[21], (L, D_MODEL, 2 * D_FF_2), D_MODEL),
        "ffn_conv_w": nrm(ks[22], (L, FFN_CONV, 2 * D_FF_2), FFN_CONV),
        "ffn_conv_b": bias(ks[23], (L, 2 * D_FF_2)),
        "w_down": nrm(ks[24], (L, D_FF_2, D_MODEL), D_FF_2),
        "final_g": gain(ks[25], (D_MODEL,)),
    }

def second_block(x, c, positions, w_ada, b_ada, norm1_g, w_in, conv_w, conv_b,
              w_gate_a, b_gate_a, w_gate_x, b_gate_x, lru_param, q_norm_g, w_uq,
              kv_norm_g, w_ukv, w_proj_rnn, w_proj_mla, w_out, norm2_g, w_up,
              ffn_conv_w, ffn_conv_b, w_down, final_g):
    B, S, D = x.shape
    H = N_HEADS_MLA
    c_act = jax.nn.silu(c)
    for l in range(DEPTH):
        mod = c_act @ w_ada[l] + b_ada[l]
        shift1, scale1, gate1, shift2, scale2, gate2 = [m[:, None, :] for m in jnp.split(mod, 6, axis=-1)]

        h = rmsnorm_2(x, norm1_g[l]) * (1.0 + scale1) + shift1
        proj = h @ w_in[l]
        o0 = D_RNN
        o1 = o0 + Q_LORA
        o2 = o1 + KV_LORA
        o3 = o2 + QK_ROPE
        o4 = o3 + D_MODEL
        x_rnn, q_lat, kv_lat, k_rope, g_rnn, g_mla = (
            proj[..., :o0], proj[..., o0:o1], proj[..., o1:o2],
            proj[..., o2:o3], proj[..., o3:o4], proj[..., o4:])

        xc = causal_dwconv(x_rnn, conv_w[l], conv_b[l])
        y_rnn = rg_lru(xc, positions, w_gate_a[l], b_gate_a[l], w_gate_x[l], b_gate_x[l], lru_param[l])

        q = (rmsnorm_2(q_lat, q_norm_g[l]) @ w_uq[l]).reshape(B, S, H, QK_NOPE + QK_ROPE)
        q_rope = rotary(q[..., QK_NOPE:], positions)
        q = jnp.concatenate([q[..., :QK_NOPE], q_rope], axis=-1)
        kv = (rmsnorm_2(kv_lat, kv_norm_g[l]) @ w_ukv[l]).reshape(B, S, H, QK_NOPE + V_HEAD)
        k_nope, v = kv[..., :QK_NOPE], kv[..., QK_NOPE:]
        k_r = jnp.broadcast_to(rotary(k_rope, positions)[:, :, None, :], (B, S, H, QK_ROPE))
        k = jnp.concatenate([k_nope, k_r], axis=-1)
        y_mla = causal_block_attention(q, k, v)

        merged = (jax.nn.sigmoid(g_rnn) * (y_rnn @ w_proj_rnn[l])
                  + jax.nn.sigmoid(g_mla) * (y_mla @ w_proj_mla[l]))
        x = x + gate1 * (merged @ w_out[l])

        h2 = rmsnorm_2(x, norm2_g[l]) * (1.0 + scale2) + shift2
        u = causal_dwconv(h2 @ w_up[l], ffn_conv_w[l], ffn_conv_b[l])
        u_gate, u_val = u[..., :D_FF_2], u[..., D_FF_2:]
        x = x + gate2 * ((jax.nn.silu(u_gate) * u_val) @ w_down[l])

    return rmsnorm_2(x, final_g)


def setup_inputs(seed=0):
    out = dict(first_inputs(seed))
    for name, value in second_inputs(seed + 1).items():
        if name != "x":
            out[name + "_2"] = value
    return out


def reference(
    x, p, positions, g_mix, w_in, a_re, a_im, log_dt, b_re, b_im, c_re, c_im, d_skip,
    w_attn_proj, w_glu_a, w_glu_b, w_out, g_ffn, w_ffn_gate, w_ffn_up, w_ffn_down, w_ple_gate,
    w_ple_proj, g_final, c_2, positions_2, w_ada_2, b_ada_2, norm1_g_2, w_in_2, conv_w_2,
    conv_b_2, w_gate_a_2, b_gate_a_2, w_gate_x_2, b_gate_x_2, lru_param_2, q_norm_g_2, w_uq_2,
    kv_norm_g_2, w_ukv_2, w_proj_rnn_2, w_proj_mla_2, w_out_2, norm2_g_2, w_up_2, ffn_conv_w_2,
    ffn_conv_b_2, w_down_2, final_g_2,
):
    x = first_block(
        x, p, positions, g_mix, w_in, a_re, a_im, log_dt, b_re, b_im, c_re, c_im, d_skip,
        w_attn_proj, w_glu_a, w_glu_b, w_out, g_ffn, w_ffn_gate, w_ffn_up, w_ffn_down,
        w_ple_gate, w_ple_proj, g_final,
    )
    return second_block(
        x, c_2, positions_2, w_ada_2, b_ada_2, norm1_g_2, w_in_2, conv_w_2, conv_b_2,
        w_gate_a_2, b_gate_a_2, w_gate_x_2, b_gate_x_2, lru_param_2, q_norm_g_2, w_uq_2,
        kv_norm_g_2, w_ukv_2, w_proj_rnn_2, w_proj_mla_2, w_out_2, norm2_g_2, w_up_2,
        ffn_conv_w_2, ffn_conv_b_2, w_down_2, final_g_2,
    )


_drawn_inputs = setup_inputs


def setup_inputs(seed=0):
    import zlib

    import numpy as np

    out = dict(_drawn_inputs(seed))
    spreads = {}
    factors = {'g_mix': 4.196,
     'a_re': 64.0,
     'a_im': 3.316,
     'log_dt': 3.399,
     'b_re': 4.681,
     'b_im': 4.644,
     'c_re': 4.599,
     'c_im': 4.662,
     'b_ada_2': 3.9,
     'norm1_g_2': 8.0,
     'conv_b_2': 7.179,
     'b_gate_a_2': 64.0,
     'b_gate_x_2': 59.294,
     'q_norm_g_2': 8.0,
     'w_uq_2': 2.888,
     'kv_norm_g_2': 8.0,
     'norm2_g_2': 8.0,
     'ffn_conv_b_2': 34.467,
     'final_g_2': 7.57}
    for name, (base, spread) in spreads.items():
        noise = np.random.default_rng([zlib.crc32(name.encode()), seed]).standard_normal(out[name].shape)
        drawn = base * np.exp(spread * noise) if base else spread * noise
        out[name] = __import__('jax').numpy.asarray(drawn.astype(out[name].dtype))
    for name, factor in factors.items():
        out[name] = (out[name] * factor).astype(out[name].dtype)
    return out
```

```python
import math
from collections import deque
from contextlib import ExitStack

import numpy as np

import concourse.bass as bass
from concourse import mybir

F32 = mybir.dt.float32
F32R = mybir.dt.float32r
BF16 = mybir.dt.bfloat16
I32 = mybir.dt.int32
ALU = mybir.AluOpType
ACT = mybir.ActivationFunctionType
AX = mybir.AxisListType.X
ADD, SUB, MUL, MAX, MIN = ALU.add, ALU.subtract, ALU.mult, ALU.max, ALU.min

T = 512
CB = 8
NRAW, NHL = 4, 3
NSLOT = 78
NCHUNK = 286
HALF_PI = math.pi / 2
PI_IN = 3.1415925
MAGIC = 12582912.0
TWO_PI_1 = 6.28125
TWO_PI_2 = 0.0019350051879882812
TWO_PI_3 = 3.0199159819e-07

SMALL = [("g_mix", 8), ("g_ffn", 8), ("g_final", 8), ("n1", 8), ("n2", 8), ("gf2", 8), ("b_ada", 48),
         ("convw", 40), ("convb", 10), ("ba", 10), ("bx", 10), ("lru", 10), ("qg", 3), ("kg", 2),
         ("fcw", 132), ("fcb", 44), ("dskip", 4), ("are", 16), ("aim", 16), ("ldt", 16),
         ("if1", 1), ("sg1", 1), ("if2", 1), ("sg2", 1)]
SOFF = {}
_o = 0
for _n, _w in SMALL:
    SOFF[_n] = _o
    _o += _w
NSMALL = _o


class Token:

    def __init__(self, queue, index):
        self.queue, self.index = queue, index


class Queue:

    def __init__(self, sem):
        self.sem, self.ops, self.signals = sem, [], []

    def __call__(self, fn, *after):
        after = [t for t in after if t is not None]
        for t in after:
            if isinstance(t, Token):
                t.queue.signals[t.index] = True
        self.ops.append((fn, after))
        self.signals.append(False)
        return Token(self, len(self.ops) - 1)

    def last(self):
        return Token(self, len(self.ops) - 1)

    def value(self, index):
        return self.counts[index]

    def count(self):
        n, self.counts = 0, []
        for s in self.signals:
            n += s
            self.counts.append(n)

    def emit(self, eng):
        seen = {}
        for (fn, after), signal in zip(self.ops, self.signals):
            need = {}
            for t in after:
                sem, val = (t.queue.sem, t.queue.value(t.index)) if isinstance(t, Token) else t
                key = id(sem)
                if key not in need or need[key][1] < val:
                    need[key] = (sem, val)
            for key, (sem, val) in need.items():
                if seen.get(key, 0) < val:
                    eng.wait_ge(sem, val)
                    seen[key] = val
            ins = fn(eng)
            if signal:
                ins.then_inc(self.sem, 1)


class Bank:
    def __init__(self, ap):
        self.ap, self.free = ap, None


class Slot:
    def __init__(self, f, r):
        self.f, self.r, self.free = f, r, []


class Pool:

    def __init__(self, places):
        self.q = deque(places)
        self.least = len(places)

    def take(self):
        p = self.q.popleft()
        self.least = min(self.least, len(self.q))
        return p

    def give(self, p, *tokens):
        p.free = list(tokens)
        self.q.append(p)


def program(nc, stage, blocks, wst, xT, pT, small, consts, pos1, pos2, cT, wadaT, bcmp, cpad, gblk, out):
    ctx = ExitStack()
    with ctx:
        def sb(name, shape, dt=F32):
            return ctx.enter_context(nc.sbuf_tensor(name, shape, dt))

        def sem(name):
            return ctx.enter_context(nc.semaphore(name))

        raw = sb("raw", [128, NRAW * CB * 128])
        whi = sb("whi", [128, NHL * CB * 128], F32R)
        wlo = sb("wlo", [128, NHL * CB * 128], F32R)
        sm = sb("sm", [128, NSMALL])
        ident = sb("ident", [128, 128])
        ones = sb("ones", [128, 128])
        maskb = sb("maskb", [128, 3 * 128], BF16)
        identb = sb("identb", [128, 128], BF16)
        mod = sb("mod", [128, 48])
        scl = sb("scl", [128, 96])
        stat = sb("stat", [128, 320])
        places = []
        for i in range(NSLOT):
            with nc.sbuf_tensor(f"slotf{i}", [128, T], F32) as slotf:
                pass
            places.append(Slot(slotf[:, :], sb(f"slotr{i}", [128, T], F32R)[:, :]))
        banks = [ctx.enter_context(nc.psum_tensor(f"bank{i}", [128, 512], F32)) for i in range(8)]

        P = Queue(sem("s_pe"))
        A = Queue(sem("s_act"))
        V = Queue(sem("s_dve"))
        G = Queue(sem("s_pool"))
        S = Queue(sem("s_sp"))

        psum = Pool([Bank(b) for b in banks])
        pool = Pool(places)

        dma_sems = [sem(f"s_d{i}") for i in range(24)]
        dma_count = [0] * 24
        dma_turn = [0]

        def load(dst, src, *after):
            i = dma_turn[0] % 24
            dma_turn[0] += 1
            prev = (dma_sems[i], dma_count[i]) if dma_count[i] else None
            dma_count[i] += 16
            s, n = dma_sems[i], dma_count[i]
            S(lambda e: e.dma_start(dst, src).then_inc(s, 16), prev, *after)
            return (s, n)

        def col(name, i=0, n=1):
            return sm[:, SOFF[name] + i:SOFF[name] + i + n]

        W = CB * 128
        s_w = [sem(f"s_w{i}") for i in range(NRAW)]
        raw_free = [None] * NRAW
        hl_free = [None] * NHL
        chunk_tok = {}
        lo_turn = {"mode": "VG"}
        state = {"dma": 0, "prep": 0, "n": 0}

        def chunk_dma(c):
            if c >= NCHUNK:
                return
            i = c % NRAW
            s = s_w[i]
            S(lambda e: e.dma_start(raw[:, i * W:(i + 1) * W], wst[c]).then_inc(s, 16), raw_free[i])

        def chunk_prep(c):
            if c >= NCHUNK:
                return
            i, j = c % NRAW, c % NHL
            r, h, l = raw[:, i * W:(i + 1) * W], whi[:, j * W:(j + 1) * W], wlo[:, j * W:(j + 1) * W]
            th = A(lambda e: e.activation(h, r, ACT.Copy), (s_w[i], 16 * (c // NRAW + 1)), hl_free[j])
            m = lo_turn["mode"]
            q = V if m[c % len(m)] == "V" else G
            tl = q(lambda e: e.tensor_tensor(l, r, h.bitcast(F32), SUB), th, hl_free[j])
            raw_free[i] = tl
            chunk_tok[c] = (th, tl)

        for c in range(NRAW):
            chunk_dma(c)
            state["dma"] = c + 1

        def block(name, kt, mt):
            n = len(blocks)
            blocks.append((name, kt, mt))
            c = n // CB
            if n % CB == 0:
                if c > 0:
                    hl_free[(c - 1) % NHL] = P.last()
                if c == 0:
                    chunk_prep(0)
                    chunk_prep(1)
                chunk_prep(c + 2)
                chunk_dma(c + NRAW - 1) if c > 0 else None
            o = (c % NHL) * W + (n % CB) * 128
            return o, chunk_tok[c]

        def align4():
            while len(blocks) % 4:
                block("zero", 0, 0)

        def mm(bank, o, rhs_hi, rhs_lo, first, last, *after, cols=512, width=128):
            wh, wl = whi[:, o:o + width], wlo[:, o:o + width]
            P(lambda e: e.matmul(bank, wh, rhs_hi, start=first, stop=False), *after)
            P(lambda e: e.matmul(bank, wh, rhs_lo, start=False, stop=False))
            return P(lambda e: e.matmul(bank, wl, rhs_hi, start=False, stop=last))

        def project(name, mt, xs, k0=0):
            b = psum.take()
            n = len(xs)
            for k, (hi, lo, toks) in enumerate(xs):
                o, wt = block(name, k0 + k, mt)
                tok = mm(b.ap[:, :], o, hi, lo, k == 0, k == n - 1, *toks, *wt, *([b.free] if k == 0 else []))
            return b, tok

        def split(src, *after, q=None, hi_scale=None):
            h, l = pool.take(), pool.take()
            q = q or V
            th = A(lambda e: e.activation(h.r, src, ACT.Copy), *h.free, *after)
            tl = q(lambda e: e.tensor_tensor(l.r, src, h.r.bitcast(F32), SUB), th, *l.free)
            return h, l, th, tl

        def operand(h, l, th, tl):
            return (h.r, l.r, (th, tl))

        t_sm = load(sm[:, :], small[:, :])
        cst = pool.take()
        t_c = load(cst.f[:, 0:512], consts[:, 0:512])
        t_o = load(ones[:, :], consts[:, 512:640])
        t_id = load(ident[:, :], consts[:, 0:128])
        t_idb = V(lambda e: e.tensor_copy(identb[:, :], cst.f[:, 0:128]), t_c)
        t_mb = V(lambda e: e.tensor_copy(maskb[:, :], cst.f[:, 128:512]), t_c)
        pool.give(cst, t_mb)
        m_prev, m_diag, m_blk = 0, 128, 256
        t_eps = V(lambda e: e.memset(scl[:, 95:96], 1e-6))
        t_pi2 = V(lambda e: e.memset(scl[:, 94:95], 0.0))

        def sincos(src, dst_s, dst_c, tmp, q, *after):
            t = q(lambda e: e.tensor_scalar(tmp, src, 1.0 / (2 * math.pi), MAGIC, MUL, ADD), *after)
            t = q(lambda e: e.tensor_scalar(tmp, tmp, MAGIC, None, SUB), t)
            for c in (TWO_PI_1, TWO_PI_2, TWO_PI_3):
                t = V(lambda e, c=c: e.scalar_tensor_tensor(out=src, in0=tmp, scalar=-c, in1=src, op0=MUL, op1=ADD), t)
            t1 = q(lambda e: e.tensor_scalar(src, src, PI_IN, -PI_IN, MIN, MAX), t)
            ts = A(lambda e: e.activation(dst_s, src, ACT.Sin), t1)
            t = q(lambda e: e.tensor_scalar(tmp, src, HALF_PI, 2 * math.pi, ALU.is_gt, MUL), t1)
            t = V(lambda e: e.scalar_tensor_tensor(out=tmp, in0=src, scalar=HALF_PI, in1=tmp, op0=ADD, op1=SUB), t)
            t = q(lambda e: e.tensor_scalar(tmp, tmp, PI_IN, -PI_IN, MIN, MAX), t)
            tc = A(lambda e: e.activation(dst_c, tmp, ACT.Sin), t)
            return ts, tc

        def rope_table(pos, invf, sign):
            pi, c, s, tmp = pool.take(), pool.take(), pool.take(), pool.take()
            tp = load(pi.f.bitcast(I32), pos[:, :], *pi.free)
            t = V(lambda e: e.tensor_copy(s.f, pi.f.bitcast(I32)), tp, *s.free)
            t = V(lambda e: e.tensor_scalar(pi.f, s.f, invf, None, MUL), t, t_sm)
            ts, tc = sincos(pi.f, s.f, c.f, tmp.f, V, t, *c.free, *tmp.free)
            t = V(lambda e: e.tensor_scalar(s.f, s.f, sign, None, MUL), ts)
            pool.give(pi, ts, tc)
            pool.give(tmp, tc)
            return c, s, tc, t

        class Norm:

            def __init__(self, n):
                self.b, self.n, self.k = psum.take(), n, 0

            def add(self, src, *after):
                sq = pool.take()
                t = A(lambda e: e.activation(sq.f, src, ACT.Square), *sq.free, *after)
                b, k, n = self.b, self.k, self.n
                for j in range(4):
                    tok = P(lambda e, j=j: e.matmul(b.ap[:, j:j + 1], sq.f[:, j * 128:(j + 1) * 128], ones[:, 0:1],
                                                    start=(k == 0 and j == 0), stop=(k == n - 1),
                                                    skip_group_check=True), t, t_o, b.free)
                pool.give(sq, tok)
                self.tok = tok
                self.k += 1
                return t

            def finish(self, width, so):
                b = self.b
                st = stat[:, so:so + 4]
                t = A(lambda e: e.activation(st, b.ap[:, 0:4], ACT.Sqrt, bias=scl[:, 95:96], scale=1.0 / width), self.tok, t_eps)
                psum.give(b, t)
                b.free = t
                t = V(lambda e: e.reciprocal(st, st), t)
                dg = pool.take()
                t = V(lambda e: e.tensor_tensor(dg.f.rearrange("p (j c) -> p j c", j=4),
                                                ident[:, :].unsqueeze(1).to_broadcast([128, 4, 128]),
                                                st.unsqueeze(2).to_broadcast([128, 4, 128]), MUL), t, *dg.free, t_id)
                o = psum.take()
                t = P(lambda e: e.matmul(o.ap[:, :], ones[:, :], dg.f, start=True, stop=True), t, o.free)
                pool.give(dg, t)
                return o, t

        def bank_give(b, tok):
            psum.q.append(b)
            b.free = tok

        psum.give = bank_give

        so_next = [0]

        def stat_cols(n):
            o = so_next[0]
            so_next[0] = o + n
            if o + n > 320:
                raise ValueError("stat")
            return o

        xs = []
        for k in range(8):
            s = pool.take()
            xs.append((s, load(s.f, xT[k], *s.free)))
        nrm = Norm(8)
        for s, t in xs:
            nrm.add(s.f, t)
        rb, trb = nrm.finish(1024, stat_cols(4))
        n1 = []
        for k, (s, t) in enumerate(xs):
            t = V(lambda e, s=s, k=k, rb=rb: e.scalar_tensor_tensor(out=s.f, in0=s.f, scalar=col("g_mix", k), in1=rb.ap[:, :],
                                                             op0=MUL, op1=MUL), t, trb, t_sm)
            last = t
            h, l, th, tl = split(s.f, t, q=(G if k % 2 else V))
            n1.append(operand(h, l, th, tl) + (h, l))
            pool.give(s, th, tl)
        psum.give(rb, last)
        n1s = n1
        n1 = [x[:3] for x in n1]

        rc1, rs1, t_rc1, t_rs1 = rope_table(pos1, col("if1"), col("sg1"))

        pp = pool.take()
        pv = [pp.f[:, 16 * i:16 * i + 16] for i in range(32)]
        (dt, x_, e_, ang, tmp, sn, cs, mag, bre, bim, nr, den, zre, zim, u1, u2) = pv[:16]
        t_dt = A(lambda e: e.activation(dt, col("ldt", 0, 16), ACT.Exp), t_sm, *pp.free)
        t = V(lambda e: e.tensor_tensor(x_, col("are", 0, 16), dt, MUL), t_dt)
        t = V(lambda e: e.tensor_scalar(x_, x_, 1.0 / 256, None, MUL), t)
        t = V(lambda e: e.tensor_scalar(e_, x_, 1.0 / 720, 1.0 / 120, MUL, ADD), t)
        for c in (1.0 / 24, 1.0 / 6, 0.5, 1.0):
            t = V(lambda e: e.tensor_tensor(e_, e_, x_, MUL), t)
            t = V(lambda e, c=c: e.tensor_scalar(e_, e_, c, None, ADD), t)
        t = V(lambda e: e.tensor_tensor(e_, e_, x_, MUL), t)
        for _ in range(8):
            t = V(lambda e: e.scalar_tensor_tensor(out=e_, in0=e_, scalar=2.0, in1=e_, op0=ADD, op1=MUL), t)
        t_mag = V(lambda e: e.tensor_scalar(mag, e_, 1.0, None, ADD), t)
        t = V(lambda e: e.tensor_tensor(ang, col("aim", 0, 16), dt, MUL), t_dt)
        ts, tc = sincos(ang, sn, cs, tmp, V, t)
        t1 = V(lambda e: e.tensor_tensor(bre, mag, cs, MUL), tc, t_mag)
        t2 = V(lambda e: e.tensor_tensor(bim, mag, sn, MUL), ts)
        t = V(lambda e: e.tensor_scalar(nr, bre, 1.0, None, SUB), t1)
        t3 = V(lambda e: e.tensor_tensor(den, col("are", 0, 16), col("are", 0, 16), MUL))
        t4 = V(lambda e: e.tensor_tensor(u1, col("aim", 0, 16), col("aim", 0, 16), MUL))
        t3 = V(lambda e: e.tensor_tensor(den, den, u1, ADD), t3, t4)
        t3 = V(lambda e: e.reciprocal(den, den), t3)
        t = V(lambda e: e.tensor_tensor(zre, nr, col("are", 0, 16), MUL), t)
        t2 = V(lambda e: e.tensor_tensor(u1, bim, col("aim", 0, 16), MUL), t2, t3)
        t = V(lambda e: e.tensor_tensor(zre, zre, u1, ADD), t, t2)
        t_zr = V(lambda e: e.tensor_tensor(zre, zre, den, MUL), t, t3)
        t = V(lambda e: e.tensor_tensor(zim, bim, col("are", 0, 16), MUL), t2)
        t2 = V(lambda e: e.tensor_tensor(u2, nr, col("aim", 0, 16), MUL), t)
        t = V(lambda e: e.tensor_tensor(zim, zim, u2, SUB), t2)
        t_zi = V(lambda e: e.tensor_tensor(zim, zim, den, MUL), t, t3)

        bs = pool.take()
        tb = load(bs.f[:, :], bcmp[:, :], *bs.free)
        b_re, b_im = (bs.f[:, 256 * i:256 * i + 256].rearrange("p (i c) -> p i c", i=16) for i in range(2))
        bq, bw = pool.take(), pool.take()
        q_re, q_im = (bq.f[:, 256 * i:256 * i + 256].rearrange("p (i c) -> p i c", i=16) for i in range(2))
        w_re, w_im = (bw.f[:, 256 * i:256 * i + 256].rearrange("p (i c) -> p i c", i=16) for i in range(2))
        zr_b = zre.unsqueeze(2).to_broadcast([128, 16, 16])
        zi_b = zim.unsqueeze(2).to_broadcast([128, 16, 16])
        t1 = V(lambda e: e.tensor_tensor(q_re, b_re, zr_b, MUL), tb, t_zr, *bq.free)
        t2 = V(lambda e: e.tensor_tensor(w_re, b_im, zi_b, MUL), t_zi, *bw.free)
        t3 = V(lambda e: e.tensor_tensor(q_im, b_im, zr_b, MUL))
        t4 = V(lambda e: e.tensor_tensor(w_im, b_re, zi_b, MUL))
        bpad = [pool.take() for _ in range(8)]
        bt = []
        for c, (qq, ww, op) in enumerate(((q_re, w_re, SUB), (q_im, w_im, ADD))):
            for j in range(4):
                d = bpad[4 * c + j]
                tz = G(lambda e, d=d: e.memset(d.f, 0.0), *d.free)
                for half in range(2):
                    rows = slice(64 * half, 64 * half + 64)
                    for k in range(4):
                        o = k * 160 + half * 16
                        t = V(lambda e, d=d, rows=rows, o=o, j=j, k=k, qq=qq, ww=ww, op=op: e.tensor_tensor(
                            d.f[rows, o:o + 16], qq[rows, 4 * j + k, :], ww[rows, 4 * j + k, :], op), tz, t1, t2, t3, t4)
                bt.append(t)
        pool.give(bs, t4)
        pool.give(bq, bt[-1])
        pool.give(bw, bt[-1])

        el_r, el_i, eh = pool.take(), pool.take(), pool.take()
        lr, li = (s.f.rearrange("p (i t) -> p i t", i=16) for s in (el_r, el_i))
        hr, hi_ = (eh.f[:, 256 * i:256 * i + 256].rearrange("p (i t) -> p i t", i=16) for i in range(2))
        pw = pool.take()
        wa, wb = (pw.f[:, 256 * i:256 * i + 256] for i in range(2))
        cur_r, cur_i, nxt_r, nxt_i = pv[16], pv[17], pv[18], pv[19]

        def square(*after):
            a = V(lambda e, r=cur_r: e.tensor_tensor(u1, r, r, MUL), *after)
            b = V(lambda e, i=cur_i: e.tensor_tensor(u2, i, i, MUL), *after)
            d = V(lambda e, r=cur_r, i=cur_i: e.tensor_tensor(nxt_i, r, i, MUL), *after)
            a = V(lambda e: e.tensor_tensor(nxt_r, u1, u2, SUB), a, b)
            d = V(lambda e: e.tensor_scalar(nxt_i, nxt_i, 2.0, None, MUL), d)
            a = V(lambda e: e.tensor_copy(cur_r, nxt_r), a)
            d = V(lambda e: e.tensor_copy(cur_i, nxt_i), d)
            return a, d

        ta = V(lambda e: e.tensor_copy(cur_r, cs), tc)
        tb_ = V(lambda e: e.tensor_copy(cur_i, sn), ts)

        def table(R, I, bits, tr, ti, *after):
            t1 = V(lambda e: e.memset(R[:, :, 0:1], 1.0), *after)
            t2 = V(lambda e: e.memset(I[:, :, 0:1], 0.0), *after)
            w1 = lambda n: wa[:, 0:16 * n].rearrange("p (i t) -> p i t", i=16)
            w2 = lambda n: wb[:, 0:16 * n].rearrange("p (i t) -> p i t", i=16)
            for b in range(bits):
                n = 1 << b
                cr = cur_r.unsqueeze(2).to_broadcast([128, 16, n])
                ci = cur_i.unsqueeze(2).to_broadcast([128, 16, n])
                a = V(lambda e, n=n, cr=cr: e.tensor_tensor(w1(n), R[:, :, 0:n], cr, MUL), tr, t1, t2)
                d = V(lambda e, n=n, ci=ci: e.tensor_tensor(w2(n), I[:, :, 0:n], ci, MUL), ti, t1, t2)
                t1 = V(lambda e, n=n: e.tensor_tensor(R[:, :, n:2 * n], w1(n), w2(n), SUB), a, d)
                a = V(lambda e, n=n, ci=ci: e.tensor_tensor(w1(n), R[:, :, 0:n], ci, MUL), t1)
                d = V(lambda e, n=n, cr=cr: e.tensor_tensor(w2(n), I[:, :, 0:n], cr, MUL), t1)
                t2 = V(lambda e, n=n: e.tensor_tensor(I[:, :, n:2 * n], w1(n), w2(n), ADD), a, d)
                tr, ti = square(t2)
            return tr, ti, t1, t2

        tr, ti, l1, l2 = table(lr, li, 5, ta, tb_, *el_r.free, *el_i.free, *pw.free)
        tr, ti, h1_, h2_ = table(hr, hi_, 4, tr, ti, *eh.free)
        pool.give(pw, h2_)
        t_pow = h2_

        def ssm():
            ys = []
            us = []
            for j in range(4):
                b, tok = project("in", 36 + j, n1)
                u = pool.take()
                t = A(lambda e, b=b, u=u: e.activation(u.f, b.ap[:, :], ACT.Copy), tok, *u.free)
                psum.give(b, t)
                us.append((u, t))
                yield
            for j in range(4):
                u, tu = us[j]
                bT = []
                for c in range(2):
                    b = psum.take()
                    d = bpad[4 * c + j]
                    for k in range(4):
                        tok = P(lambda e, b=b, d=d, k=k: e.transpose(b.ap[:, k * 128:(k + 1) * 128],
                                                                     d.f[:, k * 128:(k + 1) * 128], ident[:, :]),
                                bt[4 * c + j], b.free, t_id)
                    s = pool.take()
                    t = A(lambda e, b=b, s=s: e.activation(s.f, b.ap[:, :], ACT.Copy), tok, *s.free)
                    psum.give(b, t)
                    pool.give(d, tok)
                    bT.append((s, t))
                cc = []
                for c in range(2):
                    s = pool.take()
                    cc.append((s, load(s.f, cpad[c, j], *s.free)))
                yb = None
                pend = None
                for k in range(4):
                    i = 4 * j + k
                    er, ei, w = pool.take(), pool.take(), pool.take()
                    v3 = lambda s: s.f.rearrange("p (a b) -> p a b", a=16)
                    br_ = lr[:, i, :].unsqueeze(1).to_broadcast([128, 16, 32])
                    bi_ = li[:, i, :].unsqueeze(1).to_broadcast([128, 16, 32])
                    ar_ = hr[:, i, :].unsqueeze(2).to_broadcast([128, 16, 32])
                    ai_ = hi_[:, i, :].unsqueeze(2).to_broadcast([128, 16, 32])
                    t1 = G(lambda e, er=er, a=ar_, b=br_: e.tensor_tensor(v3(er), a, b, MUL), t_pow, *er.free)
                    t2 = G(lambda e, w=w, a=ai_, b=bi_: e.tensor_tensor(v3(w), a, b, MUL), *w.free)
                    t_er = G(lambda e, er=er, w=w: e.tensor_tensor(er.f, er.f, w.f, SUB), t1, t2)
                    t1 = G(lambda e, ei=ei, a=ar_, b=bi_: e.tensor_tensor(v3(ei), a, b, MUL), *ei.free)
                    t2 = G(lambda e, w=w, a=ai_, b=br_: e.tensor_tensor(v3(w), a, b, MUL), t_er)
                    t_ei = G(lambda e, ei=ei, w=w: e.tensor_tensor(ei.f, ei.f, w.f, ADD), t1, t2)
                    pool.give(w, t_ei)
                    bk = []
                    for c in range(2):
                        b = psum.take()
                        s, t = bT[c]
                        bk.append((b, P(lambda e, b=b, s=s, k=k, u=u: e.matmul(b.ap[:, :], s.f[:, k * 128:(k + 1) * 128], u.f,
                                                                          start=True, stop=True), t, tu, b.free)))
                    (b0, p0), (b1, p1) = bk
                    gr, gi, w1, w2 = (pool.take() for _ in range(4))
                    t1 = V(lambda e, gr=gr, b0=b0, er=er: e.tensor_tensor(gr.f, b0.ap[:, :], er.f, MUL), p0, t_er, *gr.free)
                    t2 = V(lambda e, w1=w1, b1=b1, ei=ei: e.tensor_tensor(w1.f, b1.ap[:, :], ei.f, MUL), p1, t_ei, *w1.free)
                    t3 = V(lambda e, gi=gi, b1=b1, er=er: e.tensor_tensor(gi.f, b1.ap[:, :], er.f, MUL), *gi.free)
                    psum.give(b1, t3)
                    t4 = V(lambda e, w2=w2, b0=b0, ei=ei: e.tensor_tensor(w2.f, b0.ap[:, :], ei.f, MUL), *w2.free)
                    psum.give(b0, t4)
                    t1 = G(lambda e, gr=gr, w1=w1: e.tensor_tensor(gr.f, gr.f, w1.f, ADD), t1, t2)
                    t3 = G(lambda e, gi=gi, w2=w2: e.tensor_tensor(gi.f, gi.f, w2.f, SUB), t3, t4)
                    yield
                    mg = mag[:, i:i + 1].to_broadcast([128, 512])
                    sr = V(lambda e, w1=w1, gr=gr, mg=mg: e.tensor_tensor_scan(w1.f, mg, gr.f, 0.0, MUL, ADD), t1, t_mag)
                    si = V(lambda e, w2=w2, gi=gi, mg=mg: e.tensor_tensor_scan(w2.f, mg, gi.f, 0.0, MUL, ADD), t3)
                    h2 = pool.take()
                    t1 = V(lambda e, gr=gr, w1=w1, er=er: e.tensor_tensor(gr.f, w1.f, er.f, MUL), sr)
                    t2 = V(lambda e, gi=gi, w2=w2, ei=ei: e.tensor_tensor(gi.f, w2.f, ei.f, MUL), si)
                    t1 = V(lambda e, gr=gr, gi=gi: e.tensor_tensor(gr.f, gr.f, gi.f, SUB), t1, t2)
                    t3 = V(lambda e, h2=h2, w1=w1, ei=ei: e.tensor_tensor(h2.f, w1.f, ei.f, MUL), *h2.free)
                    t4 = V(lambda e, gi=gi, w2=w2, er=er: e.tensor_tensor(gi.f, w2.f, er.f, MUL), t1)
                    t3 = V(lambda e, h2=h2, gi=gi: e.scalar_tensor_tensor(out=h2.f, in0=h2.f, scalar=-1.0, in1=gi.f,
                                                                          op0=MUL, op1=SUB), t3, t4)
                    pool.give(w1, t3)
                    pool.give(w2, t4)
                    pool.give(er, t4)
                    pool.give(ei, t3)
                    pool.give(gi, t3)
                    yield
                    if yb is None:
                        yb = psum.take()
                    for c, (hh, th) in enumerate(((gr, t1), (h2, t3))):
                        s, tcx = cc[c]
                        tok = P(lambda e, c=c, k=k, s=s, hh=hh, yb=yb: e.matmul(
                            yb.ap[:, :], s.f[:, k * 128:(k + 1) * 128], hh.f, start=(k == 0 and c == 0),
                            stop=(k == 3 and c == 1)), th, tcx, yb.free)
                        pool.give(hh, tok)
                yt = pool.take()
                t = V(lambda e, yt=yt, u=u, yb=yb, j=j: e.scalar_tensor_tensor(
                    out=yt.f, in0=u.f, scalar=col("dskip", j), in1=yb.ap[:, :], op0=MUL, op1=ADD), tok, tu, *yt.free)
                psum.give(yb, t)
                pool.give(u, t)
                for s, _ in bT + cc:
                    pool.give(s, tok)
                t = A(lambda e, yt=yt: e.activation(yt.f, yt.f, ACT.Gelu_apprx_tanh), t)
                h, l, th, tl = split(yt.f, t)
                pool.give(yt, tl)
                ys.append(operand(h, l, th, tl) + (h, l))
                yield
            ssm_out.extend(ys)
            for s in (el_r, el_i, eh):
                pool.give(s, t_ei)
            pool.give(pp, t3)

        ssm_out = []
        bg = ssm()

        def step(n=1):
            for _ in range(n):
                try:
                    next(bg)
                except StopIteration:
                    return

        for _ in range(4):
            step()

        DIL = (1, 4, 16)
        SCALE = 1.0 / math.sqrt(128.0)
        OT = [[None] * 4 for _ in range(3)]
        st_t = {}
        MO, DO = stat_cols(48), stat_cols(48)

        def perm(ap, d):
            if d == 1:
                return ap
            if len(ap.shape) == 2:
                return ap.rearrange("p (r l) -> p l r", r=d)

        def nat(ap, d):
            return ap if d == 1 else ap.rearrange("p (l r) -> p l r", r=d)

        def rope(b, dst, rows, tbl, d, tok_copy):
            c, s, tc_, ts_ = tbl
            w1, w2 = pool.take(), pool.take()
            mask = list(range(16, 32)) + list(range(16))
            t1 = V(lambda e: e.tensor_tensor(w1.f[rows, :], b.ap[rows, :], c.f[rows, :], MUL), tok_copy, tc_, *w1.free)
            t2 = V(lambda e: e.stream_shuffle(w2.f[rows, :], b.ap[rows, :], mask), *w2.free)
            psum.give(b, t2)
            q = G if rows.start == 0 else V
            t2 = q(lambda e: e.tensor_tensor(w2.f[rows, :], w2.f[rows, :], s.f[rows, :], MUL), t2, ts_)
            t = q(lambda e: e.tensor_tensor(perm(dst.f[rows, :], d), nat(w1.f[rows, :], d), nat(w2.f[rows, :], d), ADD),
                  t1, t2, tok_copy)
            pool.give(w1, t)
            pool.give(w2, t)
            return t

        tbl1 = (rc1, rs1, t_rc1, t_rs1)

        def qkv(g, h):
            d = DIL[g]
            got = []
            for part in range(3):
                b, tok = project("in", part * 12 + g * 4 + h, n1)
                s = pool.take()
                t = A(lambda e, b=b, s=s: e.activation(perm(s.f, d), nat(b.ap[:, :], d), ACT.Copy), tok, *s.free)
                if part < 2:
                    t = rope(b, s, slice(0, 32), tbl1, d, t)
                else:
                    psum.give(b, t)
                got.append((s, t))
                step()
            return got

        def scores(g, h, got):
            (q, tq), (k, tk), (v, tv) = got
            vb = psum.take()
            for n in range(4):
                tok = P(lambda e, n=n: e.transpose(vb.ap[:, n * 128:(n + 1) * 128], v.f[:, n * 128:(n + 1) * 128], ident[:, :]),
                        tv, vb.free)
            vn = pool.take()
            t_vn = A(lambda e: e.activation(vn.f, vb.ap[:, :], ACT.Copy), tok, *vn.free)
            psum.give(vb, t_vn)
            pool.give(v, tok)
            if g == 0:
                parts = [[(0, 0, 128, m_diag, 128), (1, 128, 256, m_prev, 256)],
                         [(2, 0, 256, m_prev, 256), (3, 256, 256, m_prev, 256)]]
            else:
                parts = [[(n, n * 128, 128, m_diag if g == 1 else m_blk, 128) for n in range(4)]]
            probs = {}
            for part in parts:
                b = psum.take()
                for n, o, w, mo, mw in part:
                    k0 = (n - 1) * 128 if w == 256 else n * 128
                    P(lambda e, n=n, o=o, w=w, k0=k0, b=b: e.matmul(b.ap[:, o:o + w], q.f[:, n * 128:(n + 1) * 128],
                                                                    k.f[:, k0:k0 + w], start=True, stop=False),
                      tq, tk, b.free)
                    tok = P(lambda e, o=o, w=w, mo=mo, b=b: e.matmul(b.ap[:, o:o + w], identb[:, :], maskb[:, mo:mo + w],
                                                                     start=False, stop=True), t_idb, t_mb)
                mcol = lambda n: MO + g * 16 + n * 4 + h
                t = None
                if g == 0:
                    for n, o, w, *_ in part:
                        t = V(lambda e, n=n, o=o, w=w, b=b: e.tensor_reduce(stat[:, mcol(n):mcol(n) + 1], b.ap[:, o:o + w], AX, MAX), tok)
                else:
                    t = V(lambda e, b=b: e.tensor_reduce(stat[:, MO + g * 16 + h:MO + g * 16 + 16:4],
                                                         b.ap[:, :].rearrange("p (n c) -> p n c", n=4), AX, MAX), tok)
                n0, n1_ = part[0][0], part[-1][0]
                neg = scl[:, 4 * ((h * 3 + g) % 8) + n0:4 * ((h * 3 + g) % 8) + n1_ + 1]
                t_m = t
                t = V(lambda e, neg=neg, n0=n0, n1_=n1_: e.tensor_scalar(neg, stat[:, mcol(n0):mcol(n1_) + 1:4], -SCALE, None, MUL), t,
                      neg_free[(h * 3 + g) % 8])
                p = pool.take()
                for n, o, w, *_ in part:
                    te = A(lambda e, p=p, b=b, n=n, o=o, w=w, neg=neg, n0=n0: e.activation(
                        p.f[:, o:o + w], b.ap[:, o:o + w], ACT.Exp, bias=neg[:, n - n0:n - n0 + 1], scale=SCALE,
                        accum_out=stat[:, DO + g * 16 + n * 4 + h:DO + g * 16 + n * 4 + h + 1]), t, *p.free)
                    probs[n] = (p, o, w, te)
                psum.give(b, te)
                neg_free[(h * 3 + g) % 8] = te
            st_t[(g, h)] = (t_m, te)
            pool.give(q, tok)
            pool.give(k, tok)
            return vn, t_vn, probs, parts

        neg_free = [None] * 8

        def values(g, h, sc):
            vn, t_vn, probs, parts = sc
            ob = psum.take()
            for part in parts:
                p = probs[part[0][0]][0]
                b = psum.take()
                width = part[-1][1] + part[-1][2]
                te = probs[part[-1][0]][3]
                for c in range(width // 128):
                    tok = P(lambda e, c=c, b=b, p=p: e.transpose(b.ap[:, c * 128:(c + 1) * 128], p.f[:, c * 128:(c + 1) * 128],
                                                                 ident[:, :]), te, b.free)
                pool.give(p, tok)
                pt = pool.take()
                t = V(lambda e, b=b, pt=pt, width=width: e.tensor_copy(pt.f[:, 0:width], b.ap[:, 0:width]), tok, *pt.free)
                psum.give(b, t)
                for n, o, w, *_ in part:
                    keys = [n] if w == 128 else [n - 1, n]
                    for x, kb in enumerate(keys):
                        tok = P(lambda e, n=n, o=o, x=x, kb=kb, pt=pt, last=(x == len(keys) - 1), ff=(x == 0): e.matmul(
                            ob.ap[:, n * 128:(n + 1) * 128], vn.f[:, kb * 128:(kb + 1) * 128],
                            pt.f[:, o + x * 128:o + (x + 1) * 128], start=ff, stop=last), t, t_vn, ob.free)
                pool.give(pt, tok)
            pool.give(vn, tok)
            o_ = pool.take()
            d = DIL[g]
            src = ob.ap[:, :] if d == 1 else ob.ap[:, :].rearrange("p (r l) -> p l r", r=d)
            t = A(lambda e: e.activation(nat(o_.f, d), src, ACT.Copy), tok, *o_.free)
            psum.give(ob, t)
            OT[g][h] = (o_, t)

        prev = None
        sc_prev = None
        for h in range(4):
            for g in range(3):
                got = qkv(g, h)
                if sc_prev is not None:
                    values(*sc_prev)
                    sc_prev = None
                sc_prev = (g, h, scores(g, h, got))
        step()
        values(*sc_prev)
        pool.give(rc1, t_rc1, G.last())
        pool.give(rs1, t_rs1, G.last())

        if stage == 1:
            pass
        rows_m, rows_d = [], []
        for kind, base, lst in ((0, MO, rows_m), (1, DO, rows_d)):
            for g in range(3):
                b = psum.take()
                for n in range(4):
                    c0 = base + g * 16 + n * 4
                    tok = P(lambda e, b=b, n=n, c0=c0: e.transpose(b.ap[0:4, n * 128:(n + 1) * 128], stat[:, c0:c0 + 4], ident[:, :]),
                            *[st_t[(g, h)][kind] for h in range(4)], b.free)
                s = pool.take()
                d = DIL[g]
                src = b.ap[0:4, :] if d == 1 else b.ap[0:4, :].rearrange("p (r l) -> p l r", r=d)
                t = A(lambda e, s=s, src=src, d=d: e.activation(nat(s.f[0:4, :], d), src, ACT.Copy), tok, *s.free)
                psum.give(b, t)
                lst.append((s, t))
        for _ in range(80):
            step()
        mx = pool.take()
        (m0, a0), (m1, a1), (m2, a2) = rows_m
        t = V(lambda e: e.tensor_tensor(mx.f[0:4, :], m0.f[0:4, :], m1.f[0:4, :], MAX), a0, a1, *mx.free)
        t = V(lambda e: e.tensor_tensor(mx.f[0:4, :], mx.f[0:4, :], m2.f[0:4, :], MAX), t, a2)
        te = []
        for s, _ in rows_m:
            x = V(lambda e, s=s: e.tensor_tensor(s.f[0:4, :], s.f[0:4, :], mx.f[0:4, :], SUB), t)
            te.append(A(lambda e, s=s: e.activation(s.f[0:4, :], s.f[0:4, :], ACT.Exp, scale=SCALE), x))
        tz = None
        for g in range(3):
            (e_s, _), (d_s, td) = rows_m[g], rows_d[g]
            x = V(lambda e, e_s=e_s, d_s=d_s: e.tensor_tensor(d_s.f[0:4, :], d_s.f[0:4, :], e_s.f[0:4, :], MUL), te[g], td)
            if g == 0:
                tz = V(lambda e, d_s=d_s: e.tensor_copy(mx.f[0:4, :], d_s.f[0:4, :]), x)
            else:
                tz = V(lambda e, d_s=d_s: e.tensor_tensor(mx.f[0:4, :], mx.f[0:4, :], d_s.f[0:4, :], ADD), x, tz)
            pool.give(d_s, tz)
        tz = V(lambda e: e.reciprocal(mx.f[0:4, :], mx.f[0:4, :]), tz)
        tw = []
        for g in range(3):
            s = rows_m[g][0]
            tw.append(V(lambda e, s=s: e.tensor_tensor(s.f[0:4, :], s.f[0:4, :], mx.f[0:4, :], MUL), tz))
        pool.give(mx, tw[-1])
        attn = []
        selp = pool.take()
        t_sel = load(selp.f[0:4, :], consts[0:4, 640:1152], *selp.free)
        for h in range(4):
            acc = None
            for g in range(3):
                b = psum.take()
                s = rows_m[g][0]
                tok = P(lambda e, b=b, s=s, h=h: e.matmul(b.ap[:, :], selp.f[0:4, h * 128:(h + 1) * 128], s.f[0:4, :],
                                                          start=True, stop=True), tw[g], t_sel, b.free)
                o_, to = OT[g][h]
                t = V(lambda e, o_=o_, b=b: e.tensor_tensor(o_.f, o_.f, b.ap[:, :], MUL), to, tok)
                psum.give(b, t)
                if acc is None:
                    acc, ta = o_, t
                else:
                    ta = G(lambda e, acc=acc, o_=o_: e.tensor_tensor(acc.f, acc.f, o_.f, ADD), t, ta)
                    pool.give(o_, ta)
            hs, ls, th, tl = split(acc.f, ta)
            pool.give(acc, tl)
            attn.append(operand(hs, ls, th, tl) + (hs, ls))
        for s, _ in rows_m:
            pool.give(s, tok)
        pool.give(selp, tok)

        def free_ops(ops, tok):
            for x in ops:
                pool.give(x[3], tok)
                pool.give(x[4], tok)

        def three(ops):
            return [x[:3] for x in ops]

        def sigmoid_of(b, tok):
            s = pool.take()
            t = A(lambda e: e.activation(s.f, b.ap[:, :], ACT.Sigmoid), tok, *s.free)
            psum.give(b, t)
            return s, t

        at3, y3 = three(attn), three(ssm_out)
        merged = []
        for m in range(8):
            ga, tga = sigmoid_of(*project("in", 40 + m, n1))
            gs, tgs = sigmoid_of(*project("in", 48 + m, n1))
            b, tok = project("ap", m, at3)
            t = V(lambda e, ga=ga, b=b: e.tensor_tensor(ga.f, ga.f, b.ap[:, :], MUL), tga, tok)
            psum.give(b, t)
            sb_, tsb = sigmoid_of(*project("gb", m, y3))
            b, tok = project("ga", m, y3)
            t2 = V(lambda e, sb_=sb_, b=b: e.tensor_tensor(sb_.f, sb_.f, b.ap[:, :], MUL), tsb, tok)
            psum.give(b, t2)
            t2 = G(lambda e, sb_=sb_, gs=gs: e.tensor_tensor(gs.f, gs.f, sb_.f, MUL), t2, tgs)
            pool.give(sb_, t2)
            t = G(lambda e, ga=ga, gs=gs: e.tensor_tensor(ga.f, ga.f, gs.f, ADD), t, t2)
            pool.give(gs, t)
            h, l, th, tl = split(ga.f, t)
            pool.give(ga, tl)
            merged.append(operand(h, l, th, tl) + (h, l))
        free_ops(n1s, P.last())
        free_ops(attn, P.last())
        free_ops(ssm_out, P.last())

        hs_ = []
        for k in range(8):
            s = pool.take()
            hs_.append([s, load(s.f, xT[k], *s.free)])
        mg3 = three(merged)
        nrm = Norm(8)

        def residual(name, ops, nrm=None, k0=0, gate=None):
            late = None
            for m in range(8):
                b, tok = project(name, m, ops, k0)
                s, ts_ = hs_[m]
                if gate is None:
                    t = V(lambda e, s=s, b=b: e.tensor_tensor(s.f, s.f, b.ap[:, :], ADD), tok, ts_)
                else:
                    t = V(lambda e, s=s, b=b, m=m: e.scalar_tensor_tensor(out=s.f, in0=b.ap[:, :], scalar=gate(m), in1=s.f,
                                                                          op0=MUL, op1=ADD), tok, ts_)
                psum.give(b, t)
                hs_[m][1] = t
                if nrm is not None:
                    if late is not None:
                        nrm.add(*late)
                    late = (s.f, t)
            if nrm is not None:
                nrm.add(*late)

        residual("out", mg3, nrm)
        free_ops(merged, P.last())

        pl = []
        for k in range(2):
            s = pool.take()
            t = load(s.f, pT[k], *s.free)
            h, l, th, tl = split(s.f, t)
            pool.give(s, tl)
            pl.append(operand(h, l, th, tl) + (h, l))
        rb, trb = nrm.finish(1024, stat_cols(4))
        ple = []

        def ple_tile(m):
            b, tok = project("pp", m, three(pl))
            s = pool.take()
            t = A(lambda e: e.activation(s.f, b.ap[:, :], ACT.Copy), tok, *s.free)
            psum.give(b, t)
            ple.append((s, t))

        def normed(rb, trb, g, q2=None):
            ops = []
            for k in range(8):
                s, ts_ = hs_[k]
                w = pool.take()
                t = V(lambda e, s=s, w=w, k=k: e.scalar_tensor_tensor(out=w.f, in0=s.f, scalar=g(k), in1=rb.ap[:, :],
                                                                      op0=MUL, op1=MUL), ts_, trb, *w.free)
                h, l, th, tl = split(w.f, t, q=(G if k % 2 else V))
                pool.give(w, th, tl)
                ops.append(operand(h, l, th, tl) + (h, l))
            psum.give(rb, t)
            return ops

        n2 = normed(rb, trb, lambda k: col("g_ffn", k))
        for m in range(8):
            ple_tile(m)
        free_ops(pl, P.last())

        def ada():
            cr = [pool.take() for _ in range(2)]
            tcs = []
            for i, s in enumerate(cr):
                t = load(s.f, cT[:, i * 512:(i + 1) * 512], *s.free)
                tcs.append(A(lambda e, s=s: e.activation(s.f, s.f, ACT.Silu), t))
            part = pool.take()
            for m in range(48):
                ws = [pool.take() for _ in range(2)]
                for i, s in enumerate(ws):
                    t = load(s.f, wadaT[m, :, i * 512:(i + 1) * 512], *s.free)
                    t = V(lambda e, s=s, i=i, m=m: e.tensor_tensor_reduce(
                        s.f, s.f, cr[i].f, 1.0, 0.0, MUL, ADD, part.f[:, 2 * m + i:2 * m + i + 1]), t, tcs[i], *part.free)
                    pool.give(s, t)
                yield
            t = V(lambda e: e.tensor_tensor(mod[:, :], part.f[:, 0:96:2], part.f[:, 1:96:2], ADD), t)
            t = V(lambda e: e.tensor_tensor(mod[:, :], mod[:, :], col("b_ada", 0, 48), ADD), t)
            V(lambda e: e.scalar_tensor_tensor(out=scl[:, 32:40], in0=mod[:, 8:16], scalar=1.0, in1=col("n1", 0, 8),
                                               op0=ADD, op1=MUL), t)
            t = V(lambda e: e.scalar_tensor_tensor(out=scl[:, 40:48], in0=mod[:, 32:40], scalar=1.0, in1=col("n2", 0, 8),
                                                   op0=ADD, op1=MUL))
            t_mod.append(t)
            for s in cr:
                pool.give(s, t)
            pool.give(part, t)

        t_mod = []
        bg = ada()

        def gated(name_g, name_u, m, ops):
            b, tok = project(name_g, m, ops)
            s = pool.take()
            t = A(lambda e: e.activation(s.f, b.ap[:, :], ACT.Silu), tok, *s.free)
            psum.give(b, t)
            b2, tok = project(name_u, m, ops)
            t = V(lambda e: e.tensor_tensor(s.f, s.f, b2.ap[:, :], MUL), tok, t)
            psum.give(b2, t)
            h, l, th, tl = split(s.f, t)
            pool.give(s, tl)
            return operand(h, l, th, tl) + (h, l)

        n23 = three(n2)
        for half in range(2):
            acts = []
            for m in range(11):
                acts.append(gated("fg", "fu", half * 11 + m, n23))
                step(2)
            if half == 1:
                free_ops(n2, P.last())
            residual("fd", three(acts), None, half * 11)
            free_ops(acts, P.last())
            step(8)
        for _ in range(50):
            step()

        h2 = []
        for k in range(8):
            s, t = hs_[k]
            h, l, th, tl = split(s.f, t, q=(G if k % 2 else V))
            h2.append(operand(h, l, th, tl) + (h, l))
        nrm = Norm(8)
        late = None
        for m in range(8):
            s_, t = sigmoid_of(*project("pg", m, three(h2)))
            w, tw_ = ple[m]
            t = G(lambda e, s_=s_, w=w: e.tensor_tensor(s_.f, s_.f, w.f, MUL), t, tw_)
            pool.give(w, t)
            s, ts_ = hs_[m]
            t = G(lambda e, s=s, s_=s_: e.tensor_tensor(s.f, s.f, s_.f, ADD), t, ts_, h2[m][2][0], h2[m][2][1])
            pool.give(s_, t)
            hs_[m][1] = t
            if late is not None:
                nrm.add(*late)
            late = (s.f, t)
        nrm.add(*late)
        free_ops(h2, P.last())
        rb, trb = nrm.finish(1024, stat_cols(4))

        rc2, rs2, t_rc2, t_rs2 = rope_table(pos2, col("if2"), col("sg2"))
        nrm = Norm(8)
        for k in range(8):
            s, ts_ = hs_[k]
            t = V(lambda e, s=s, k=k, rb=rb: e.scalar_tensor_tensor(out=s.f, in0=s.f, scalar=col("g_final", k), in1=rb.ap[:, :],
                                                             op0=MUL, op1=MUL), ts_, trb)
            hs_[k][1] = t
            nrm.add(s.f, t)
        psum.give(rb, t)
        rb, trb = nrm.finish(1024, stat_cols(4))

        def modulated(rb, trb, so, sh):
            ops = []
            for k in range(8):
                s, ts_ = hs_[k]
                w = pool.take()
                t = V(lambda e, s=s, w=w: e.tensor_tensor(w.f, s.f, rb.ap[:, :], MUL), ts_, trb, *w.free)
                t = V(lambda e, w=w, k=k: e.tensor_scalar(w.f, w.f, scl[:, so + k:so + k + 1], mod[:, sh + k:sh + k + 1], MUL, ADD),
                      t, t_mod[0])
                h, l, th, tl = split(w.f, t, q=(G if k % 2 else V))
                pool.give(w, th, tl)
                ops.append(operand(h, l, th, tl) + (h, l))
            psum.give(rb, t)
            return ops

        nn = modulated(rb, trb, 32, 0)
        nn3 = three(nn)

        sp = stat_cols(60)
        spv = [stat[:, sp + 10 * i:sp + 10 * i + 10] for i in range(6)]
        lru = col("lru", 0, 10)
        a_, z_, s_2, u_, acc_, r_ = spv
        t = V(lambda e: e.tensor_scalar(a_, lru, -1.0, None, MUL), t_sm)
        t = V(lambda e: e.tensor_tensor(a_, a_, lru, MIN), t)
        t = A(lambda e: e.activation(z_, a_, ACT.Exp), t)
        t = V(lambda e: e.tensor_scalar(u_, z_, 2.0, None, ADD), t)
        t = V(lambda e: e.reciprocal(u_, u_), t)
        t = V(lambda e: e.tensor_tensor(z_, z_, u_, MUL), t)
        t = V(lambda e: e.tensor_tensor(s_2, z_, z_, MUL), t)
        t = V(lambda e: e.tensor_scalar(acc_, s_2, 1.0 / 17, 1.0 / 15, MUL, ADD), t)
        for n in (13, 11, 9, 7, 5, 3, 1):
            t = V(lambda e: e.tensor_tensor(acc_, acc_, s_2, MUL), t)
            t = V(lambda e, n=n: e.tensor_scalar(acc_, acc_, 1.0 / n, None, ADD), t)
        t = V(lambda e: e.tensor_tensor(acc_, acc_, z_, MUL), t)
        t = V(lambda e: e.tensor_scalar(acc_, acc_, 8.0, None, MUL), t)
        t = V(lambda e: e.tensor_scalar(r_, lru, -4.0, 0.0, MUL, MAX), t)
        t_sp = V(lambda e: e.tensor_tensor(r_, r_, acc_, ADD), t)

        rst = pool.take()
        pi = pool.take()
        tp = load(pi.f.bitcast(I32), pos2[:, :], *pi.free)
        t = V(lambda e: e.tensor_copy(rst.f, pi.f.bitcast(I32)), tp, *rst.free)
        pool.give(pi, t)
        t_rst = V(lambda e: e.tensor_scalar(rst.f, rst.f, 0.0, None, ALU.is_equal), t)

        gw = []
        for i in range(5):
            s = pool.take()
            gw.append((s, load(s.f, gblk[i], *s.free)))

        def lru_tiles():
            done = []
            for i in range(10):
                b, tok = project("in2", i, nn3)
                xc = pool.take()
                t = V(lambda e, b=b, xc=xc, i=i: e.tensor_scalar(xc.f, b.ap[:, :], col("convw", 30 + i), col("convb", i), MUL, ADD),
                      tok, *xc.free)
                for k in (1, 2, 3):
                    t = V(lambda e, b=b, xc=xc, i=i, k=k: e.scalar_tensor_tensor(
                        out=xc.f[:, k:512], in0=b.ap[:, 0:512 - k], scalar=col("convw", (3 - k) * 10 + i), in1=xc.f[:, k:512],
                        op0=MUL, op1=ADD), t)
                psum.give(b, t)
                done.append((i, xc, t))
                yield
                if len(done) > 1:
                    lru_gate(*done[-2])
            lru_gate(*done[-1])
            yield
            for i in range(10):
                lru_b(i)
                if i % 2:
                    yield

        lr_st = {}

        def lru_gate(i, xc, t):
            g_s, tg = gw[i // 2]
            o = (i % 2) * 256
            b1, b2 = psum.take(), psum.take()
            tk1 = P(lambda e: e.matmul(b1.ap[:, :], g_s.f[:, o:o + 128], xc.f, start=True, stop=True), t, tg, b1.free)
            tk2 = P(lambda e: e.matmul(b2.ap[:, :], g_s.f[:, o + 128:o + 256], xc.f, start=True, stop=True), b2.free)
            if i % 2:
                pool.give(g_s, tk2)
            r, x = pool.take(), pool.take()
            t1 = A(lambda e: e.activation(r.f, b1.ap[:, :], ACT.Sigmoid, bias=col("ba", i)), tk1, *r.free)
            psum.give(b1, t1)
            t2 = A(lambda e: e.activation(x.f, b2.ap[:, :], ACT.Sigmoid, bias=col("bx", i)), tk2, *x.free)
            psum.give(b2, t2)
            t1 = A(lambda e: e.activation(r.f, r.f, ACT.Tanh, scale=r_[:, i:i + 1]), t1, t_sp)
            t1 = V(lambda e: e.tensor_tensor(r.f, r.f, rst.f, MAX), t1, t_rst)
            t2 = G(lambda e: e.tensor_tensor(x.f, x.f, xc.f, MUL), t2, tk2)
            t3 = V(lambda e: e.tensor_scalar(xc.f, r.f, 1.0, None, ADD), t1, t2)
            t3 = V(lambda e: e.reciprocal(xc.f, xc.f), t3)
            t2 = V(lambda e: e.scalar_tensor_tensor(out=x.f, in0=x.f, scalar=2.0, in1=xc.f, op0=MUL, op1=MUL), t2, t3)
            t3 = V(lambda e: e.tensor_scalar(xc.f, xc.f, 2.0, -1.0, MUL, ADD), t2)
            lr_st[i] = (r, x, xc, t1, t2, t3)

        def lru_b(i):
            r, x, a, t1, t2, t3 = lr_st[i]
            t1 = A(lambda e: e.activation(r.f, r.f, ACT.Sqrt), t1, t3)
            t = G(lambda e: e.tensor_tensor(x.f, x.f, r.f, MUL), t1, t2)
            t = V(lambda e: e.tensor_tensor_scan(r.f, a.f, x.f, 0.0, MUL, ADD), t, t3)
            pool.give(x, t)
            pool.give(a, t)
            h, l, th, tl = split(r.f, t)
            pool.give(r, tl)
            yr.append(operand(h, l, th, tl) + (h, l))

        yr = []
        bg = lru_tiles()
        for _ in range(11):
            step()

        lat = []
        nq, nk = Norm(3), Norm(2)
        pend = None
        for i in range(5):
            b, tok = project("in2", 10 + i, nn3)
            s = pool.take()
            t = A(lambda e, s=s, b=b: e.activation(s.f, b.ap[:, :], ACT.Copy), tok, *s.free)
            psum.give(b, t)
            (nq if i < 3 else nk).add(s.f, t)
            lat.append((s, t))
            step()
        b, tok = project("in2", 15, nn3)
        kr = pool.take()
        tkr = A(lambda e, b=b: e.activation(kr.f, b.ap[:, :], ACT.Copy), tok, *kr.free)
        tbl2 = (rc2, rs2, t_rc2, t_rs2)
        w1, w2 = pool.take(), pool.take()
        mask = list(range(16, 32)) + list(range(16))
        t1 = V(lambda e, b=b: e.tensor_tensor(w1.f, b.ap[:, :], rc2.f, MUL), tkr, t_rc2, *w1.free)
        t2 = V(lambda e, b=b: e.stream_shuffle(w2.f, b.ap[:, :], mask), *w2.free)
        psum.give(b, t2)
        t2 = G(lambda e: e.tensor_tensor(w2.f, w2.f, rs2.f, MUL), t2, t_rs2)
        tkr = G(lambda e: e.tensor_tensor(kr.f, w1.f, w2.f, ADD), t1, t2, tkr)
        pool.give(w1, tkr)
        pool.give(w2, tkr)

        def latent(nrm, tiles, width, gname):
            rb, trb = nrm.finish(width, stat_cols(4))
            ops = []
            for k, (s, ts_) in enumerate(tiles):
                t = V(lambda e, s=s, k=k: e.scalar_tensor_tensor(out=s.f, in0=s.f, scalar=col(gname, k), in1=rb.ap[:, :],
                                                                 op0=MUL, op1=MUL), ts_, trb)
                h, l, th, tl = split(s.f, t)
                pool.give(s, tl)
                ops.append(operand(h, l, th, tl) + (h, l))
            psum.give(rb, t)
            return ops

        ql = latent(nq, lat[:3], 384, "qg")
        kl = latent(nk, lat[3:], 256, "kg")
        g_rnn, g_mla = [], []
        for m in range(8):
            g_rnn.append(sigmoid_of(*project("in2", 16 + m, nn3)))
            step()
        for _ in range(12):
            step()
        for m in range(8):
            g_mla.append(sigmoid_of(*project("in2", 24 + m, nn3)))
        free_ops(nn, P.last())

        for m in range(8):
            b, tok = project("pr", m, three(yr))
            s, t = g_rnn[m]
            t = V(lambda e, s=s, b=b: e.tensor_tensor(s.f, s.f, b.ap[:, :], MUL), tok, t)
            psum.give(b, t)
            g_rnn[m] = (s, t)
        free_ops(yr, P.last())
        pool.give(rst, G.last())

        vs = {}
        align4()
        for half in range(2):
            bk = [psum.take() for _ in range(4)]
            for k in range(2):
                offs = [block("uv", k, half * 4 + i) for i in range(4)]
                o, wt = offs[0]
                hi, lo, toks = kl[k][:3]
                for j in range(4):
                    b = bk[j]
                    js = slice(j * 128, (j + 1) * 128)
                    rh, rl = whi[:, o:o + 512], wlo[:, o:o + 512]
                    P(lambda e, b=b, js=js, hi=hi, rh=rh, k=k: e.matmul(b.ap[:, :], hi[:, js], rh, start=(k == 0), stop=False),
                      *toks, *wt, b.free)
                    P(lambda e, b=b, js=js, lo=lo, rh=rh: e.matmul(b.ap[:, :], lo[:, js], rh, start=False, stop=False))
                    tok = P(lambda e, b=b, js=js, hi=hi, rl=rl, k=k: e.matmul(b.ap[:, :], hi[:, js], rl, start=False, stop=(k == 1)))
            for j in range(4):
                b, s = bk[j], pool.take()
                q = A if j % 2 else V
                if q is A:
                    t = A(lambda e, b=b, s=s: e.activation(s.f, b.ap[:, :], ACT.Copy), tok, *s.free)
                else:
                    t = V(lambda e, b=b, s=s: e.tensor_copy(s.f, b.ap[:, :]), tok, *s.free)
                psum.give(b, t)
                vs[(j, half)] = (s, t)

        SC2 = 1.0 / math.sqrt(96.0)
        ql3, kl3 = three(ql), three(kl)
        MS, DS = stat_cols(16), stat_cols(16)
        st_free = [None] * 4
        kpair = {}

        def head_qk(h):
            if h % 2 == 0:
                b, tok = project("uk", h // 2, kl3)
                for odd in range(2):
                    s = pool.take()
                    rows = slice(64 * odd, 64 * odd + 64)
                    t = A(lambda e, s=s, b=b, rows=rows: e.activation(s.f[rows, :], b.ap[rows, :], ACT.Copy), tok, *s.free)
                    rr = slice(64, 96) if odd == 0 else slice(0, 32)
                    t2 = V(lambda e, s=s, rr=rr: e.tensor_copy(s.f[rr, :], kr.f[rr, :]), tkr, *s.free)
                    t3 = V(lambda e, s=s: e.memset(s.f[32:64, :], 0.0), *s.free) if odd else None
                    kpair[odd] = (s, t, t2, t3)
                psum.give(b, t)
            b, tok = project("uq", h, ql3)
            q = pool.take()
            t = A(lambda e: e.activation(q.f, b.ap[:, :], ACT.Copy), tok, *q.free)
            rr = slice(64, 96) if h % 2 == 0 else slice(0, 32)
            t = rope(b, q, rr, tbl2, 1, t)
            return q, t, kpair[h % 2]

        def head_scores(h, qk):
            q, tq, (k, *tks) = qk
            K = slice(0, 96) if h % 2 == 0 else slice(0, 128)
            z = 4 * (h % 4)
            res = []
            for n in range(4):
                b = psum.take()
                w = (n + 1) * 128
                P(lambda e, b=b, n=n, w=w: e.matmul(b.ap[:, 0:w], q.f[K, n * 128:(n + 1) * 128], k.f[K, 0:w],
                                                    start=True, stop=True, skip_group_check=True), tq, *tks, b.free)
                tok = P(lambda e, b=b, n=n, w=w: e.matmul(b.ap[:, n * 128:w], identb[:, :], maskb[:, m_diag:m_diag + 128],
                                                          start=False, stop=True, skip_group_check=True))
                mc, dc = stat[:, MS + z + n:MS + z + n + 1], stat[:, DS + z + n:DS + z + n + 1]
                t = V(lambda e, b=b, w=w, mc=mc: e.tensor_reduce(mc, b.ap[:, 0:w], AX, MAX), tok, st_free[h % 4])
                t = V(lambda e, mc=mc: e.tensor_scalar(mc, mc, -SC2, None, MUL), t)
                p = pool.take()
                te = A(lambda e, p=p, b=b, w=w, mc=mc, dc=dc: e.activation(p.f[:, 0:w], b.ap[:, 0:w], ACT.Exp, bias=mc,
                                                                           scale=SC2, accum_out=dc), t, *p.free, st_free[h % 4])
                psum.give(b, te)
                res.append((p, te))
            pool.give(q, tok)
            pool.give(k, tok)
            return res

        def head_values(h, res, ob):
            z = 4 * (h % 4)
            dc = stat[:, DS + z:DS + z + 4]
            t = V(lambda e: e.reciprocal(dc, dc), res[3][1])
            st_free[h % 4] = t
            ps = []
            for n in range(4):
                p, te = res[n]
                w = (n + 1) * 128
                tp = V(lambda e, p=p, w=w, n=n: e.tensor_scalar(p.f[:, 0:w], p.f[:, 0:w], dc[:, n:n + 1], None, MUL), t, te)
                ps.append((p, tp))
                st_free[h % 4] = tp
            rows = slice(64 * (h % 2), 64 * (h % 2) + 64)
            for kb in range(4):
                b = psum.take()
                for n in range(kb, 4):
                    p, tp = ps[n]
                    tok = P(lambda e, b=b, p=p, n=n, kb=kb: e.transpose(b.ap[:, n * 128:(n + 1) * 128],
                                                                        p.f[:, kb * 128:(kb + 1) * 128], ident[:, :]), tp, b.free)
                pool.give(ps[kb][0], tok) if kb == 3 else None
                pt = pool.take()
                c0 = kb * 128
                if kb % 2:
                    t = V(lambda e, b=b, pt=pt, c0=c0: e.tensor_copy(pt.f[:, c0:512], b.ap[:, c0:512]), tok, *pt.free)
                else:
                    t = A(lambda e, b=b, pt=pt, c0=c0: e.activation(pt.f[:, c0:512], b.ap[:, c0:512], ACT.Copy), tok, *pt.free)
                psum.give(b, t)
                v, tv = vs[(kb, h // 8)]
                vo = (h % 8) * 64
                tok2 = P(lambda e, pt=pt, v=v, vo=vo, c0=c0, kb=kb: e.matmul(
                    ob.ap[rows, c0:512], v.f[:, vo:vo + 64], pt.f[:, c0:512], start=(kb == 0), stop=True,
                    skip_group_check=True), t, tv, ob.free)
                pool.give(pt, tok2)
            for n in range(3):
                pool.give(ps[n][0], tok)
            return tok2

        ym = []
        ob = None
        cur = head_scores(0, head_qk(0))
        qk = head_qk(1)
        for h in range(16):
            if h % 2 == 0:
                ob = psum.take()
            nxt = head_scores(h + 1, qk) if h < 15 else None
            if h < 14:
                qk = head_qk(h + 2)
            tok = head_values(h, cur, ob)
            cur = nxt
            if h % 2:
                h_, l_, th, tl = split(ob.ap[:, :], tok)
                psum.give(ob, tl)
                ym.append(operand(h_, l_, th, tl) + (h_, l_))
        free_ops(ql, P.last())
        free_ops(kl, P.last())
        pool.give(kr, G.last())
        pool.give(rc2, V.last())
        pool.give(rs2, G.last())
        for s, _ in vs.values():
            pool.give(s, P.last())

        merged = []
        for m in range(8):
            b, tok = project("pm", m, three(ym))
            s, t = g_mla[m]
            t = V(lambda e, s=s, b=b: e.tensor_tensor(s.f, s.f, b.ap[:, :], MUL), tok, t)
            psum.give(b, t)
            w, tw_ = g_rnn[m]
            t = G(lambda e, s=s, w=w: e.tensor_tensor(s.f, s.f, w.f, ADD), t, tw_)
            pool.give(w, t)
            h, l, th, tl = split(s.f, t)
            pool.give(s, tl)
            merged.append(operand(h, l, th, tl) + (h, l))
        free_ops(ym, P.last())
        nrm = Norm(8)
        residual("out2", three(merged), nrm, gate=lambda m: mod[:, 16 + m:17 + m])
        free_ops(merged, P.last())
        rb, trb = nrm.finish(1024, stat_cols(4))
        nn = modulated(rb, trb, 40, 24)
        nn3 = three(nn)

        def conv(mt):
            b, tok = project("up", mt, nn3)
            s = pool.take()
            t = A(lambda e: e.activation(s.f, b.ap[:, :], ACT.Identity, bias=col("fcb", mt), scale=col("fcw", 88 + mt)), tok, *s.free)
            for k in (1, 2):
                t = V(lambda e, k=k: e.scalar_tensor_tensor(out=s.f[:, k:512], in0=b.ap[:, 0:512 - k],
                                                            scalar=col("fcw", (2 - k) * 44 + mt), in1=s.f[:, k:512],
                                                            op0=MUL, op1=ADD), t)
            psum.give(b, t)
            return s, t

        nrm = Norm(8)
        for half in range(2):
            acts = []
            for m in range(11):
                mt = half * 11 + m
                g_, tg = conv(mt)
                tg = A(lambda e, g_=g_: e.activation(g_.f, g_.f, ACT.Silu), tg)
                u_s, tu = conv(22 + mt)
                t = G(lambda e, g_=g_, u_s=u_s: e.tensor_tensor(g_.f, g_.f, u_s.f, MUL), tg, tu)
                pool.give(u_s, t)
                h, l, th, tl = split(g_.f, t)
                pool.give(g_, tl)
                acts.append(operand(h, l, th, tl) + (h, l))
            if half == 1:
                free_ops(nn, P.last())
            residual("dn", three(acts), nrm if half else None, half * 11, gate=lambda m: mod[:, 40 + m:41 + m])
            free_ops(acts, P.last())

        rb, trb = nrm.finish(1024, stat_cols(4))
        ends = []
        for k in range(8):
            s, ts_ = hs_[k]
            t = V(lambda e, s=s, k=k, rb=rb: e.scalar_tensor_tensor(out=s.f, in0=s.f, scalar=col("gf2", k), in1=rb.ap[:, :],
                                                             op0=MUL, op1=MUL), ts_, trb)
            ends.append(load(out[k], s.f, t))

        for q in (P, A, V, G, S):
            q.count()
        if (len(blocks) + CB - 1) // CB != NCHUNK:
            raise ValueError(f"NCHUNK should be {(len(blocks) + CB - 1) // CB}")
        with nc.Block() as block_:
            @block_.sync
            def _(e):
                S.emit(e)
                for s, n in ends:
                    e.wait_ge(s, n)

            @block_.tensor
            def _(e):
                P.emit(e)

            @block_.scalar
            def _(e):
                A.emit(e)

            @block_.vector
            def _(e):
                V.emit(e)

            @block_.gpsimd
            def _(e):
                G.emit(e)
    return nc


def columns(v, n):
    return np.asarray(v).reshape(n, 128).T


def lay_out(x):
    f = np.float32
    rs = np.concatenate
    invf1 = (np.float32(500000.0) ** (-np.arange(16, dtype=f) * f(2.0) / f(32))).astype(f)
    invf2 = (np.float32(10000.0) ** (-np.arange(16, dtype=f) / f(16))).astype(f)
    parts = dict(
        g_mix=columns(x["g_mix"], 8), g_ffn=columns(x["g_ffn"], 8), g_final=columns(x["g_final"], 8),
        n1=columns(x["norm1_g_2"], 8), n2=columns(x["norm2_g_2"], 8), gf2=columns(x["final_g_2"], 8),
        b_ada=columns(x["b_ada_2"], 48),
        convw=rs([columns(x["conv_w_2"][0, k], 10) for k in range(4)], axis=1), convb=columns(x["conv_b_2"], 10),
        ba=columns(x["b_gate_a_2"], 10), bx=columns(x["b_gate_x_2"], 10), lru=columns(x["lru_param_2"], 10),
        qg=columns(x["q_norm_g_2"], 3), kg=columns(x["kv_norm_g_2"], 2),
        fcw=rs([columns(x["ffn_conv_w_2"][0, k], 44) for k in range(3)], axis=1), fcb=columns(x["ffn_conv_b_2"], 44),
        dskip=columns(x["d_skip"], 4), are=columns(x["a_re"], 16), aim=columns(x["a_im"], 16),
        ldt=columns(np.repeat(x["log_dt"][0], 64), 16),
        if1=np.tile(invf1, 8)[:, None], sg1=np.tile(rs([-np.ones(16, f), np.ones(16, f)]), 4)[:, None],
        if2=np.tile(invf2, 8)[:, None], sg2=np.tile(rs([-np.ones(16, f), np.ones(16, f)]), 4)[:, None])
    small = np.empty((128, NSMALL), f)
    for n, w in SMALL:
        small[:, SOFF[n]:SOFF[n] + w] = parts[n]
    q, k = np.arange(128)[:, None], np.arange(128)[None, :]
    neg = f(-1e30)
    consts = np.zeros((128, 1152), f)
    consts[:, 0:128] = np.eye(128, dtype=f)
    consts[:, 128:256] = np.where(k >= q, f(0), neg)
    consts[:, 256:384] = np.where(k <= q, f(0), neg)
    consts[:, 384:512] = np.where((k <= q) & (k // 32 == q // 32), f(0), neg)
    consts[:, 512:640] = 1
    for h in range(4):
        consts[h, 640 + h * 128:640 + (h + 1) * 128] = 1
    bc = np.empty((128, 2, 16, 16), f)
    cp = np.zeros((2, 4, 128, 4, 128), f)
    for c, (bn, cn) in enumerate((("b_re", "c_re"), ("b_im", "c_im"))):
        for g in range(32):
            i, half = g // 2, g % 2
            bc[64 * half:64 * half + 64, c, i, :] = x[bn][0, g]
            o = (g % 8) * 16
            cp[c, i // 4, 64 * half:64 * half + 64, i % 4, o:o + 16] = np.asarray(x[cn][0, g]).T
    gb = np.zeros((5, 128, 2, 2, 128), f)
    for i in range(10):
        for c, n in enumerate(("w_gate_a_2", "w_gate_x_2")):
            for s in range(2):
                gb[i // 2, 64 * s:64 * s + 64, i % 2, c, 64 * s:64 * s + 64] = x[n][0, 2 * i + s]
    c_ = np.ascontiguousarray
    return dict(
        xT=c_(x["x"][0].T).reshape(8, 128, T), pT=c_(x["p"][0, 0].T).reshape(2, 128, T), small=small, consts=consts,
        pos1=c_(np.broadcast_to(x["positions"], (128, T))), pos2=c_(np.broadcast_to(x["positions_2"], (128, T))),
        cT=c_(np.broadcast_to(x["c_2"], (128, 1024))), wadaT=c_(x["w_ada_2"][0].T).reshape(48, 128, 1024),
        bcmp=bc.reshape(128, 512), cpad=cp.reshape(2, 4, 128, 512), gblk=gb.reshape(5, 128, 512))


def stream(x, blocks):
    f = np.float32
    w2 = x["w_in_2"][0]
    z = lambda r, c: np.zeros((r, c), f)
    kr = w2[:, 1920:1952]
    in2 = np.concatenate([w2[:, :1920], kr, z(1024, 32), kr, z(1024, 32), w2[:, 1952:]], axis=1)
    uq = x["w_uq_2"][0].reshape(384, 16, 96)
    uqp = np.zeros((384, 16, 128), f)
    uqp[:, 0::2, 0:96] = uq[:, 0::2]
    uqp[:, 1::2, 0:32] = uq[:, 1::2, 64:96]
    uqp[:, 1::2, 64:128] = uq[:, 1::2, 0:64]
    ukv = x["w_ukv_2"][0].reshape(256, 16, 128)
    ws = {"in": x["w_in"][0], "ap": x["w_attn_proj"][0], "ga": x["w_glu_a"][0], "gb": x["w_glu_b"][0],
          "out": x["w_out"][0], "fg": x["w_ffn_gate"][0], "fu": x["w_ffn_up"][0], "fd": x["w_ffn_down"][0],
          "pg": x["w_ple_gate"][0], "pp": x["w_ple_proj"][0], "in2": in2, "uq": uqp.reshape(384, 2048),
          "uk": ukv[:, :, :64].reshape(256, 1024), "uv": ukv[:, :, 64:].reshape(256, 1024),
          "pr": x["w_proj_rnn_2"][0], "pm": x["w_proj_mla_2"][0], "out2": x["w_out_2"][0],
          "up": x["w_up_2"][0], "dn": x["w_down_2"][0], "zero": z(128, 128)}
    out = np.zeros((NCHUNK, 128, CB * 128), f)
    for n, (name, k, m) in enumerate(blocks):
        out[n // CB, :, (n % CB) * 128:(n % CB + 1) * 128] = ws[name][k * 128:(k + 1) * 128, m * 128:(m + 1) * 128]
    return out


def kernel(**inputs):
    import concourse.bacc as bacc
    from concourse.bass_utils import run_bass_kernel_spmd

    x = {n: np.asarray(a) for n, a in inputs.items()}
    nc = bacc.Bacc("TRN2", target_bir_lowering=False, num_devices=1)
    arrays = lay_out(x)
    args = {n: nc.dram_tensor(n, a.shape, mybir.dt.from_np(a.dtype), kind="ExternalInput").ap() for n, a in arrays.items()}
    wst = nc.dram_tensor("wst", (NCHUNK, 128, CB * 128), F32, kind="ExternalInput").ap()
    out = nc.dram_tensor("out", (8, 128, T), F32, kind="ExternalOutput").ap()
    blocks = []
    program(nc, 0, blocks, wst, out=out, **args)
    arrays["wst"] = stream(x, blocks)
    r = run_bass_kernel_spmd(nc, [arrays], core_ids=[0])
    got = r.results[0]["out"]
    return np.ascontiguousarray(np.asarray(got).reshape(1024, T).T).reshape(1, T, 1024)
```

```python
import math
from collections import deque
from contextlib import ExitStack

import numpy as np

import concourse.bass as bass
from concourse import mybir

F32 = mybir.dt.float32
F32R = mybir.dt.float32r
BF16 = mybir.dt.bfloat16
I32 = mybir.dt.int32
ALU = mybir.AluOpType
ACT = mybir.ActivationFunctionType
AX = mybir.AxisListType.X
ADD, SUB, MUL, MAX, MIN = ALU.add, ALU.subtract, ALU.mult, ALU.max, ALU.min

T = 512
CB = 8
NRAW, NHL = 4, 3
NSLOT = 78
NCHUNK = 286
NFILL = 8
HALF_PI = math.pi / 2
PI_IN = 3.1415925
MAGIC = 12582912.0
TWO_PI_1 = 6.28125
TWO_PI_2 = 0.0019350051879882812
TWO_PI_3 = 3.0199159819e-07

SMALL = [("g_mix", 8), ("g_ffn", 8), ("g_final", 8), ("n1", 8), ("n2", 8), ("gf2", 8), ("b_ada", 48),
         ("convw", 40), ("convb", 10), ("ba", 10), ("bx", 10), ("lru", 10), ("qg", 3), ("kg", 2),
         ("fcw", 132), ("fcb", 44), ("dskip", 4), ("are", 16), ("aim", 16), ("ldt", 16),
         ("if1", 1), ("sg1", 1), ("if2", 1), ("sg2", 1)]
SOFF = {}
_o = 0
for _n, _w in SMALL:
    SOFF[_n] = _o
    _o += _w
NSMALL = _o


class Token:

    def __init__(self, queue, index):
        self.queue, self.index = queue, index


class Queue:

    def __init__(self, sem):
        self.sem, self.ops, self.signals = sem, [], []

    def __call__(self, fn, *after):
        after = [t for t in after if t is not None]
        for t in after:
            if isinstance(t, Token):
                t.queue.signals[t.index] = True
        self.ops.append((fn, after))
        self.signals.append(False)
        return Token(self, len(self.ops) - 1)

    def last(self):
        return Token(self, len(self.ops) - 1)

    def value(self, index):
        return self.counts[index]

    def count(self):
        n, self.counts = 0, []
        for s in self.signals:
            n += s
            self.counts.append(n)

    def emit(self, eng):
        seen = {}
        for (fn, after), signal in zip(self.ops, self.signals):
            need = {}
            for t in after:
                sem, val = (t.queue.sem, t.queue.value(t.index)) if isinstance(t, Token) else t
                key = id(sem)
                if key not in need or need[key][1] < val:
                    need[key] = (sem, val)
            for key, (sem, val) in need.items():
                if seen.get(key, 0) < val:
                    eng.wait_ge(sem, val)
                    seen[key] = val
            ins = fn(eng)
            if signal:
                ins.then_inc(self.sem, 1)


class Bank:
    def __init__(self, ap):
        self.ap, self.free = ap, None


class Slot:
    def __init__(self, f, r):
        self.f, self.r, self.free = f, r, []


class Pool:

    def __init__(self, places):
        self.q = deque(places)
        self.least = len(places)

    def take(self):
        p = self.q.popleft()
        self.least = min(self.least, len(self.q))
        return p

    def give(self, p, *tokens):
        p.free = list(tokens)
        self.q.append(p)


def program(nc, blocks, wst, xT, pT, small, consts, pos1, pos2, cT, wadaT, bcmp, cpad, gblk, spare, out):
    ctx = ExitStack()
    with ctx:
        def sb(name, shape, dt=F32):
            return ctx.enter_context(nc.sbuf_tensor(name, shape, dt))

        def sem(name):
            return ctx.enter_context(nc.semaphore(name))

        raw = sb("raw", [128, NRAW * CB * 128])
        whi = sb("whi", [128, NHL * CB * 128], F32R)
        wlo = sb("wlo", [128, NHL * CB * 128], F32R)
        sm = sb("sm", [128, NSMALL])
        ident = sb("ident", [128, 128])
        ones = sb("ones", [128, 128])
        maskb = sb("maskb", [128, 3 * 128], BF16)
        identb = sb("identb", [128, 128], BF16)
        mod = sb("mod", [128, 48])
        scl = sb("scl", [128, 96])
        stat = sb("stat", [128, 320])
        places = []
        for i in range(NSLOT):
            with nc.sbuf_tensor(f"slotf{i}", [128, T], F32) as slotf:
                pass
            places.append(Slot(slotf[:, :], sb(f"slotr{i}", [128, T], F32R)[:, :]))
        banks = [ctx.enter_context(nc.psum_tensor(f"bank{i}", [128, 512], F32)) for i in range(8)]

        P = Queue(sem("s_pe"))
        A = Queue(sem("s_act"))
        V = Queue(sem("s_dve"))
        G = Queue(sem("s_pool"))
        S = Queue(sem("s_sp"))

        psum = Pool([Bank(b) for b in banks])
        pool = Pool(places)

        dma_sems = [sem(f"s_d{i}") for i in range(24)]
        dma_count = [0] * 24
        dma_turn = [0]

        def load(dst, src, *after):
            i = dma_turn[0] % 24
            dma_turn[0] += 1
            prev = (dma_sems[i], dma_count[i]) if dma_count[i] else None
            dma_count[i] += 16
            s, n = dma_sems[i], dma_count[i]
            S(lambda e: e.dma_start(dst, src).then_inc(s, 16), prev, *after)
            return (s, n)

        def col(name, i=0, n=1):
            return sm[:, SOFF[name] + i:SOFF[name] + i + n]

        W = CB * 128
        s_w = [sem(f"s_w{i}") for i in range(NRAW)]
        raw_free = [None] * NRAW
        hl_free = [None] * NHL
        chunk_tok = {}
        lo_turn = {"mode": "VG"}
        
        def chunk_dma(c):
            if c >= NCHUNK:
                return
            i = c % NRAW
            s = s_w[i]
            S(lambda e: e.dma_start(raw[:, i * W:(i + 1) * W], wst[c]).then_inc(s, 16), raw_free[i])

        def chunk_prep(c):
            if c >= NCHUNK:
                return
            i, j = c % NRAW, c % NHL
            r, h, l = raw[:, i * W:(i + 1) * W], whi[:, j * W:(j + 1) * W], wlo[:, j * W:(j + 1) * W]
            th = A(lambda e: e.activation(h, r, ACT.Copy), (s_w[i], 16 * (c // NRAW + 1)), hl_free[j])
            m = lo_turn["mode"]
            q = V if m[c % len(m)] == "V" else G
            tl = q(lambda e: e.tensor_tensor(l, r, h.bitcast(F32), SUB), th, hl_free[j])
            raw_free[i] = tl
            chunk_tok[c] = (th, tl)


        def block(name, kt, mt):
            n = len(blocks)
            blocks.append((name, kt, mt))
            c = n // CB
            if n % CB == 0:
                if c > 0:
                    hl_free[(c - 1) % NHL] = P.last()
                if c == 0:
                    chunk_prep(0)
                    chunk_prep(1)
                chunk_prep(c + 2)
                chunk_dma(c + NRAW - 1) if c > 0 else None
            o = (c % NHL) * W + (n % CB) * 128
            return o, chunk_tok[c]

        def align4():
            while len(blocks) % 4:
                block("zero", 0, 0)

        def mm(bank, o, rhs_hi, rhs_lo, first, last, *after, cols=512, width=128):
            wh, wl = whi[:, o:o + width], wlo[:, o:o + width]
            P(lambda e: e.matmul(bank, wh, rhs_hi, start=first, stop=False), *after)
            P(lambda e: e.matmul(bank, wh, rhs_lo, start=False, stop=False))
            return P(lambda e: e.matmul(bank, wl, rhs_hi, start=False, stop=last))

        def project(name, mt, xs, k0=0):
            return whole(gproject(name, mt, xs, k0))

        def whole(gen):
            while True:
                try:
                    next(gen)
                except StopIteration as e:
                    return e.value

        def gproject(name, mt, xs, k0=0):
            b = psum.take()
            n = len(xs)
            for k, (hi, lo, toks) in enumerate(xs):
                o, wt = block(name, k0 + k, mt)
                tok = mm(b.ap[:, :], o, hi, lo, k == 0, k == n - 1, *toks, *wt, *([b.free] if k == 0 else []))
                yield
            return b, tok

        def beside(gen, blocks_, pieces, count):
            n = done = 0
            while True:
                try:
                    next(gen)
                except StopIteration as e:
                    for _ in pieces:
                        pass
                    return e.value
                n += 1
                while done < count and done * blocks_ < n * count:
                    done += 1
                    next(pieces, None)

        def project2(name, m0, name1, m1, xs):
            b0, b1 = psum.take(), psum.take()
            n = len(xs)
            for k, (hi, lo, toks) in enumerate(xs):
                for b, nm, m in ((b0, name, m0), (b1, name1, m1)):
                    o, wt = block(nm, k, m)
                    tok = mm(b.ap[:, :], o, hi, lo, k == 0, k == n - 1, *toks, *wt, *([b.free] if k == 0 else []))
                    if b is b0:
                        tok0 = tok
            return (b0, tok0), (b1, tok)

        def split(src, *after, q=None, hi_scale=None):
            h, l = pool.take(), pool.take()
            q = q or V
            th = A(lambda e: e.activation(h.r, src, ACT.Copy), *h.free, *after)
            tl = q(lambda e: e.tensor_tensor(l.r, src, h.r.bitcast(F32), SUB), th, *l.free)
            return h, l, th, tl

        def operand(h, l, th, tl):
            return (h.r, l.r, (th, tl))

        xs = []
        for k in range(8):
            s = pool.take()
            xs.append((s, load(s.f, xT[k], *s.free)))
        t_sm = load(sm[:, :], small[:, :])
        cst = pool.take()
        t_c = load(cst.f[:, 0:512], consts[:, 0:512])
        t_o = load(ones[:, :], consts[:, 512:640])
        t_id = load(ident[:, :], consts[:, 0:128])
        t_idb = V(lambda e: e.tensor_copy(identb[:, :], cst.f[:, 0:128]), t_c)
        t_mb = V(lambda e: e.tensor_copy(maskb[:, :], cst.f[:, 128:512]), t_c)
        pool.give(cst, t_mb)
        m_prev, m_diag, m_blk = 0, 128, 256
        t_eps = V(lambda e: e.memset(scl[:, 95:96], 1e-6))
        t_half = V(lambda e: e.memset(scl[:, 94:95], -0.5))

        def sincos(src, dst_s, dst_c, tmp, q, *after):
            t = q(lambda e: e.tensor_scalar(tmp, src, 1.0 / (2 * math.pi), MAGIC, MUL, ADD), *after)
            t = q(lambda e: e.tensor_scalar(tmp, tmp, MAGIC, None, SUB), t)
            for c in (TWO_PI_1, TWO_PI_2, TWO_PI_3):
                t = V(lambda e, c=c: e.scalar_tensor_tensor(out=src, in0=tmp, scalar=-c, in1=src, op0=MUL, op1=ADD), t)
            t1 = q(lambda e: e.tensor_scalar(src, src, PI_IN, -PI_IN, MIN, MAX), t)
            ts = A(lambda e: e.activation(dst_s, src, ACT.Sin), t1)
            t = q(lambda e: e.tensor_scalar(tmp, src, HALF_PI, 2 * math.pi, ALU.is_gt, MUL), t1)
            t = V(lambda e: e.scalar_tensor_tensor(out=tmp, in0=src, scalar=HALF_PI, in1=tmp, op0=ADD, op1=SUB), t)
            t = q(lambda e: e.tensor_scalar(tmp, tmp, PI_IN, -PI_IN, MIN, MAX), t)
            tc = A(lambda e: e.activation(dst_c, tmp, ACT.Sin), t)
            return ts, tc

        def rope_table(pos, invf, sign):
            pi, c, s, tmp = pool.take(), pool.take(), pool.take(), pool.take()
            tp = load(pi.f.bitcast(I32), pos[:, :], *pi.free)
            t = V(lambda e: e.tensor_copy(s.f, pi.f.bitcast(I32)), tp, *s.free)
            t = V(lambda e: e.tensor_scalar(pi.f, s.f, invf, None, MUL), t, t_sm)
            ts, tc = sincos(pi.f, s.f, c.f, tmp.f, V, t, *c.free, *tmp.free)
            t = V(lambda e: e.tensor_scalar(s.f, s.f, sign, None, MUL), ts)
            pool.give(pi, ts, tc)
            pool.give(tmp, tc)
            return c, s, tc, t

        class Norm:

            def __init__(self, n):
                self.b, self.n, self.k = psum.take(), n, 0

            def add(self, src, *after, scale=1.0):
                sq = pool.take()
                t = A(lambda e: e.activation(sq.f, src, ACT.Square, scale=scale), *sq.free, *after)
                b, k, n = self.b, self.k, self.n
                for j in range(4):
                    tok = P(lambda e, j=j: e.matmul(b.ap[:, j:j + 1], sq.f[:, j * 128:(j + 1) * 128], ones[:, 0:1],
                                                    start=(k == 0 and j == 0), stop=(k == n - 1),
                                                    skip_group_check=True), t, t_o, b.free)
                pool.give(sq, tok)
                self.tok = tok
                self.k += 1
                return t

            def finish(self, width, so):
                b = self.b
                st = stat[:, so:so + 4]
                t = V(lambda e: e.tensor_scalar(st, b.ap[:, 0:4], 1.0 / width, 1e-6, MUL, ADD), self.tok)
                psum.give(b, t)
                t = G(lambda e: e.tensor_tensor(st, st, scl[:, 94:95].to_broadcast([128, 4]), ALU.pow), t, t_half)
                dg = pool.take()
                t = V(lambda e: e.tensor_tensor(dg.f.rearrange("p (j c) -> p j c", j=4),
                                                ident[:, :].unsqueeze(1).to_broadcast([128, 4, 128]),
                                                st.unsqueeze(2).to_broadcast([128, 4, 128]), MUL), t, *dg.free, t_id)
                o = psum.take()
                t = P(lambda e: e.matmul(o.ap[:, :], ones[:, :], dg.f, start=True, stop=True), t, o.free)
                pool.give(dg, t)
                return o, t

        def bank_give(b, tok):
            psum.q.append(b)
            b.free = tok

        psum.give = bank_give

        so_next = [0]

        def stat_cols(n):
            o = so_next[0]
            so_next[0] = o + n
            if o + n > 320:
                raise ValueError("stat")
            return o

        for c in range(NRAW):
            chunk_dma(c)
        nrm = Norm(8)
        for s, t in xs:
            nrm.add(s.f, t)
        rb, trb = nrm.finish(1024, stat_cols(4))
        n1 = []
        for k, (s, t) in enumerate(xs):
            t = V(lambda e, s=s, k=k, rb=rb: e.scalar_tensor_tensor(out=s.f, in0=s.f, scalar=col("g_mix", k), in1=rb.ap[:, :],
                                                             op0=MUL, op1=MUL), t, trb, t_sm)
            last = t
            h, l, th, tl = split(s.f, t, q=(G if k % 2 else V))
            n1.append(operand(h, l, th, tl) + (h, l))
            pool.give(s, th, tl)
        psum.give(rb, last)
        n1s = n1
        n1 = [x[:3] for x in n1]

        def ssm():
            ys = []
            us = []
            for j in range(4):
                b, tok = project("in", 36 + j, n1)
                u = pool.take()
                t = A(lambda e, b=b, u=u: e.activation(u.f, b.ap[:, :], ACT.Copy), tok, *u.free)
                psum.give(b, t)
                us.append((u, t))
                yield
            pp = pool.take()
            pv = [pp.f[:, 16 * i:16 * i + 16] for i in range(32)]
            (dt, x_, e_, ang, tmp, sn, cs, mag, bre, bim, nr, den, zre, zim, u1, u2) = pv[:16]
            t_dt = A(lambda e: e.activation(dt, col("ldt", 0, 16), ACT.Exp), t_sm, *pp.free)
            t = V(lambda e: e.tensor_tensor(x_, col("are", 0, 16), dt, MUL), t_dt)
            t = V(lambda e: e.tensor_scalar(x_, x_, 1.0 / 256, None, MUL), t)
            t = V(lambda e: e.tensor_scalar(e_, x_, 1.0 / 720, 1.0 / 120, MUL, ADD), t)
            for c in (1.0 / 24, 1.0 / 6, 0.5, 1.0):
                t = V(lambda e: e.tensor_tensor(e_, e_, x_, MUL), t)
                t = V(lambda e, c=c: e.tensor_scalar(e_, e_, c, None, ADD), t)
            t = V(lambda e: e.tensor_tensor(e_, e_, x_, MUL), t)
            for _ in range(8):
                t = V(lambda e: e.scalar_tensor_tensor(out=e_, in0=e_, scalar=2.0, in1=e_, op0=ADD, op1=MUL), t)
            t_mag = V(lambda e: e.tensor_scalar(mag, e_, 1.0, None, ADD), t)
            yield
            t = V(lambda e: e.tensor_tensor(ang, col("aim", 0, 16), dt, MUL), t_dt)
            ts, tc = sincos(ang, sn, cs, tmp, V, t)
            yield
            t1 = V(lambda e: e.tensor_tensor(bre, mag, cs, MUL), tc, t_mag)
            t2 = V(lambda e: e.tensor_tensor(bim, mag, sn, MUL), ts)
            t = V(lambda e: e.tensor_scalar(nr, bre, 1.0, None, SUB), t1)
            t3 = V(lambda e: e.tensor_tensor(den, col("are", 0, 16), col("are", 0, 16), MUL))
            t4 = V(lambda e: e.tensor_tensor(u1, col("aim", 0, 16), col("aim", 0, 16), MUL))
            t3 = V(lambda e: e.tensor_tensor(den, den, u1, ADD), t3, t4)
            t3 = V(lambda e: e.reciprocal(den, den), t3)
            t = V(lambda e: e.tensor_tensor(zre, nr, col("are", 0, 16), MUL), t)
            t2 = V(lambda e: e.tensor_tensor(u1, bim, col("aim", 0, 16), MUL), t2, t3)
            t = V(lambda e: e.tensor_tensor(zre, zre, u1, ADD), t, t2)
            t_zr = V(lambda e: e.tensor_tensor(zre, zre, den, MUL), t, t3)
            t = V(lambda e: e.tensor_tensor(zim, bim, col("are", 0, 16), MUL), t2)
            t2 = V(lambda e: e.tensor_tensor(u2, nr, col("aim", 0, 16), MUL), t)
            t = V(lambda e: e.tensor_tensor(zim, zim, u2, SUB), t2)
            t_zi = V(lambda e: e.tensor_tensor(zim, zim, den, MUL), t, t3)
            yield

            bs = pool.take()
            tb = load(bs.f[:, :], bcmp[:, :], *bs.free)
            b_re, b_im = (bs.f[:, 256 * i:256 * i + 256].rearrange("p (i c) -> p i c", i=16) for i in range(2))
            bq, bw = pool.take(), pool.take()
            q_re, q_im = (bq.f[:, 256 * i:256 * i + 256].rearrange("p (i c) -> p i c", i=16) for i in range(2))
            w_re, w_im = (bw.f[:, 256 * i:256 * i + 256].rearrange("p (i c) -> p i c", i=16) for i in range(2))
            zr_b = zre.unsqueeze(2).to_broadcast([128, 16, 16])
            zi_b = zim.unsqueeze(2).to_broadcast([128, 16, 16])
            t1 = V(lambda e: e.tensor_tensor(q_re, b_re, zr_b, MUL), tb, t_zr, *bq.free)
            t2 = V(lambda e: e.tensor_tensor(w_re, b_im, zi_b, MUL), t_zi, *bw.free)
            t3 = V(lambda e: e.tensor_tensor(q_im, b_im, zr_b, MUL))
            t4 = V(lambda e: e.tensor_tensor(w_im, b_re, zi_b, MUL))
            yield
            bpad = [pool.take() for _ in range(8)]
            bt = []
            for c, (qq, ww, op) in enumerate(((q_re, w_re, SUB), (q_im, w_im, ADD))):
                for j in range(4):
                    d = bpad[4 * c + j]
                    tz = G(lambda e, d=d: e.memset(d.f, 0.0), *d.free)
                    for half in range(2):
                        rows = slice(64 * half, 64 * half + 64)
                        for k in range(4):
                            o = k * 160 + half * 16
                            t = V(lambda e, d=d, rows=rows, o=o, j=j, k=k, qq=qq, ww=ww, op=op: e.tensor_tensor(
                                d.f[rows, o:o + 16], qq[rows, 4 * j + k, :], ww[rows, 4 * j + k, :], op), tz, t1, t2, t3, t4)
                    bt.append(t)
                    if j % 2:
                        yield
            pool.give(bs, t4)
            pool.give(bq, bt[-1])
            pool.give(bw, bt[-1])

            el_r, el_i, eh = pool.take(), pool.take(), pool.take()
            lr, li = (s.f.rearrange("p (i t) -> p i t", i=16) for s in (el_r, el_i))
            hr, hi_ = (eh.f[:, 256 * i:256 * i + 256].rearrange("p (i t) -> p i t", i=16) for i in range(2))
            pw = pool.take()
            wa, wb = (pw.f[:, 256 * i:256 * i + 256] for i in range(2))
            cur_r, cur_i, nxt_r, nxt_i = pv[16], pv[17], pv[18], pv[19]

            def square(*after):
                a = V(lambda e, r=cur_r: e.tensor_tensor(u1, r, r, MUL), *after)
                b = V(lambda e, i=cur_i: e.tensor_tensor(u2, i, i, MUL), *after)
                d = V(lambda e, r=cur_r, i=cur_i: e.tensor_tensor(nxt_i, r, i, MUL), *after)
                a = V(lambda e: e.tensor_tensor(nxt_r, u1, u2, SUB), a, b)
                d = V(lambda e: e.tensor_scalar(nxt_i, nxt_i, 2.0, None, MUL), d)
                a = V(lambda e: e.tensor_copy(cur_r, nxt_r), a)
                d = V(lambda e: e.tensor_copy(cur_i, nxt_i), d)
                return a, d

            ta = V(lambda e: e.tensor_copy(cur_r, cs), tc)
            tb_ = V(lambda e: e.tensor_copy(cur_i, sn), ts)

            def table(R, I, bits, tr, ti, *after):
                t1 = V(lambda e: e.memset(R[:, :, 0:1], 1.0), *after)
                t2 = V(lambda e: e.memset(I[:, :, 0:1], 0.0), *after)
                w1 = lambda n: wa[:, 0:16 * n].rearrange("p (i t) -> p i t", i=16)
                w2 = lambda n: wb[:, 0:16 * n].rearrange("p (i t) -> p i t", i=16)
                for b in range(bits):
                    n = 1 << b
                    cr = cur_r.unsqueeze(2).to_broadcast([128, 16, n])
                    ci = cur_i.unsqueeze(2).to_broadcast([128, 16, n])
                    a = V(lambda e, n=n, cr=cr: e.tensor_tensor(w1(n), R[:, :, 0:n], cr, MUL), tr, t1, t2)
                    d = V(lambda e, n=n, ci=ci: e.tensor_tensor(w2(n), I[:, :, 0:n], ci, MUL), ti, t1, t2)
                    t1 = V(lambda e, n=n: e.tensor_tensor(R[:, :, n:2 * n], w1(n), w2(n), SUB), a, d)
                    a = V(lambda e, n=n, ci=ci: e.tensor_tensor(w1(n), R[:, :, 0:n], ci, MUL), t1)
                    d = V(lambda e, n=n, cr=cr: e.tensor_tensor(w2(n), I[:, :, 0:n], cr, MUL), t1)
                    t2 = V(lambda e, n=n: e.tensor_tensor(I[:, :, n:2 * n], w1(n), w2(n), ADD), a, d)
                    tr, ti = square(t2)
                    yield
                return tr, ti, t1, t2

            tr, ti, l1, l2 = yield from table(lr, li, 5, ta, tb_, *el_r.free, *el_i.free, *pw.free)
            tr, ti, h1_, h2_ = yield from table(hr, hi_, 4, tr, ti, *eh.free)
            pool.give(pw, h2_)
            t_pow = h2_

            late_c = deque()

            def c_product(st, cc, yb):
                k, gr, t1, h2, t3 = st
                for c, (hh, th) in enumerate(((gr, t1), (h2, t3))):
                    s, tcx = cc[c]
                    tok = P(lambda e, c=c, k=k, s=s, hh=hh, yb=yb: e.matmul(
                        yb.ap[:, :], s.f[:, k * 128:(k + 1) * 128], hh.f, start=(k == 0 and c == 0),
                        stop=(k == 3 and c == 1)), th, tcx, yb.free)
                    pool.give(hh, tok)
                return tok

            for j in range(4):
                u, tu = us[j]
                bT = []
                for c in range(2):
                    b = psum.take()
                    d = bpad[4 * c + j]
                    for k in range(4):
                        tok = P(lambda e, b=b, d=d, k=k: e.transpose(b.ap[:, k * 128:(k + 1) * 128],
                                                                     d.f[:, k * 128:(k + 1) * 128], ident[:, :]),
                                bt[4 * c + j], b.free, t_id)
                    s = pool.take()
                    t = A(lambda e, b=b, s=s: e.activation(s.f, b.ap[:, :], ACT.Copy), tok, *s.free)
                    psum.give(b, t)
                    pool.give(d, tok)
                    bT.append((s, t))
                cc = []
                for c in range(2):
                    s = pool.take()
                    cc.append((s, load(s.f, cpad[c, j], *s.free)))
                yb = None
                pend = None
                for k in range(4):
                    i = 4 * j + k
                    er, ei, w = pool.take(), pool.take(), pool.take()
                    v3 = lambda s: s.f.rearrange("p (a b) -> p a b", a=16)
                    br_ = lr[:, i, :].unsqueeze(1).to_broadcast([128, 16, 32])
                    bi_ = li[:, i, :].unsqueeze(1).to_broadcast([128, 16, 32])
                    ar_ = hr[:, i, :].unsqueeze(2).to_broadcast([128, 16, 32])
                    ai_ = hi_[:, i, :].unsqueeze(2).to_broadcast([128, 16, 32])
                    t1 = G(lambda e, er=er, a=ar_, b=br_: e.tensor_tensor(v3(er), a, b, MUL), t_pow, *er.free)
                    t2 = G(lambda e, w=w, a=ai_, b=bi_: e.tensor_tensor(v3(w), a, b, MUL), *w.free)
                    t_er = G(lambda e, er=er, w=w: e.tensor_tensor(er.f, er.f, w.f, SUB), t1, t2)
                    t1 = G(lambda e, ei=ei, a=ar_, b=bi_: e.tensor_tensor(v3(ei), a, b, MUL), *ei.free)
                    t2 = G(lambda e, w=w, a=ai_, b=br_: e.tensor_tensor(v3(w), a, b, MUL), t_er)
                    t_ei = G(lambda e, ei=ei, w=w: e.tensor_tensor(ei.f, ei.f, w.f, ADD), t1, t2)
                    pool.give(w, t_ei)
                    bk = []
                    for c in range(2):
                        b = psum.take()
                        s, t = bT[c]
                        bk.append((b, P(lambda e, b=b, s=s, k=k, u=u: e.matmul(b.ap[:, :], s.f[:, k * 128:(k + 1) * 128], u.f,
                                                                          start=True, stop=True), t, tu, b.free)))
                    (b0, p0), (b1, p1) = bk
                    gr, gi, w1, w2 = (pool.take() for _ in range(4))
                    t1 = V(lambda e, gr=gr, b0=b0, er=er: e.tensor_tensor(gr.f, b0.ap[:, :], er.f, MUL), p0, t_er, *gr.free)
                    t2 = V(lambda e, w1=w1, b1=b1, ei=ei: e.tensor_tensor(w1.f, b1.ap[:, :], ei.f, MUL), p1, t_ei, *w1.free)
                    t3 = V(lambda e, gi=gi, b1=b1, er=er: e.tensor_tensor(gi.f, b1.ap[:, :], er.f, MUL), *gi.free)
                    psum.give(b1, t3)
                    t4 = V(lambda e, w2=w2, b0=b0, ei=ei: e.tensor_tensor(w2.f, b0.ap[:, :], ei.f, MUL), *w2.free)
                    psum.give(b0, t4)
                    t1 = G(lambda e, gr=gr, w1=w1: e.tensor_tensor(gr.f, gr.f, w1.f, ADD), t1, t2)
                    t3 = G(lambda e, gi=gi, w2=w2: e.tensor_tensor(gi.f, gi.f, w2.f, SUB), t3, t4)
                    yield
                    if late_c:
                        c_product(late_c.popleft(), cc, yb)
                    mg = mag[:, i:i + 1].to_broadcast([128, 512])
                    sr = V(lambda e, w1=w1, gr=gr, mg=mg: e.tensor_tensor_scan(w1.f, mg, gr.f, 0.0, MUL, ADD), t1, t_mag)
                    si = V(lambda e, w2=w2, gi=gi, mg=mg: e.tensor_tensor_scan(w2.f, mg, gi.f, 0.0, MUL, ADD), t3)
                    h2 = pool.take()
                    t1 = V(lambda e, gr=gr, w1=w1, er=er: e.tensor_tensor(gr.f, w1.f, er.f, MUL), sr)
                    t2 = V(lambda e, gi=gi, w2=w2, ei=ei: e.tensor_tensor(gi.f, w2.f, ei.f, MUL), si)
                    t1 = V(lambda e, gr=gr, gi=gi: e.tensor_tensor(gr.f, gr.f, gi.f, SUB), t1, t2)
                    t3 = V(lambda e, h2=h2, w1=w1, ei=ei: e.tensor_tensor(h2.f, w1.f, ei.f, MUL), *h2.free)
                    t4 = V(lambda e, gi=gi, w2=w2, er=er: e.tensor_tensor(gi.f, w2.f, er.f, MUL), t1)
                    t3 = V(lambda e, h2=h2, gi=gi: e.scalar_tensor_tensor(out=h2.f, in0=h2.f, scalar=-1.0, in1=gi.f,
                                                                          op0=MUL, op1=SUB), t3, t4)
                    pool.give(w1, t3)
                    pool.give(w2, t4)
                    pool.give(er, t4)
                    pool.give(ei, t3)
                    pool.give(gi, t3)
                    yield
                    if yb is None:
                        yb = psum.take()
                    late_c.append((k, gr, t1, h2, t3))
                    if k == 3:
                        yield
                        tok = c_product(late_c.popleft(), cc, yb)
                yt = pool.take()
                t = V(lambda e, yt=yt, u=u, yb=yb, j=j: e.scalar_tensor_tensor(
                    out=yt.f, in0=u.f, scalar=col("dskip", j), in1=yb.ap[:, :], op0=MUL, op1=ADD), tok, tu, *yt.free)
                psum.give(yb, t)
                pool.give(u, t)
                for s, _ in bT + cc:
                    pool.give(s, tok)
                t = A(lambda e, yt=yt: e.activation(yt.f, yt.f, ACT.Gelu_apprx_tanh), t)
                h, l, th, tl = split(yt.f, t)
                pool.give(yt, tl)
                ys.append(operand(h, l, th, tl) + (h, l))
                yield
            ssm_out.extend(ys)
            for s in (el_r, el_i, eh):
                pool.give(s, t_ei)
            pool.give(pp, t3)

        ssm_out = []
        bg = ssm()

        def step(n=1):
            for _ in range(n):
                try:
                    next(bg)
                except StopIteration:
                    return

        for _ in range(4):
            step()
        rc1, rs1, t_rc1, t_rs1 = rope_table(pos1, col("if1"), col("sg1"))

        DIL = (1, 4, 16)
        SCALE = 1.0 / math.sqrt(128.0)
        OT = [[None] * 4 for _ in range(3)]
        st_t = {}
        MO, DO = stat_cols(48), stat_cols(48)

        def perm(ap, d):
            if d == 1:
                return ap
            if len(ap.shape) == 2:
                return ap.rearrange("p (r l) -> p l r", r=d)

        def nat(ap, d):
            return ap if d == 1 else ap.rearrange("p (l r) -> p l r", r=d)

        def rope(b, dst, rows, tbl, d, tok_copy):
            c, s, tc_, ts_ = tbl
            w1, w2 = pool.take(), pool.take()
            mask = list(range(16, 32)) + list(range(16))
            t1 = V(lambda e: e.tensor_tensor(w1.f[rows, :], b.ap[rows, :], c.f[rows, :], MUL), tok_copy, tc_, *w1.free)
            t2 = V(lambda e: e.stream_shuffle(w2.f[rows, :], b.ap[rows, :], mask), *w2.free)
            psum.give(b, t2)
            q = G if rows.start == 0 else V
            q2 = V if d != 1 or rows.start else q
            t2 = q(lambda e: e.tensor_tensor(w2.f[rows, :], w2.f[rows, :], s.f[rows, :], MUL), t2, ts_)
            t = q2(lambda e: e.tensor_tensor(perm(dst.f[rows, :], d), nat(w1.f[rows, :], d), nat(w2.f[rows, :], d), ADD),
                  t1, t2, tok_copy)
            pool.give(w1, t)
            pool.give(w2, t)
            return t

        tbl1 = (rc1, rs1, t_rc1, t_rs1)

        def qkv(g, h):
            d = DIL[g]
            got = []
            for part in range(3):
                b, tok = yield from gproject("in", part * 12 + g * 4 + h, n1)
                s = pool.take()
                t = A(lambda e, b=b, s=s: e.activation(perm(s.f, d), nat(b.ap[:, :], d), ACT.Copy), tok, *s.free)
                if part < 2:
                    t = rope(b, s, slice(0, 32), tbl1, d, t)
                else:
                    psum.give(b, t)
                got.append((s, t))
                step(2 if part == 0 else 1)
            return got

        def scores(g, h, got):
            (q, tq), (k, tk), (v, tv) = got
            if g == 0:
                parts = [[(0, 0, 128, m_diag, 128), (1, 128, 256, m_prev, 256)],
                         [(2, 0, 256, m_prev, 256), (3, 256, 256, m_prev, 256)]]
            else:
                parts = [[(n, n * 128, 128, m_diag if g == 1 else m_blk, 128) for n in range(4)]]
            probs = {}
            for part in parts:
                b = psum.take()
                for n, o, w, mo, mw in part:
                    k0 = (n - 1) * 128 if w == 256 else n * 128
                    P(lambda e, n=n, o=o, w=w, k0=k0, b=b: e.matmul(b.ap[:, o:o + w], q.f[:, n * 128:(n + 1) * 128],
                                                                    k.f[:, k0:k0 + w], start=True, stop=False),
                      tq, tk, b.free)
                    tok = P(lambda e, o=o, w=w, mo=mo, b=b: e.matmul(b.ap[:, o:o + w], identb[:, :], maskb[:, mo:mo + w],
                                                                     start=False, stop=True), t_idb, t_mb)
                mcol = lambda n: MO + g * 16 + n * 4 + h
                t = None
                if g == 0:
                    for n, o, w, *_ in part:
                        t = V(lambda e, n=n, o=o, w=w, b=b: e.tensor_reduce(stat[:, mcol(n):mcol(n) + 1], b.ap[:, o:o + w], AX, MAX), tok)
                else:
                    t = V(lambda e, b=b: e.tensor_reduce(stat[:, MO + g * 16 + h:MO + g * 16 + 16:4],
                                                         b.ap[:, :].rearrange("p (n c) -> p n c", n=4), AX, MAX), tok)
                n0, n1_ = part[0][0], part[-1][0]
                neg = scl[:, 4 * ((h * 3 + g) % 8) + n0:4 * ((h * 3 + g) % 8) + n1_ + 1]
                t_m = t
                t = V(lambda e, neg=neg, n0=n0, n1_=n1_: e.tensor_scalar(neg, stat[:, mcol(n0):mcol(n1_) + 1:4], -SCALE, None, MUL), t,
                      neg_free[(h * 3 + g) % 8])
                p = pool.take()
                for n, o, w, *_ in part:
                    te = A(lambda e, p=p, b=b, n=n, o=o, w=w, neg=neg, n0=n0: e.activation(
                        p.f[:, o:o + w], b.ap[:, o:o + w], ACT.Exp, bias=neg[:, n - n0:n - n0 + 1], scale=SCALE,
                        accum_out=stat[:, DO + g * 16 + n * 4 + h:DO + g * 16 + n * 4 + h + 1]), t, *p.free)
                    probs[n] = (p, o, w, te)
                psum.give(b, te)
                neg_free[(h * 3 + g) % 8] = te
                yield
            st_t[(g, h)] = (t_m, te)
            pool.give(q, tok)
            pool.give(k, tok)
            vb = psum.take()
            for n in range(4):
                tok = P(lambda e, n=n: e.transpose(vb.ap[:, n * 128:(n + 1) * 128], v.f[:, n * 128:(n + 1) * 128], ident[:, :]),
                        tv, vb.free)
            vn = pool.take()
            t_vn = A(lambda e: e.activation(vn.f, vb.ap[:, :], ACT.Copy), tok, *vn.free)
            psum.give(vb, t_vn)
            pool.give(v, tok)
            yield
            return vn, t_vn, probs, parts

        neg_free = [None] * 8

        def values(g, h, sc):
            vn, t_vn, probs, parts = sc
            ob = psum.take()
            pts = []
            for part in parts:
                p = probs[part[0][0]][0]
                b = psum.take()
                width = part[-1][1] + part[-1][2]
                te = probs[part[-1][0]][3]
                for c in range(width // 128):
                    tok = P(lambda e, c=c, b=b, p=p: e.transpose(b.ap[:, c * 128:(c + 1) * 128], p.f[:, c * 128:(c + 1) * 128],
                                                                 ident[:, :]), te, b.free)
                pool.give(p, tok)
                pt = pool.take()
                t = A(lambda e, b=b, pt=pt, width=width: e.activation(pt.f[:, 0:width], b.ap[:, 0:width], ACT.Copy), tok, *pt.free)
                psum.give(b, t)
                pts.append((part, pt, t))
                yield
            for part, pt, t in pts:
                for n, o, w, *_ in part:
                    keys = [n] if w == 128 else [n - 1, n]
                    for x, kb in enumerate(keys):
                        tok = P(lambda e, n=n, o=o, x=x, kb=kb, pt=pt, last=(x == len(keys) - 1), ff=(x == 0): e.matmul(
                            ob.ap[:, n * 128:(n + 1) * 128], vn.f[:, kb * 128:(kb + 1) * 128],
                            pt.f[:, o + x * 128:o + (x + 1) * 128], start=ff, stop=last), t, t_vn, ob.free)
                pool.give(pt, tok)
                if part is not parts[-1]:
                    yield
            pool.give(vn, tok)
            o_ = pool.take()
            d = DIL[g]
            src = ob.ap[:, :] if d == 1 else ob.ap[:, :].rearrange("p (r l) -> p l r", r=d)
            t = A(lambda e: e.activation(nat(o_.f, d), src, ACT.Copy), tok, *o_.free)
            psum.give(ob, t)
            OT[g][h] = (o_, t)

        def head(g, h, got):
            yield from values(g, h, (yield from scores(g, h, got)))

        def sigmoid_of(b, tok):
            s = pool.take()
            t = A(lambda e: e.activation(s.f, b.ap[:, :], ACT.Sigmoid), tok, *s.free)
            psum.give(b, t)
            return s, t

        gates = []

        def gate_tile(j):
            b, tok = yield from gproject("in", 40 + j, n1)
            gates.append(sigmoid_of(b, tok))

        lo_turn["mode"] = "VVG"
        pieces, count = iter(()), 0
        for h in range(4):
            for g in range(3):
                got = beside(qkv(g, h), 24, pieces, count)
                pieces, count = head(g, h, got), (7 if g == 0 else 4)
        beside(gate_tile(0), 8, pieces, count)
        step()
        pool.give(rc1, t_rc1, G.last())
        pool.give(rs1, t_rs1, G.last())

        rows_m, rows_d = [], []
        for kind, base, lst in ((0, MO, rows_m), (1, DO, rows_d)):
            for g in range(3):
                b = psum.take()
                for n in range(4):
                    c0 = base + g * 16 + n * 4
                    tok = P(lambda e, b=b, n=n, c0=c0: e.transpose(b.ap[0:4, n * 128:(n + 1) * 128], stat[:, c0:c0 + 4], ident[:, :]),
                            *[st_t[(g, h)][kind] for h in range(4)], b.free)
                s = pool.take()
                d = DIL[g]
                src = b.ap[0:4, :] if d == 1 else b.ap[0:4, :].rearrange("p (r l) -> p l r", r=d)
                t = A(lambda e, s=s, src=src, d=d: e.activation(nat(s.f[0:4, :], d), src, ACT.Copy), tok, *s.free)
                psum.give(b, t)
                lst.append((s, t))
        for j in (1, 2):
            whole(gate_tile(j))
            step(1)
        mx = pool.take()
        (m0, a0), (m1, a1), (m2, a2) = rows_m
        t = V(lambda e: e.tensor_tensor(mx.f[0:4, :], m0.f[0:4, :], m1.f[0:4, :], MAX), a0, a1, *mx.free)
        t = V(lambda e: e.tensor_tensor(mx.f[0:4, :], mx.f[0:4, :], m2.f[0:4, :], MAX), t, a2)
        te = []
        for s, _ in rows_m:
            x = V(lambda e, s=s: e.tensor_tensor(s.f[0:4, :], s.f[0:4, :], mx.f[0:4, :], SUB), t)
            te.append(A(lambda e, s=s: e.activation(s.f[0:4, :], s.f[0:4, :], ACT.Exp, scale=SCALE), x))
        tz = None
        for g in range(3):
            (e_s, _), (d_s, td) = rows_m[g], rows_d[g]
            x = V(lambda e, e_s=e_s, d_s=d_s: e.tensor_tensor(d_s.f[0:4, :], d_s.f[0:4, :], e_s.f[0:4, :], MUL), te[g], td)
            if g == 0:
                tz = V(lambda e, d_s=d_s: e.tensor_copy(mx.f[0:4, :], d_s.f[0:4, :]), x)
            else:
                tz = V(lambda e, d_s=d_s: e.tensor_tensor(mx.f[0:4, :], mx.f[0:4, :], d_s.f[0:4, :], ADD), x, tz)
            pool.give(d_s, tz)
        tz = V(lambda e: e.reciprocal(mx.f[0:4, :], mx.f[0:4, :]), tz)
        tw = []
        for g in range(3):
            s = rows_m[g][0]
            tw.append(V(lambda e, s=s: e.tensor_tensor(s.f[0:4, :], s.f[0:4, :], mx.f[0:4, :], MUL), tz))
        pool.give(mx, tw[-1])
        whole(gate_tile(3))
        step(1)
        attn = []
        selp = pool.take()
        t_sel = load(selp.f[0:4, :], consts[0:4, 640:1152], *selp.free)
        for h in range(4):
            acc = None
            for g in range(3):
                b = psum.take()
                s = rows_m[g][0]
                tok = P(lambda e, b=b, s=s, h=h: e.matmul(b.ap[:, :], selp.f[0:4, h * 128:(h + 1) * 128], s.f[0:4, :],
                                                          start=True, stop=True), tw[g], t_sel, b.free)
                o_, to = OT[g][h]
                t = V(lambda e, o_=o_, b=b: e.tensor_tensor(o_.f, o_.f, b.ap[:, :], MUL), to, tok)
                psum.give(b, t)
                if acc is None:
                    acc, ta = o_, t
                else:
                    ta = G(lambda e, acc=acc, o_=o_: e.tensor_tensor(acc.f, acc.f, o_.f, ADD), t, ta)
                    pool.give(o_, ta)
            hs, ls, th, tl = split(acc.f, ta)
            pool.give(acc, tl)
            attn.append(operand(hs, ls, th, tl) + (hs, ls))
            whole(gate_tile(4 + h))
            step(1)
        for s, _ in rows_m:
            pool.give(s, tok)
        pool.give(selp, tok)

        def free_ops(ops, tok):
            for x in ops:
                pool.give(x[3], tok)
                pool.give(x[4], tok)

        def three(ops):
            return [x[:3] for x in ops]

        at3 = three(attn)
        for m in range(8):
            b, tok = project("ap", m, at3)
            ga, tga = gates[m]
            t = V(lambda e, ga=ga, b=b: e.tensor_tensor(ga.f, ga.f, b.ap[:, :], MUL), tga, tok)
            psum.give(b, t)
            gates[m] = (ga, t)
            step(1)
        free_ops(attn, P.last())
        for m in range(8):
            whole(gate_tile(8 + m))
            step(1)
        free_ops(n1s, P.last())
        step(80)
        y3 = three(ssm_out)
        merged = []
        for m in range(8):
            (ga, t), (gs, tgs) = gates[m], gates[8 + m]
            sb_, tsb = sigmoid_of(*project("gb", m, y3))
            b, tok = project("ga", m, y3)
            t2 = V(lambda e, sb_=sb_, b=b: e.tensor_tensor(sb_.f, sb_.f, b.ap[:, :], MUL), tsb, tok)
            psum.give(b, t2)
            t2 = G(lambda e, sb_=sb_, gs=gs: e.tensor_tensor(gs.f, gs.f, sb_.f, MUL), t2, tgs)
            pool.give(sb_, t2)
            t = G(lambda e, ga=ga, gs=gs: e.tensor_tensor(ga.f, ga.f, gs.f, ADD), t, t2)
            pool.give(gs, t)
            h, l, th, tl = split(ga.f, t)
            pool.give(ga, tl)
            merged.append(operand(h, l, th, tl) + (h, l))
        free_ops(ssm_out, P.last())
        lo_turn["mode"] = "VG"

        hs_ = []
        for k in range(8):
            s = pool.take()
            hs_.append([s, load(s.f, xT[k], *s.free)])
        mg3 = three(merged)
        nrm = Norm(8)

        def residual(name, ops, nrm=None, k0=0, gate=None):
            late = None
            for m in range(8):
                b, tok = project(name, m, ops, k0)
                s, ts_ = hs_[m]
                if gate is None:
                    t = V(lambda e, s=s, b=b: e.tensor_tensor(s.f, s.f, b.ap[:, :], ADD), tok, ts_)
                else:
                    t = V(lambda e, s=s, b=b, m=m: e.scalar_tensor_tensor(out=s.f, in0=b.ap[:, :], scalar=gate(m), in1=s.f,
                                                                          op0=MUL, op1=ADD), tok, ts_)
                psum.give(b, t)
                hs_[m][1] = t
                if nrm is not None:
                    if late is not None:
                        nrm.add(*late)
                    late = (s.f, t)
            if nrm is not None:
                nrm.add(*late)

        residual("out", mg3, nrm)
        free_ops(merged, P.last())

        pl = []
        for k in range(2):
            s = pool.take()
            t = load(s.f, pT[k], *s.free)
            h, l, th, tl = split(s.f, t)
            pool.give(s, tl)
            pl.append(operand(h, l, th, tl) + (h, l))
        rb, trb = nrm.finish(1024, stat_cols(4))
        ple = []

        def ple_tile(m):
            b, tok = project("pp", m, three(pl))
            s = pool.take()
            t = A(lambda e: e.activation(s.f, b.ap[:, :], ACT.Copy), tok, *s.free)
            psum.give(b, t)
            ple.append((s, t))

        def normed(rb, trb, g, q2=None):
            ops = []
            for k in range(8):
                s, ts_ = hs_[k]
                w = pool.take()
                t = V(lambda e, s=s, w=w, k=k: e.scalar_tensor_tensor(out=w.f, in0=s.f, scalar=g(k), in1=rb.ap[:, :],
                                                                      op0=MUL, op1=MUL), ts_, trb, *w.free)
                h, l, th, tl = split(w.f, t, q=(G if k % 2 else V))
                pool.give(w, th, tl)
                ops.append(operand(h, l, th, tl) + (h, l))
            psum.give(rb, t)
            return ops

        n2 = normed(rb, trb, lambda k: col("g_ffn", k))
        for m in range(8):
            ple_tile(m)
        free_ops(pl, P.last())

        def ada():
            cr = [pool.take() for _ in range(2)]
            tcs = []
            for i, s in enumerate(cr):
                t = load(s.f, cT[:, i * 512:(i + 1) * 512], *s.free)
                tcs.append(A(lambda e, s=s: e.activation(s.f, s.f, ACT.Silu), t))
            part = pool.take()
            for m in range(48):
                ws = [pool.take() for _ in range(2)]
                for i, s in enumerate(ws):
                    t = load(s.f, wadaT[m, :, i * 512:(i + 1) * 512], *s.free)
                    t = V(lambda e, s=s, i=i, m=m: e.tensor_tensor_reduce(
                        s.f, s.f, cr[i].f, 1.0, 0.0, MUL, ADD, part.f[:, 2 * m + i:2 * m + i + 1]), t, tcs[i], *part.free)
                    pool.give(s, t)
                yield
            t = V(lambda e: e.tensor_tensor(mod[:, :], part.f[:, 0:96:2], part.f[:, 1:96:2], ADD), t)
            t = V(lambda e: e.tensor_tensor(mod[:, :], mod[:, :], col("b_ada", 0, 48), ADD), t)
            V(lambda e: e.scalar_tensor_tensor(out=scl[:, 32:40], in0=mod[:, 8:16], scalar=1.0, in1=col("n1", 0, 8),
                                               op0=ADD, op1=MUL), t)
            t = V(lambda e: e.scalar_tensor_tensor(out=scl[:, 40:48], in0=mod[:, 32:40], scalar=1.0, in1=col("n2", 0, 8),
                                                   op0=ADD, op1=MUL))
            t_mod.append(t)
            for s in cr:
                pool.give(s, t)
            pool.give(part, t)

        t_mod = []
        bg = ada()

        def gated(name_g, name_u, m, ops):
            b, tok = project(name_g, m, ops)
            s = pool.take()
            t = A(lambda e: e.activation(s.f, b.ap[:, :], ACT.Silu), tok, *s.free)
            psum.give(b, t)
            b2, tok = project(name_u, m, ops)
            t = V(lambda e: e.tensor_tensor(s.f, s.f, b2.ap[:, :], MUL), tok, t)
            psum.give(b2, t)
            h, l, th, tl = split(s.f, t)
            pool.give(s, tl)
            return operand(h, l, th, tl) + (h, l)

        rc2, rs2, t_rc2, t_rs2 = rope_table(pos2, col("if2"), col("sg2"))
        sp = stat_cols(60)
        spv = [stat[:, sp + 10 * i:sp + 10 * i + 10] for i in range(6)]
        lru = col("lru", 0, 10)
        a_, z_, s_2, u_, acc_, r_ = spv
        t = V(lambda e: e.tensor_scalar(a_, lru, -1.0, None, MUL), t_sm)
        t = V(lambda e: e.tensor_tensor(a_, a_, lru, MIN), t)
        t = A(lambda e: e.activation(z_, a_, ACT.Exp), t)
        t = V(lambda e: e.tensor_scalar(u_, z_, 2.0, None, ADD), t)
        t = V(lambda e: e.reciprocal(u_, u_), t)
        t = V(lambda e: e.tensor_tensor(z_, z_, u_, MUL), t)
        t = V(lambda e: e.tensor_tensor(s_2, z_, z_, MUL), t)
        t = V(lambda e: e.tensor_scalar(acc_, s_2, 1.0 / 17, 1.0 / 15, MUL, ADD), t)
        for n in (13, 11, 9, 7, 5, 3, 1):
            t = V(lambda e: e.tensor_tensor(acc_, acc_, s_2, MUL), t)
            t = V(lambda e, n=n: e.tensor_scalar(acc_, acc_, 1.0 / n, None, ADD), t)
        t = V(lambda e: e.tensor_tensor(acc_, acc_, z_, MUL), t)
        t = V(lambda e: e.tensor_scalar(acc_, acc_, 8.0, None, MUL), t)
        t = V(lambda e: e.tensor_scalar(r_, lru, -4.0, 0.0, MUL, MAX), t)
        t_sp = V(lambda e: e.tensor_tensor(r_, r_, acc_, ADD), t)

        rst = pool.take()
        pi = pool.take()
        tp = load(pi.f.bitcast(I32), pos2[:, :], *pi.free)
        t = V(lambda e: e.tensor_copy(rst.f, pi.f.bitcast(I32)), tp, *rst.free)
        pool.give(pi, t)
        t_rst = V(lambda e: e.tensor_scalar(rst.f, rst.f, 0.0, None, ALU.is_equal), t)

        n23 = three(n2)
        for half in range(2):
            acts = []
            for m in range(11):
                acts.append(gated("fg", "fu", half * 11 + m, n23))
                step(2)
            if half == 1:
                free_ops(n2, P.last())
            residual("fd", three(acts), None, half * 11)
            free_ops(acts, P.last())
            step(8)
        for _ in range(50):
            step()

        h2 = []
        for k in range(8):
            s, t = hs_[k]
            h, l, th, tl = split(s.f, t, q=(G if k % 2 else V))
            h2.append(operand(h, l, th, tl) + (h, l))
        nrm1, nrm2 = Norm(8), Norm(8)
        late = deque()

        def two_sums():
            s, t, m = late.popleft()
            nrm1.add(s.f, t)
            nrm2.add(s.f, t, scale=col("g_final", m))

        t_g = V(lambda e: e.tensor_tensor(scl[:, 48:56], scl[:, 32:40], col("g_final", 0, 8), MUL), t_mod[0])
        h23 = three(h2)
        for mt in range(0, 8, 2):
            two = project2("pg", mt, "pg", mt + 1, h23) if mt == 0 else (project("pg", mt, h23), project("pg", mt + 1, h23))
            for m, (b, tok) in zip((mt, mt + 1), two):
                s_, t = sigmoid_of(b, tok)
                w, tw_ = ple[m]
                t = V(lambda e, s_=s_, w=w: e.tensor_tensor(s_.f, s_.f, w.f, MUL), t, tw_)
                pool.give(w, t)
                s, ts_ = hs_[m]
                t = V(lambda e, s=s, s_=s_: e.tensor_tensor(s.f, s.f, s_.f, ADD), t, ts_, h2[m][2][0], h2[m][2][1])
                pool.give(s_, t)
                hs_[m][1] = t
                late.append((s, t, m))
                if len(late) > 1:
                    two_sums()
        two_sums()
        free_ops(h2, P.last())

        def broadcast(st, t):
            dg = pool.take()
            t = V(lambda e: e.tensor_tensor(dg.f.rearrange("p (j c) -> p j c", j=4),
                                            ident[:, :].unsqueeze(1).to_broadcast([128, 4, 128]),
                                            st.unsqueeze(2).to_broadcast([128, 4, 128]), MUL), t, *dg.free, t_id)
            o = psum.take()
            t = P(lambda e: e.matmul(o.ap[:, :], ones[:, :], dg.f, start=True, stop=True), t, o.free)
            pool.give(dg, t)
            return o, t

        so = stat_cols(16)
        r1, r2, r12, v2 = (stat[:, so + 4 * i:so + 4 * i + 4] for i in range(4))
        half_ = scl[:, 94:95].to_broadcast([128, 4])
        t1 = V(lambda e: e.tensor_scalar(r1, nrm1.b.ap[:, 0:4], 1.0 / 1024, 1e-6, MUL, ADD), nrm1.tok)
        t2 = V(lambda e: e.tensor_scalar(v2, nrm2.b.ap[:, 0:4], 1.0 / 1024, None, MUL), nrm2.tok)
        psum.give(nrm1.b, t1)
        psum.give(nrm2.b, t2)
        t1 = G(lambda e: e.tensor_tensor(r1, r1, half_, ALU.pow), t1, t_half)
        t = G(lambda e: e.tensor_tensor(r2, r1, r1, MUL), t1)
        t = G(lambda e: e.tensor_tensor(r2, r2, v2, MUL), t, t2)
        t = G(lambda e: e.tensor_tensor(r2, r2, scl[:, 95:96].to_broadcast([128, 4]), ADD), t, t_eps)
        t = G(lambda e: e.tensor_tensor(r2, r2, half_, ALU.pow), t)
        t = G(lambda e: e.tensor_tensor(r12, r1, r2, MUL), t)
        rb, trb = broadcast(r12, t)
        rb1, trb1 = broadcast(r1, t1)

        def modulated(rb, trb, so, sh):
            ops = []
            for k in range(8):
                s, ts_ = hs_[k]
                w, h, l = pool.take(), pool.take(), pool.take()
                shift = mod[:, sh + k:sh + k + 1]
                t = V(lambda e, s=s, w=w, k=k: e.scalar_tensor_tensor(out=w.f, in0=s.f, scalar=scl[:, so + k:so + k + 1],
                                                                      in1=rb.ap[:, :], op0=MUL, op1=MUL),
                      ts_, trb, t_mod[0], *w.free)
                th = A(lambda e, w=w, h=h, shift=shift: e.activation(h.r, w.f, ACT.Identity, bias=shift), t, *h.free)
                tl = V(lambda e, w=w, h=h, l=l, shift=shift: e.scalar_tensor_tensor(
                    out=l.r, in0=w.f, scalar=shift, in1=h.r.bitcast(F32), op0=ADD, op1=SUB), th, *l.free)
                pool.give(w, th, tl)
                ops.append(operand(h, l, th, tl) + (h, l))
            psum.give(rb, t)
            return ops

        lo_turn["mode"] = "G"
        nn = modulated(rb, trb, 48, 0)
        nn3 = three(nn)

        gw = []
        for i in range(5):
            s = pool.take()
            gw.append((s, load(s.f, gblk[i], *s.free)))

        def x2_tile(k):
            s, ts_ = hs_[k]
            t = V(lambda e: e.scalar_tensor_tensor(out=s.f, in0=s.f, scalar=col("g_final", k), in1=rb1.ap[:, :],
                                                   op0=MUL, op1=MUL), ts_, trb1, nn[k][2][0])
            keep = load(spare[k], s.f, t)
            pool.give(s, keep)
            hs_[k] = keep
            return t

        def lru_conv(i, b, tok):
            xc = pool.take()
            t = V(lambda e: e.tensor_scalar(xc.f, b.ap[:, :], col("convw", 30 + i), col("convb", i), MUL, ADD), tok, *xc.free)
            for k in (1, 2, 3):
                t = V(lambda e, k=k: e.scalar_tensor_tensor(
                    out=xc.f[:, k:512], in0=b.ap[:, 0:512 - k], scalar=col("convw", (3 - k) * 10 + i), in1=xc.f[:, k:512],
                    op0=MUL, op1=ADD), t)
            psum.give(b, t)
            return i, xc, t

        def lru_work(convs):
            for part in range(2):
                for i in range(5 * part, 5 * part + 5):
                    lru_gate(*convs[i])
                    yield
                for i in range(5 * part, 5 * part + 5):
                    lru_b(i)
                    if i % 5 in (1, 3, 4):
                        yield

        lr_st = {}

        def lru_gate(i, xc, t):
            g_s, tg = gw[i // 2]
            o = (i % 2) * 256
            b1, b2 = psum.take(), psum.take()
            tk1 = P(lambda e: e.matmul(b1.ap[:, :], g_s.f[:, o:o + 128], xc.f, start=True, stop=True), t, tg, b1.free)
            tk2 = P(lambda e: e.matmul(b2.ap[:, :], g_s.f[:, o + 128:o + 256], xc.f, start=True, stop=True), b2.free)
            if i % 2:
                pool.give(g_s, tk2)
            r, x = pool.take(), pool.take()
            t1 = A(lambda e: e.activation(r.f, b1.ap[:, :], ACT.Sigmoid, bias=col("ba", i)), tk1, *r.free)
            psum.give(b1, t1)
            t2 = A(lambda e: e.activation(x.f, b2.ap[:, :], ACT.Sigmoid, bias=col("bx", i)), tk2, *x.free)
            psum.give(b2, t2)
            t1 = A(lambda e: e.activation(r.f, r.f, ACT.Tanh, scale=r_[:, i:i + 1]), t1, t_sp)
            t1 = V(lambda e: e.tensor_tensor(r.f, r.f, rst.f, MAX), t1, t_rst)
            t2 = G(lambda e: e.tensor_tensor(x.f, x.f, xc.f, MUL), t2, tk2)
            t3 = V(lambda e: e.tensor_scalar(xc.f, r.f, 1.0, None, ADD), t1, t2)
            t3 = V(lambda e: e.reciprocal(xc.f, xc.f), t3)
            t2 = V(lambda e: e.scalar_tensor_tensor(out=x.f, in0=x.f, scalar=2.0, in1=xc.f, op0=MUL, op1=MUL), t2, t3)
            t3 = V(lambda e: e.tensor_scalar(xc.f, xc.f, 2.0, -1.0, MUL, ADD), t2)
            lr_st[i] = (r, x, xc, t1, t2, t3)

        def lru_b(i):
            r, x, a, t1, t2, t3 = lr_st[i]
            t1 = A(lambda e: e.activation(r.f, r.f, ACT.Sqrt), t1, t3)
            t = G(lambda e: e.tensor_tensor(x.f, x.f, r.f, MUL), t1, t2)
            t = V(lambda e: e.tensor_tensor_scan(r.f, a.f, x.f, 0.0, MUL, ADD), t, t3)
            pool.give(x, t)
            pool.give(a, t)
            t_lru.append(t)
            h, l, th, tl = split(r.f, t)
            pool.give(r, tl)
            yr.append(operand(h, l, th, tl) + (h, l))

        yr, t_lru = [], []
        convs = []
        two = project2("in2", 0, "in2", 1, nn3)
        convs.append(lru_conv(0, *two[0]))
        convs.append(lru_conv(1, *two[1]))
        bg = lru_work(convs)
        for i in range(2, 10):
            convs.append(lru_conv(i, *project("in2", i, nn3)))
            tx = x2_tile(i - 2)
            if i % 2:
                step()
        psum.give(rb1, tx)

        lat = []
        nq, nk = Norm(3), Norm(2)
        pend = None
        for i in range(5):
            b, tok = project("in2", 10 + i, nn3)
            s = pool.take()
            t = A(lambda e, s=s, b=b: e.activation(s.f, b.ap[:, :], ACT.Copy), tok, *s.free)
            psum.give(b, t)
            (nq if i < 3 else nk).add(s.f, t)
            lat.append((s, t))
            step()
        b, tok = project("in2", 15, nn3)
        kr = pool.take()
        tkr = A(lambda e, b=b: e.activation(kr.f, b.ap[:, :], ACT.Copy), tok, *kr.free)
        tbl2 = (rc2, rs2, t_rc2, t_rs2)
        w1, w2 = pool.take(), pool.take()
        mask = list(range(16, 32)) + list(range(16))
        t1 = V(lambda e, b=b: e.tensor_tensor(w1.f, b.ap[:, :], rc2.f, MUL), tkr, t_rc2, *w1.free)
        t2 = V(lambda e, b=b: e.stream_shuffle(w2.f, b.ap[:, :], mask), *w2.free)
        psum.give(b, t2)
        t2 = G(lambda e: e.tensor_tensor(w2.f, w2.f, rs2.f, MUL), t2, t_rs2)
        tkr = G(lambda e: e.tensor_tensor(kr.f, w1.f, w2.f, ADD), t1, t2, tkr)
        pool.give(w1, tkr)
        pool.give(w2, tkr)

        def latent(nrm, tiles, width, gname):
            rb, trb = nrm.finish(width, stat_cols(4))
            ops = []
            for k, (s, ts_) in enumerate(tiles):
                t = V(lambda e, s=s, k=k: e.scalar_tensor_tensor(out=s.f, in0=s.f, scalar=col(gname, k), in1=rb.ap[:, :],
                                                                 op0=MUL, op1=MUL), ts_, trb)
                h, l, th, tl = split(s.f, t)
                pool.give(s, tl)
                ops.append(operand(h, l, th, tl) + (h, l))
            psum.give(rb, t)
            return ops

        ql = latent(nq, lat[:3], 384, "qg")
        kl = latent(nk, lat[3:], 256, "kg")
        g_rnn, g_mla = [], []
        for m in range(8):
            g_rnn.append(sigmoid_of(*project("in2", 16 + m, nn3)))
            step()

        def fill():
            for m in range(8):
                b, tok = yield from gproject("in2", 24 + m, nn3)
                s = pool.take()
                t = A(lambda e, b=b, s=s: e.activation(s.f, b.ap[:, :], ACT.Copy), tok, *s.free)
                psum.give(b, t)
                g_mla.append((s, t))
            free_ops(nn, P.last())

        vs = {}
        align4()
        for half in range(2):
            bk = [psum.take() for _ in range(4)]
            for k in range(2):
                offs = [block("uv", k, half * 4 + i) for i in range(4)]
                o, wt = offs[0]
                hi, lo, toks = kl[k][:3]
                for j in range(4):
                    b = bk[j]
                    js = slice(j * 128, (j + 1) * 128)
                    rh, rl = whi[:, o:o + 512], wlo[:, o:o + 512]
                    P(lambda e, b=b, js=js, hi=hi, rh=rh, k=k: e.matmul(b.ap[:, :], hi[:, js], rh, start=(k == 0), stop=False),
                      *toks, *wt, b.free)
                    P(lambda e, b=b, js=js, lo=lo, rh=rh: e.matmul(b.ap[:, :], lo[:, js], rh, start=False, stop=False))
                    tok = P(lambda e, b=b, js=js, hi=hi, rl=rl, k=k: e.matmul(b.ap[:, :], hi[:, js], rl, start=False, stop=(k == 1)))
            for j in range(4):
                b, s = bk[j], pool.take()
                q = A if j % 2 else V
                if q is A:
                    t = A(lambda e, b=b, s=s: e.activation(s.f, b.ap[:, :], ACT.Copy), tok, *s.free)
                else:
                    t = V(lambda e, b=b, s=s: e.tensor_copy(s.f, b.ap[:, :]), tok, *s.free)
                psum.give(b, t)
                vs[(j, half)] = (s, t)

        step(30)
        for m in range(8):
            b, tok = project("pr", m, three(yr))
            s, t = g_rnn[m]
            t = V(lambda e, s=s, b=b: e.tensor_tensor(s.f, s.f, b.ap[:, :], MUL), tok, t)
            psum.give(b, t)
            g_rnn[m] = (s, t)
        free_ops(yr, P.last())
        pool.give(rst, t_lru[-1])

        SC2 = 1.0 / math.sqrt(96.0)
        ql3, kl3 = three(ql), three(kl)
        MS, DS = stat_cols(16), stat_cols(16)
        st_free = [None] * 4
        kpair = {}

        def head_qk(h):
            if h % 2 == 0:
                b, tok = yield from gproject("uk", h // 2, kl3)
                for odd in range(2):
                    s = pool.take()
                    rows = slice(64 * odd, 64 * odd + 64)
                    t = A(lambda e, s=s, b=b, rows=rows: e.activation(s.f[rows, :], b.ap[rows, :], ACT.Copy), tok, *s.free)
                    rr = slice(64, 96) if odd == 0 else slice(0, 32)
                    t2 = V(lambda e, s=s, rr=rr: e.tensor_copy(s.f[rr, :], kr.f[rr, :]), tkr, *s.free)
                    t3 = V(lambda e, s=s: e.memset(s.f[32:64, :], 0.0), *s.free) if odd else None
                    kpair[odd] = (s, t, t2, t3)
                psum.give(b, t)
            b, tok = yield from gproject("uq", h, ql3)
            q = pool.take()
            t = A(lambda e: e.activation(q.f, b.ap[:, :], ACT.Copy), tok, *q.free)
            rr = slice(64, 96) if h % 2 == 0 else slice(0, 32)
            t = rope(b, q, rr, tbl2, 1, t)
            return q, t, kpair[h % 2]

        def head_scores(h, qk):
            q, tq, (k, *tks) = qk
            K = slice(0, 96) if h % 2 == 0 else slice(0, 128)
            z = 4 * (h % 4)
            for n in (3, 2, 1, 0):
                b = psum.take()
                w = (n + 1) * 128
                P(lambda e, b=b, n=n, w=w: e.matmul(b.ap[:, 0:w], q.f[K, n * 128:(n + 1) * 128], k.f[K, 0:w],
                                                    start=True, stop=True, skip_group_check=True), tq, *tks, b.free)
                tok = P(lambda e, b=b, n=n, w=w: e.matmul(b.ap[:, n * 128:w], identb[:, :], maskb[:, m_diag:m_diag + 128],
                                                          start=False, stop=True, skip_group_check=True))
                mc, dc = stat[:, MS + z + n:MS + z + n + 1], stat[:, DS + z + n:DS + z + n + 1]
                t = V(lambda e, b=b, w=w, mc=mc: e.tensor_reduce(mc, b.ap[:, 0:w], AX, MAX), tok, st_free[h % 4])
                t = V(lambda e, mc=mc: e.tensor_scalar(mc, mc, -SC2, None, MUL), t)
                p = pool.take()
                te = A(lambda e, p=p, b=b, w=w, mc=mc, dc=dc: e.activation(p.f[:, 0:w], b.ap[:, 0:w], ACT.Exp, bias=mc,
                                                                           scale=SC2, accum_out=dc), t, *p.free, st_free[h % 4])
                psum.give(b, te)
                probs2[h][n] = (p, te)
                if n == 0:
                    pool.give(q, tok)
                    pool.give(k, tok)
                yield

        def head_values(h, ob):
            z = 4 * (h % 4)
            dc = stat[:, DS + z:DS + z + 4]
            res = probs2.pop(h)
            t = V(lambda e: e.reciprocal(dc, dc), *[r[1] for r in res.values()])
            ps = []
            for n in range(4):
                p, te = res[n]
                w = (n + 1) * 128
                tp = V(lambda e, p=p, w=w, n=n: e.tensor_scalar(p.f[:, 0:w], p.f[:, 0:w], dc[:, n:n + 1], None, MUL), t, te)
                ps.append((p, tp))
                st_free[h % 4] = tp
            rows = slice(64 * (h % 2), 64 * (h % 2) + 64)

            def turn(kb):
                b = psum.take()
                for n in range(kb, 4):
                    p, tp = ps[n]
                    tok = P(lambda e, b=b, p=p, n=n, kb=kb: e.transpose(b.ap[:, n * 128:(n + 1) * 128],
                                                                        p.f[:, kb * 128:(kb + 1) * 128], ident[:, :]), tp, b.free)
                if kb == 3:
                    for p, _ in ps:
                        pool.give(p, tok)
                pt = pool.take()
                c0 = kb * 128
                if kb == 1:
                    t = V(lambda e, b=b, pt=pt, c0=c0: e.tensor_copy(pt.f[:, c0:512], b.ap[:, c0:512]), tok, *pt.free)
                else:
                    t = A(lambda e, b=b, pt=pt, c0=c0: e.activation(pt.f[:, c0:512], b.ap[:, c0:512], ACT.Copy), tok, *pt.free)
                psum.give(b, t)
                return pt, t

            def times(kb, pt, t):
                v, tv = vs[(kb, h // 8)]
                vo = (h % 8) * 64
                c0 = kb * 128
                tok = P(lambda e: e.matmul(ob.ap[rows, c0:512], v.f[:, vo:vo + 64], pt.f[:, c0:512], start=(kb == 0), stop=True,
                                           skip_group_check=True), t, tv, ob.free)
                pool.give(pt, tok)
                return tok

            prev = None
            for kb in range(4):
                cur = turn(kb)
                yield
                if prev is not None:
                    times(kb - 1, *prev)
                    yield
                prev = cur
            t_head[h] = times(3, *prev)
            yield

        ym = []
        ob = None
        t_head = {}
        probs2 = {h: {} for h in range(16)}
        filler = fill()

        def side(h):
            n = 0
            if h < 16:
                gen = head_qk(h)
                while True:
                    try:
                        next(gen)
                    except StopIteration as e:
                        qks[h] = e.value
                        break
                    n += 1
                    yield
            for _ in range(NFILL - n):
                next(filler, None)
                yield

        qks = {}
        whole(side(0))
        sc = head_scores(0, qks[0])
        for _ in side(1):
            next(sc, None)
        for _ in sc:
            pass
        for h in range(16):
            if h % 2 == 0:
                ob = psum.take()
            work = side(h + 2)
            val = head_values(h, ob)
            sc = head_scores(h + 1, qks[h + 1]) if h < 15 else iter(())
            for c in "VSVVSVVSVVSV" if h < 15 else "V" * 8:
                next(val if c == "V" else sc, None)
                next(work, None)
            for _ in work:
                pass
            for g_ in (val, sc):
                for _ in g_:
                    raise ValueError("a head's pieces are not done")
            if h % 2:
                h_, l_, th, tl = split(ob.ap[:, :], t_head[h])
                psum.give(ob, tl)
                ym.append(operand(h_, l_, th, tl) + (h_, l_))
        whole(filler)
        free_ops(ql, P.last())
        free_ops(kl, P.last())
        pool.give(kr, G.last())
        pool.give(rc2, V.last())
        pool.give(rs2, G.last())
        for s, _ in vs.values():
            pool.give(s, P.last())

        for k in range(8):
            s = pool.take()
            hs_[k] = [s, load(s.f, spare[k], hs_[k], *s.free)]
        merged = []
        for m in range(8):
            b, tok = project("pm", m, three(ym))
            s, t = g_mla[m]
            t = A(lambda e, s=s: e.activation(s.f, s.f, ACT.Sigmoid), t)
            t = V(lambda e, s=s, b=b: e.tensor_tensor(s.f, s.f, b.ap[:, :], MUL), tok, t)
            psum.give(b, t)
            w, tw_ = g_rnn[m]
            t = G(lambda e, s=s, w=w: e.tensor_tensor(s.f, s.f, w.f, ADD), t, tw_)
            pool.give(w, t)
            h, l, th, tl = split(s.f, t)
            pool.give(s, tl)
            merged.append(operand(h, l, th, tl) + (h, l))
        free_ops(ym, P.last())
        nrm = Norm(8)
        residual("out2", three(merged), nrm, gate=lambda m: mod[:, 16 + m:17 + m])
        free_ops(merged, P.last())
        rb, trb = nrm.finish(1024, stat_cols(4))
        lo_turn["mode"] = "G"
        nn = modulated(rb, trb, 40, 24)
        nn3 = three(nn)

        def conv(mt):
            b, tok = project("up", mt, nn3)
            s = pool.take()
            t = A(lambda e: e.activation(s.f, b.ap[:, :], ACT.Identity, bias=col("fcb", mt), scale=col("fcw", 88 + mt)), tok, *s.free)
            for k in (1, 2):
                t = V(lambda e, k=k: e.scalar_tensor_tensor(out=s.f[:, k:512], in0=b.ap[:, 0:512 - k],
                                                            scalar=col("fcw", (2 - k) * 44 + mt), in1=s.f[:, k:512],
                                                            op0=MUL, op1=ADD), t)
            psum.give(b, t)
            return s, t

        nrm = Norm(8)
        for half in range(2):
            acts = []
            for m in range(11):
                mt = half * 11 + m
                g_, tg = conv(mt)
                tg = A(lambda e, g_=g_: e.activation(g_.f, g_.f, ACT.Silu), tg)
                u_s, tu = conv(22 + mt)
                t = G(lambda e, g_=g_, u_s=u_s: e.tensor_tensor(g_.f, g_.f, u_s.f, MUL), tg, tu)
                pool.give(u_s, t)
                h, l, th, tl = split(g_.f, t)
                pool.give(g_, tl)
                acts.append(operand(h, l, th, tl) + (h, l))
            if half == 1:
                free_ops(nn, P.last())
            residual("dn", three(acts), nrm if half else None, half * 11, gate=lambda m: mod[:, 40 + m:41 + m])
            free_ops(acts, P.last())

        rb, trb = nrm.finish(1024, stat_cols(4))
        ends = []
        for k in range(8):
            s, ts_ = hs_[k]
            t = V(lambda e, s=s, k=k, rb=rb: e.scalar_tensor_tensor(out=s.f, in0=s.f, scalar=col("gf2", k), in1=rb.ap[:, :],
                                                             op0=MUL, op1=MUL), ts_, trb)
            ends.append(load(out[k], s.f, t))

        for q in (P, A, V, G, S):
            q.count()
        if (len(blocks) + CB - 1) // CB != NCHUNK:
            raise ValueError(f"NCHUNK should be {(len(blocks) + CB - 1) // CB}")
        with nc.Block() as block_:
            @block_.sync
            def _(e):
                S.emit(e)
                for s, n in ends:
                    e.wait_ge(s, n)

            @block_.tensor
            def _(e):
                P.emit(e)

            @block_.scalar
            def _(e):
                A.emit(e)

            @block_.vector
            def _(e):
                V.emit(e)

            @block_.gpsimd
            def _(e):
                G.emit(e)
    return nc


def columns(v, n):
    return np.asarray(v).reshape(n, 128).T


def lay_out(x):
    f = np.float32
    rs = np.concatenate
    invf1 = (np.float32(500000.0) ** (-np.arange(16, dtype=f) * f(2.0) / f(32))).astype(f)
    invf2 = (np.float32(10000.0) ** (-np.arange(16, dtype=f) / f(16))).astype(f)
    parts = dict(
        g_mix=columns(x["g_mix"], 8), g_ffn=columns(x["g_ffn"], 8), g_final=columns(x["g_final"], 8),
        n1=columns(x["norm1_g_2"], 8), n2=columns(x["norm2_g_2"], 8), gf2=columns(x["final_g_2"], 8),
        b_ada=columns(x["b_ada_2"], 48),
        convw=rs([columns(x["conv_w_2"][0, k], 10) for k in range(4)], axis=1), convb=columns(x["conv_b_2"], 10),
        ba=columns(x["b_gate_a_2"], 10), bx=columns(x["b_gate_x_2"], 10), lru=columns(x["lru_param_2"], 10),
        qg=columns(x["q_norm_g_2"], 3), kg=columns(x["kv_norm_g_2"], 2),
        fcw=rs([columns(x["ffn_conv_w_2"][0, k], 44) for k in range(3)], axis=1), fcb=columns(x["ffn_conv_b_2"], 44),
        dskip=columns(x["d_skip"], 4), are=columns(x["a_re"], 16), aim=columns(x["a_im"], 16),
        ldt=columns(np.repeat(x["log_dt"][0], 64), 16),
        if1=np.tile(invf1, 8)[:, None], sg1=np.tile(rs([-np.ones(16, f), np.ones(16, f)]), 4)[:, None],
        if2=np.tile(invf2, 8)[:, None], sg2=np.tile(rs([-np.ones(16, f), np.ones(16, f)]), 4)[:, None])
    small = np.empty((128, NSMALL), f)
    for n, w in SMALL:
        small[:, SOFF[n]:SOFF[n] + w] = parts[n]
    q, k = np.arange(128)[:, None], np.arange(128)[None, :]
    neg = f(-1e30)
    consts = np.zeros((128, 1152), f)
    consts[:, 0:128] = np.eye(128, dtype=f)
    consts[:, 128:256] = np.where(k >= q, f(0), neg)
    consts[:, 256:384] = np.where(k <= q, f(0), neg)
    consts[:, 384:512] = np.where((k <= q) & (k // 32 == q // 32), f(0), neg)
    consts[:, 512:640] = 1
    for h in range(4):
        consts[h, 640 + h * 128:640 + (h + 1) * 128] = 1
    bc = np.empty((128, 2, 16, 16), f)
    cp = np.zeros((2, 4, 128, 4, 128), f)
    for c, (bn, cn) in enumerate((("b_re", "c_re"), ("b_im", "c_im"))):
        for g in range(32):
            i, half = g // 2, g % 2
            bc[64 * half:64 * half + 64, c, i, :] = x[bn][0, g]
            o = (g % 8) * 16
            cp[c, i // 4, 64 * half:64 * half + 64, i % 4, o:o + 16] = np.asarray(x[cn][0, g]).T
    gb = np.zeros((5, 128, 2, 2, 128), f)
    for i in range(10):
        for c, n in enumerate(("w_gate_a_2", "w_gate_x_2")):
            for s in range(2):
                gb[i // 2, 64 * s:64 * s + 64, i % 2, c, 64 * s:64 * s + 64] = x[n][0, 2 * i + s]
    c_ = np.ascontiguousarray
    return dict(
        xT=c_(x["x"][0].T).reshape(8, 128, T), pT=c_(x["p"][0, 0].T).reshape(2, 128, T), small=small, consts=consts,
        pos1=c_(np.broadcast_to(x["positions"], (128, T))), pos2=c_(np.broadcast_to(x["positions_2"], (128, T))),
        cT=c_(np.broadcast_to(x["c_2"], (128, 1024))), wadaT=c_(x["w_ada_2"][0].T).reshape(48, 128, 1024),
        bcmp=bc.reshape(128, 512), cpad=cp.reshape(2, 4, 128, 512), gblk=gb.reshape(5, 128, 512))


def stream(x, blocks):
    f = np.float32
    w2 = x["w_in_2"][0]
    z = lambda r, c: np.zeros((r, c), f)
    kr = w2[:, 1920:1952]
    in2 = np.concatenate([w2[:, :1920], kr, z(1024, 32), kr, z(1024, 32), w2[:, 1952:]], axis=1)
    uq = x["w_uq_2"][0].reshape(384, 16, 96)
    uqp = np.zeros((384, 16, 128), f)
    uqp[:, 0::2, 0:96] = uq[:, 0::2]
    uqp[:, 1::2, 0:32] = uq[:, 1::2, 64:96]
    uqp[:, 1::2, 64:128] = uq[:, 1::2, 0:64]
    ukv = x["w_ukv_2"][0].reshape(256, 16, 128)
    ws = {"in": x["w_in"][0], "ap": x["w_attn_proj"][0], "ga": x["w_glu_a"][0], "gb": x["w_glu_b"][0],
          "out": x["w_out"][0], "fg": x["w_ffn_gate"][0], "fu": x["w_ffn_up"][0], "fd": x["w_ffn_down"][0],
          "pg": x["w_ple_gate"][0], "pp": x["w_ple_proj"][0], "in2": in2, "uq": uqp.reshape(384, 2048),
          "uk": ukv[:, :, :64].reshape(256, 1024), "uv": ukv[:, :, 64:].reshape(256, 1024),
          "pr": x["w_proj_rnn_2"][0], "pm": x["w_proj_mla_2"][0], "out2": x["w_out_2"][0],
          "up": x["w_up_2"][0], "dn": x["w_down_2"][0], "zero": z(128, 128)}
    out = np.zeros((NCHUNK, 128, CB * 128), f)
    for n, (name, k, m) in enumerate(blocks):
        out[n // CB, :, (n % CB) * 128:(n % CB + 1) * 128] = ws[name][k * 128:(k + 1) * 128, m * 128:(m + 1) * 128]
    return out


def kernel(**inputs):
    import concourse.bacc as bacc
    from concourse.bass_utils import run_bass_kernel_spmd

    x = {n: np.asarray(a) for n, a in inputs.items()}
    nc = bacc.Bacc("TRN2", target_bir_lowering=False, num_devices=1)
    arrays = lay_out(x)
    args = {n: nc.dram_tensor(n, a.shape, mybir.dt.from_np(a.dtype), kind="ExternalInput").ap() for n, a in arrays.items()}
    wst = nc.dram_tensor("wst", (NCHUNK, 128, CB * 128), F32, kind="ExternalInput").ap()
    out = nc.dram_tensor("out", (8, 128, T), F32, kind="ExternalOutput").ap()
    spare = nc.dram_tensor("spare", (8, 128, T), F32, kind="Internal").ap()
    blocks = []
    program(nc, blocks, wst, spare=spare, out=out, **args)
    arrays["wst"] = stream(x, blocks)
    r = run_bass_kernel_spmd(nc, [arrays], core_ids=[0])
    got = r.results[0]["out"]
    return np.ascontiguousarray(np.asarray(got).reshape(1024, T).T).reshape(1, T, 1024)
```

```python
import math
from collections import deque
from contextlib import ExitStack

import numpy as np

import concourse.bass as bass
from concourse import mybir

F32 = mybir.dt.float32
F32R = mybir.dt.float32r
BF16 = mybir.dt.bfloat16
I32 = mybir.dt.int32
ALU = mybir.AluOpType
ACT = mybir.ActivationFunctionType
AX = mybir.AxisListType.X
ADD, SUB, MUL, MAX, MIN = ALU.add, ALU.subtract, ALU.mult, ALU.max, ALU.min

T = 512
CB = 8
NRAW, NHL = 4, 3
NSLOT = 78
NCHUNK = 286
STEPS = [2, 2, 1] * 3 + [1] * 27
LATE = 1
NFILL = 8
ORDER = "FVSSVFVSFSFVVFFVFVVF"
LAST_HEAD = "VFFVFFVFFVFFVFFVFVFVF"
HALF_PI = math.pi / 2
PI_IN = 3.1415925
MAGIC = 12582912.0
TWO_PI_1 = 6.28125
TWO_PI_2 = 0.0019350051879882812
TWO_PI_3 = 3.0199159819e-07

SMALL = [("g_mix", 8), ("g_ffn", 8), ("g_final", 8), ("n1", 8), ("n2", 8), ("gf2", 8), ("b_ada", 48),
         ("convw", 40), ("convb", 10), ("ba", 10), ("bx", 10), ("lru", 10), ("qg", 3), ("kg", 2),
         ("fcw", 132), ("fcb", 44), ("dskip", 4), ("are", 16), ("aim", 16), ("ldt", 16),
         ("if1", 1), ("sg1", 1), ("if2", 1), ("sg2", 1)]
SOFF = {}
_o = 0
for _n, _w in SMALL:
    SOFF[_n] = _o
    _o += _w
NSMALL = _o


class Token:

    def __init__(self, queue, index):
        self.queue, self.index = queue, index


class Queue:

    def __init__(self, sem):
        self.sem, self.ops, self.signals = sem, [], []

    def __call__(self, fn, *after):
        after = [t for t in after if t is not None]
        for t in after:
            if isinstance(t, Token):
                t.queue.signals[t.index] = True
        self.ops.append((fn, after))
        self.signals.append(False)
        return Token(self, len(self.ops) - 1)

    def last(self):
        return Token(self, len(self.ops) - 1)

    def value(self, index):
        return self.counts[index]

    def count(self):
        n, self.counts = 0, []
        for s in self.signals:
            n += s
            self.counts.append(n)

    def emit(self, eng):
        seen = {}
        for (fn, after), signal in zip(self.ops, self.signals):
            need = {}
            for t in after:
                sem, val = (t.queue.sem, t.queue.value(t.index)) if isinstance(t, Token) else t
                key = id(sem)
                if key not in need or need[key][1] < val:
                    need[key] = (sem, val)
            for key, (sem, val) in need.items():
                if seen.get(key, 0) < val:
                    eng.wait_ge(sem, val)
                    seen[key] = val
            ins = fn(eng)
            if signal:
                ins.then_inc(self.sem, 1)


class Bank:
    def __init__(self, ap):
        self.ap, self.free = ap, None


class Slot:
    def __init__(self, f, r):
        self.f, self.r, self.free = f, r, []


class Pool:

    def __init__(self, places):
        self.q = deque(places)
        self.least = len(places)

    def take(self):
        p = self.q.popleft()
        self.least = min(self.least, len(self.q))
        return p

    def give(self, p, *tokens):
        p.free = list(tokens)
        self.q.append(p)


def program(nc, blocks, wst, xT, pT, small, consts, pos1, pos2, cT, wadaT, bcmp, cpad, gblk, spare, out):
    ctx = ExitStack()
    with ctx:
        def sb(name, shape, dt=F32):
            return ctx.enter_context(nc.sbuf_tensor(name, shape, dt))

        def sem(name):
            return ctx.enter_context(nc.semaphore(name))

        raw = sb("raw", [128, NRAW * CB * 128])
        whi = sb("whi", [128, NHL * CB * 128], F32R)
        wlo = sb("wlo", [128, NHL * CB * 128], F32R)
        sm = sb("sm", [128, NSMALL])
        ident = sb("ident", [128, 128])
        ones = sb("ones", [128, 128])
        maskb = sb("maskb", [128, 3 * 128], BF16)
        identb = sb("identb", [128, 128], BF16)
        mod = sb("mod", [128, 48])
        scl = sb("scl", [128, 96])
        stat = sb("stat", [128, 320])
        places = []
        for i in range(NSLOT):
            with nc.sbuf_tensor(f"slotf{i}", [128, T], F32) as slotf:
                pass
            places.append(Slot(slotf[:, :], sb(f"slotr{i}", [128, T], F32R)[:, :]))
        banks = [ctx.enter_context(nc.psum_tensor(f"bank{i}", [128, 512], F32)) for i in range(8)]

        P = Queue(sem("s_pe"))
        A = Queue(sem("s_act"))
        V = Queue(sem("s_dve"))
        G = Queue(sem("s_pool"))
        S = Queue(sem("s_sp"))

        psum = Pool([Bank(b) for b in banks])
        pool = Pool(places)

        dma_sems = [sem(f"s_d{i}") for i in range(24)]
        dma_count = [0] * 24
        dma_turn = [0]

        def load(dst, src, *after):
            i = dma_turn[0] % 24
            dma_turn[0] += 1
            prev = (dma_sems[i], dma_count[i]) if dma_count[i] else None
            dma_count[i] += 16
            s, n = dma_sems[i], dma_count[i]
            S(lambda e: e.dma_start(dst, src).then_inc(s, 16), prev, *after)
            return (s, n)

        def col(name, i=0, n=1):
            return sm[:, SOFF[name] + i:SOFF[name] + i + n]

        W = CB * 128
        s_w = [sem(f"s_w{i}") for i in range(NRAW)]
        raw_free = [None] * NRAW
        hl_free = [None] * NHL
        chunk_tok = {}
        lo_turn = {"mode": "VG"}
        
        def chunk_dma(c):
            if c >= NCHUNK:
                return
            i = c % NRAW
            s = s_w[i]
            S(lambda e: e.dma_start(raw[:, i * W:(i + 1) * W], wst[c]).then_inc(s, 16), raw_free[i])

        def chunk_prep(c):
            if c >= NCHUNK:
                return
            i, j = c % NRAW, c % NHL
            r, h, l = raw[:, i * W:(i + 1) * W], whi[:, j * W:(j + 1) * W], wlo[:, j * W:(j + 1) * W]
            th = A(lambda e: e.activation(h, r, ACT.Copy), (s_w[i], 16 * (c // NRAW + 1)), hl_free[j])
            m = lo_turn["mode"]
            q = V if m[c % len(m)] == "V" else G
            tl = q(lambda e: e.tensor_tensor(l, r, h.bitcast(F32), SUB), th, hl_free[j])
            raw_free[i] = tl
            chunk_tok[c] = (th, tl)


        def block(name, kt, mt):
            n = len(blocks)
            blocks.append((name, kt, mt))
            c = n // CB
            if n % CB == 0:
                if c > 0:
                    hl_free[(c - 1) % NHL] = P.last()
                chunk_prep(c + 2)
                chunk_dma(c + NRAW - 1) if c > 0 else None
            o = (c % NHL) * W + (n % CB) * 128
            return o, chunk_tok[c]

        def align4():
            while len(blocks) % 4:
                block("zero", 0, 0)

        def mm(bank, o, rhs_hi, rhs_lo, first, last, *after, cols=512, width=128):
            wh, wl = whi[:, o:o + width], wlo[:, o:o + width]
            P(lambda e: e.matmul(bank, wh, rhs_hi, start=first, stop=False), *after)
            P(lambda e: e.matmul(bank, wh, rhs_lo, start=False, stop=False))
            return P(lambda e: e.matmul(bank, wl, rhs_hi, start=False, stop=last))

        def project(name, mt, xs, k0=0):
            return whole(gproject(name, mt, xs, k0))

        def whole(gen):
            while True:
                try:
                    next(gen)
                except StopIteration as e:
                    return e.value

        def gproject(name, mt, xs, k0=0):
            b = psum.take()
            n = len(xs)
            for k, (hi, lo, toks) in enumerate(xs):
                o, wt = block(name, k0 + k, mt)
                tok = mm(b.ap[:, :], o, hi, lo, k == 0, k == n - 1, *toks, *wt, *([b.free] if k == 0 else []))
                yield
            return b, tok

        def beside(gen, blocks_, pieces, count):
            n = done = 0
            while True:
                try:
                    next(gen)
                except StopIteration as e:
                    for _ in pieces:
                        pass
                    return e.value
                n += 1
                while done < count and done * blocks_ < n * count:
                    done += 1
                    next(pieces, None)

        def project2(name, m0, name1, m1, xs, k0=0):
            return whole(gproject2(name, m0, name1, m1, xs, len(xs), k0))

        def gproject2(name, m0, name1, m1, xs, n, k0=0):
            b0, b1 = psum.take(), psum.take()
            for k in range(n):
                for b, nm, m in ((b0, name, m0), (b1, name1, m1)):
                    hi, lo, toks = xs[k][:3]
                    o, wt = block(nm, k0 + k, m)
                    tok = mm(b.ap[:, :], o, hi, lo, k == 0, k == n - 1, *toks, *wt, *([b.free] if k == 0 else []))
                    if b is b0:
                        tok0 = tok
                    yield
            return (b0, tok0), (b1, tok)

        def split(src, *after, q=None, hi_scale=None):
            h, l = pool.take(), pool.take()
            q = q or V
            th = A(lambda e: e.activation(h.r, src, ACT.Copy), *h.free, *after)
            tl = q(lambda e: e.tensor_tensor(l.r, src, h.r.bitcast(F32), SUB), th, *l.free)
            return h, l, th, tl

        def operand(h, l, th, tl):
            return (h.r, l.r, (th, tl))

        t_o = V(lambda e: e.memset(ones[:, :], 1.0))
        t_half = V(lambda e: e.memset(scl[:, 94:95], -0.5))
        xs = []
        for k in range(8):
            s = pool.take()
            xs.append((s, load(s.f, xT[k], *s.free)))
        t_id = load(ident[:, :], consts[:, 0:128])
        chunk_dma(0)
        t_sm = load(sm[:, :], small[:, :])
        chunk_dma(1)
        cst = pool.take()
        t_c = load(cst.f[:, 0:512], consts[:, 0:512])
        m_prev, m_diag, m_blk = 0, 128, 256

        def sincos(src, dst_s, dst_c, tmp, q, *after):
            t = q(lambda e: e.tensor_scalar(tmp, src, 1.0 / (2 * math.pi), MAGIC, MUL, ADD), *after)
            t = q(lambda e: e.tensor_scalar(tmp, tmp, MAGIC, None, SUB), t)
            for c in (TWO_PI_1, TWO_PI_2, TWO_PI_3):
                t = V(lambda e, c=c: e.scalar_tensor_tensor(out=src, in0=tmp, scalar=-c, in1=src, op0=MUL, op1=ADD), t)
            t1 = q(lambda e: e.tensor_scalar(src, src, PI_IN, -PI_IN, MIN, MAX), t)
            ts = A(lambda e: e.activation(dst_s, src, ACT.Sin), t1)
            t = q(lambda e: e.tensor_scalar(tmp, src, HALF_PI, 2 * math.pi, ALU.is_gt, MUL), t1)
            t = V(lambda e: e.scalar_tensor_tensor(out=tmp, in0=src, scalar=HALF_PI, in1=tmp, op0=ADD, op1=SUB), t)
            t = q(lambda e: e.tensor_scalar(tmp, tmp, PI_IN, -PI_IN, MIN, MAX), t)
            tc = A(lambda e: e.activation(dst_c, tmp, ACT.Sin), t)
            return ts, tc

        def rope_table(pos, invf, sign):
            return whole(rope_steps(pos, invf, sign))

        def rope_steps(pos, invf, sign):
            pi, c, s, tmp = pool.take(), pool.take(), pool.take(), pool.take()
            tp = load(pi.f.bitcast(I32), pos[:, :], *pi.free)
            yield
            t = V(lambda e: e.tensor_copy(s.f, pi.f.bitcast(I32)), tp, *s.free)
            t = V(lambda e: e.tensor_scalar(pi.f, s.f, invf, None, MUL), t, t_sm)
            ts, tc = sincos(pi.f, s.f, c.f, tmp.f, V, t, *c.free, *tmp.free)
            yield
            t = V(lambda e: e.tensor_scalar(s.f, s.f, sign, None, MUL), ts)
            pool.give(pi, ts, tc)
            pool.give(tmp, tc)
            return c, s, tc, t

        class Norm:

            def __init__(self):
                self.acc = None

            def add(self, src, *after, scale=1.0):
                sq = pool.take()
                t = A(lambda e: e.activation(sq.f, src, ACT.Square, scale=scale), *sq.free, *after)
                if self.acc is None:
                    self.acc, self.tok = sq, t
                else:
                    acc = self.acc
                    self.tok = V(lambda e: e.tensor_tensor(acc.f, acc.f, sq.f, ADD), t, self.tok)
                    pool.give(sq, self.tok)

            def total(self):
                b, acc = psum.take(), self.acc
                for j in range(4):
                    tok = P(lambda e, j=j: e.matmul(b.ap[:, j:j + 1], acc.f[:, j * 128:(j + 1) * 128], ones[:, 0:1],
                                                    start=True, stop=True, skip_group_check=True), self.tok, t_o, b.free)
                pool.give(acc, tok)
                return b, tok

            def rstd(self, width, so):
                b, tok = self.total()
                st = stat[:, so:so + 4]
                t = V(lambda e: e.tensor_scalar(st, b.ap[:, 0:4], 1.0 / width, 1e-6, MUL, ADD), tok)
                psum.give(b, t)
                t = G(lambda e: e.tensor_tensor(st, st, scl[:, 94:95].to_broadcast([128, 4]), ALU.pow), t, t_half)
                return diagonal(st, t)

            def finish(self, width, so):
                return broadcast(*self.rstd(width, so))

        def diagonal(st, t):
            dg = pool.take()
            t = V(lambda e: e.tensor_tensor(dg.f.rearrange("p (j c) -> p j c", j=4),
                                            ident[:, :].unsqueeze(1).to_broadcast([128, 4, 128]),
                                            st.unsqueeze(2).to_broadcast([128, 4, 128]), MUL), t, *dg.free, t_id)
            return dg, t

        def broadcast(dg, t):
            o = psum.take()
            t = P(lambda e: e.matmul(o.ap[:, :], ones[:, :], dg.f, start=True, stop=True), t, o.free)
            pool.give(dg, t)
            return o, t

        def bank_give(b, tok):
            psum.q.append(b)
            b.free = tok

        psum.give = bank_give

        so_next = [0]

        def stat_cols(n):
            o = so_next[0]
            so_next[0] = o + n
            if o + n > 320:
                raise ValueError("stat")
            return o

        for c in range(2, NRAW):
            chunk_dma(c)
        nrm = Norm()
        for s, t in xs:
            nrm.add(s.f, t)
        dg = nrm.rstd(1024, stat_cols(4))
        chunk_prep(0)
        rb, trb = broadcast(*dg)
        def scaled(ops_in, g, rb, trb):
            ops, late = [], None

            def low(w, h, l, th, q):
                tl = q(lambda e: e.tensor_tensor(l.r, w.f, h.r.bitcast(F32), SUB), th, *l.free)
                pool.give(w, th, tl)
                ops.append(operand(h, l, th, tl) + (h, l))

            for k, (s, ts_) in enumerate(ops_in):
                w, h, l = pool.take(), pool.take(), pool.take()
                t = V(lambda e, s=s, w=w, k=k: e.scalar_tensor_tensor(out=w.f, in0=s.f, scalar=g(k), in1=rb.ap[:, :],
                                                                      op0=MUL, op1=MUL), ts_, trb, t_sm, *w.free)
                th = A(lambda e, w=w, h=h: e.activation(h.r, w.f, ACT.Copy), t, *h.free)
                if late:
                    low(*late)
                late = (w, h, l, th, G if k % 2 else V)
                yield k, t, ops
            low(*late)
            psum.give(rb, t)

        for k, t, n1 in scaled(xs, lambda k: col("g_mix", k), rb, trb):
            pool.give(xs[k][0], t)
            if k == 3:
                chunk_prep(1)
        t_idb = V(lambda e: e.tensor_copy(identb[:, :], cst.f[:, 0:128]), t_c)
        t_mb = V(lambda e: e.tensor_copy(maskb[:, :], cst.f[:, 128:512]), t_c)
        pool.give(cst, t_mb)
        n1s = n1
        n1 = [x[:3] for x in n1]

        def ssm():
            ys = []
            us = []
            two = project2("in", 36, "in", 37, n1)
            for j in range(4):
                b, tok = two[j] if j < 2 else project("in", 36 + j, n1)
                u = pool.take()
                t = A(lambda e, b=b, u=u: e.activation(u.f, b.ap[:, :], ACT.Copy), tok, *u.free)
                psum.give(b, t)
                us.append((u, t))
                yield
            pp = pool.take()
            pv = [pp.f[:, 16 * i:16 * i + 16] for i in range(32)]
            (dt, x_, e_, ang, tmp, sn, cs, mag, bre, bim, nr, den, zre, zim, u1, u2) = pv[:16]
            t_dt = A(lambda e: e.activation(dt, col("ldt", 0, 16), ACT.Exp), t_sm, *pp.free)
            t = V(lambda e: e.tensor_tensor(x_, col("are", 0, 16), dt, MUL), t_dt)
            t = V(lambda e: e.tensor_scalar(x_, x_, 1.0 / 256, None, MUL), t)
            t = V(lambda e: e.tensor_scalar(e_, x_, 1.0 / 720, 1.0 / 120, MUL, ADD), t)
            for c in (1.0 / 24, 1.0 / 6, 0.5, 1.0):
                t = V(lambda e: e.tensor_tensor(e_, e_, x_, MUL), t)
                t = V(lambda e, c=c: e.tensor_scalar(e_, e_, c, None, ADD), t)
            t = V(lambda e: e.tensor_tensor(e_, e_, x_, MUL), t)
            for _ in range(8):
                t = V(lambda e: e.scalar_tensor_tensor(out=e_, in0=e_, scalar=2.0, in1=e_, op0=ADD, op1=MUL), t)
            t_mag = V(lambda e: e.tensor_scalar(mag, e_, 1.0, None, ADD), t)
            yield
            t = V(lambda e: e.tensor_tensor(ang, col("aim", 0, 16), dt, MUL), t_dt)
            ts, tc = sincos(ang, sn, cs, tmp, V, t)
            yield
            t1 = V(lambda e: e.tensor_tensor(bre, mag, cs, MUL), tc, t_mag)
            t2 = V(lambda e: e.tensor_tensor(bim, mag, sn, MUL), ts)
            t = V(lambda e: e.tensor_scalar(nr, bre, 1.0, None, SUB), t1)
            t3 = V(lambda e: e.tensor_tensor(den, col("are", 0, 16), col("are", 0, 16), MUL))
            t4 = V(lambda e: e.tensor_tensor(u1, col("aim", 0, 16), col("aim", 0, 16), MUL))
            t3 = V(lambda e: e.tensor_tensor(den, den, u1, ADD), t3, t4)
            t3 = V(lambda e: e.reciprocal(den, den), t3)
            t = V(lambda e: e.tensor_tensor(zre, nr, col("are", 0, 16), MUL), t)
            t2 = V(lambda e: e.tensor_tensor(u1, bim, col("aim", 0, 16), MUL), t2, t3)
            t = V(lambda e: e.tensor_tensor(zre, zre, u1, ADD), t, t2)
            t_zr = V(lambda e: e.tensor_tensor(zre, zre, den, MUL), t, t3)
            t = V(lambda e: e.tensor_tensor(zim, bim, col("are", 0, 16), MUL), t2)
            t2 = V(lambda e: e.tensor_tensor(u2, nr, col("aim", 0, 16), MUL), t)
            t = V(lambda e: e.tensor_tensor(zim, zim, u2, SUB), t2)
            t_zi = V(lambda e: e.tensor_tensor(zim, zim, den, MUL), t, t3)
            yield

            bs = pool.take()
            tb = load(bs.f[:, :], bcmp[:, :], *bs.free)
            b_re, b_im = (bs.f[:, 256 * i:256 * i + 256].rearrange("p (i c) -> p i c", i=16) for i in range(2))
            bq, bw = pool.take(), pool.take()
            q_re, q_im = (bq.f[:, 256 * i:256 * i + 256].rearrange("p (i c) -> p i c", i=16) for i in range(2))
            w_re, w_im = (bw.f[:, 256 * i:256 * i + 256].rearrange("p (i c) -> p i c", i=16) for i in range(2))
            zr_b = zre.unsqueeze(2).to_broadcast([128, 16, 16])
            zi_b = zim.unsqueeze(2).to_broadcast([128, 16, 16])
            t1 = V(lambda e: e.tensor_tensor(q_re, b_re, zr_b, MUL), tb, t_zr, *bq.free)
            t2 = V(lambda e: e.tensor_tensor(w_re, b_im, zi_b, MUL), t_zi, *bw.free)
            t3 = V(lambda e: e.tensor_tensor(q_im, b_im, zr_b, MUL))
            t4 = V(lambda e: e.tensor_tensor(w_im, b_re, zi_b, MUL))
            yield
            bpad = [pool.take() for _ in range(8)]
            bt = []
            for c, (qq, ww, op) in enumerate(((q_re, w_re, SUB), (q_im, w_im, ADD))):
                for j in range(4):
                    d = bpad[4 * c + j]
                    tz = G(lambda e, d=d: e.memset(d.f, 0.0), *d.free)
                    for half in range(2):
                        rows = slice(64 * half, 64 * half + 64)
                        for k in range(4):
                            o = k * 160 + half * 16
                            t = V(lambda e, d=d, rows=rows, o=o, j=j, k=k, qq=qq, ww=ww, op=op: e.tensor_tensor(
                                d.f[rows, o:o + 16], qq[rows, 4 * j + k, :], ww[rows, 4 * j + k, :], op), tz, t1, t2, t3, t4)
                    bt.append(t)
                    if j % 2:
                        yield
            pool.give(bs, t4)
            pool.give(bq, bt[-1])
            pool.give(bw, bt[-1])

            el_r, el_i, eh = pool.take(), pool.take(), pool.take()
            lr, li = (s.f.rearrange("p (i t) -> p i t", i=16) for s in (el_r, el_i))
            hr, hi_ = (eh.f[:, 256 * i:256 * i + 256].rearrange("p (i t) -> p i t", i=16) for i in range(2))
            pw = pool.take()
            wa, wb = (pw.f[:, 256 * i:256 * i + 256] for i in range(2))
            cur_r, cur_i, nxt_r, nxt_i = pv[16], pv[17], pv[18], pv[19]

            def square(*after):
                a = V(lambda e, r=cur_r: e.tensor_tensor(u1, r, r, MUL), *after)
                b = V(lambda e, i=cur_i: e.tensor_tensor(u2, i, i, MUL), *after)
                d = V(lambda e, r=cur_r, i=cur_i: e.tensor_tensor(nxt_i, r, i, MUL), *after)
                a = V(lambda e: e.tensor_tensor(nxt_r, u1, u2, SUB), a, b)
                d = V(lambda e: e.tensor_scalar(nxt_i, nxt_i, 2.0, None, MUL), d)
                a = V(lambda e: e.tensor_copy(cur_r, nxt_r), a)
                d = V(lambda e: e.tensor_copy(cur_i, nxt_i), d)
                return a, d

            ta = V(lambda e: e.tensor_copy(cur_r, cs), tc)
            tb_ = V(lambda e: e.tensor_copy(cur_i, sn), ts)

            def table(R, I, bits, tr, ti, *after):
                t1 = V(lambda e: e.memset(R[:, :, 0:1], 1.0), *after)
                t2 = V(lambda e: e.memset(I[:, :, 0:1], 0.0), *after)
                w1 = lambda n: wa[:, 0:16 * n].rearrange("p (i t) -> p i t", i=16)
                w2 = lambda n: wb[:, 0:16 * n].rearrange("p (i t) -> p i t", i=16)
                for b in range(bits):
                    n = 1 << b
                    cr = cur_r.unsqueeze(2).to_broadcast([128, 16, n])
                    ci = cur_i.unsqueeze(2).to_broadcast([128, 16, n])
                    a = V(lambda e, n=n, cr=cr: e.tensor_tensor(w1(n), R[:, :, 0:n], cr, MUL), tr, t1, t2)
                    d = V(lambda e, n=n, ci=ci: e.tensor_tensor(w2(n), I[:, :, 0:n], ci, MUL), ti, t1, t2)
                    t1 = V(lambda e, n=n: e.tensor_tensor(R[:, :, n:2 * n], w1(n), w2(n), SUB), a, d)
                    a = V(lambda e, n=n, ci=ci: e.tensor_tensor(w1(n), R[:, :, 0:n], ci, MUL), t1)
                    d = V(lambda e, n=n, cr=cr: e.tensor_tensor(w2(n), I[:, :, 0:n], cr, MUL), t1)
                    t2 = V(lambda e, n=n: e.tensor_tensor(I[:, :, n:2 * n], w1(n), w2(n), ADD), a, d)
                    tr, ti = square(t2)
                    yield
                return tr, ti, t1, t2

            tr, ti, l1, l2 = yield from table(lr, li, 5, ta, tb_, *el_r.free, *el_i.free, *pw.free)
            tr, ti, h1_, h2_ = yield from table(hr, hi_, 4, tr, ti, *eh.free)
            pool.give(pw, h2_)
            t_pow = h2_

            late_c = deque()
            ahead = None

            def rotation(i):
                er, ei, w = pool.take(), pool.take(), pool.take()
                v3 = lambda s: s.f.rearrange("p (a b) -> p a b", a=16)
                br_ = lr[:, i, :].unsqueeze(1).to_broadcast([128, 16, 32])
                bi_ = li[:, i, :].unsqueeze(1).to_broadcast([128, 16, 32])
                ar_ = hr[:, i, :].unsqueeze(2).to_broadcast([128, 16, 32])
                ai_ = hi_[:, i, :].unsqueeze(2).to_broadcast([128, 16, 32])
                t1 = G(lambda e, er=er, a=ar_, b=br_: e.tensor_tensor(v3(er), a, b, MUL), t_pow, *er.free)
                t2 = G(lambda e, w=w, a=ai_, b=bi_: e.tensor_tensor(v3(w), a, b, MUL), *w.free)
                t_er = G(lambda e, er=er, w=w: e.tensor_tensor(er.f, er.f, w.f, SUB), t1, t2)
                t1 = G(lambda e, ei=ei, a=ar_, b=bi_: e.tensor_tensor(v3(ei), a, b, MUL), *ei.free)
                t2 = G(lambda e, w=w, a=ai_, b=br_: e.tensor_tensor(v3(w), a, b, MUL), t_er)
                t_ei = G(lambda e, ei=ei, w=w: e.tensor_tensor(ei.f, ei.f, w.f, ADD), t1, t2)
                pool.give(w, t_ei)
                return er, ei, t_er, t_ei


            def c_product(st, cc, yb):
                k, gr, t1, h2, t3 = st
                for c, (hh, th) in enumerate(((gr, t1), (h2, t3))):
                    s, tcx = cc[c]
                    tok = P(lambda e, c=c, k=k, s=s, hh=hh, yb=yb: e.matmul(
                        yb.ap[:, :], s.f[:, k * 128:(k + 1) * 128], hh.f, start=(k == 0 and c == 0),
                        stop=(k == 3 and c == 1)), th, tcx, yb.free)
                    pool.give(hh, tok)
                return tok

            mine = Pool([psum.take() for _ in range(3)])

            def mine_give(b, tok):
                mine.q.append(b)
                b.free = tok

            for j in range(4):
                u, tu = us[j]
                bT = []
                for c in range(2):
                    b = mine.take()
                    d = bpad[4 * c + j]
                    for k in range(4):
                        tok = P(lambda e, b=b, d=d, k=k: e.transpose(b.ap[:, k * 128:(k + 1) * 128],
                                                                     d.f[:, k * 128:(k + 1) * 128], ident[:, :]),
                                bt[4 * c + j], b.free, t_id)
                    s = pool.take()
                    t = A(lambda e, b=b, s=s: e.activation(s.f, b.ap[:, :], ACT.Copy), tok, *s.free)
                    mine_give(b, t)
                    pool.give(d, tok)
                    bT.append((s, t))
                cc = []
                for c in range(2):
                    s = pool.take()
                    cc.append((s, load(s.f, cpad[c, j], *s.free)))
                yb = None
                pend = None
                for k in range(4):
                    i = 4 * j + k
                    er, ei, t_er, t_ei = ahead or rotation(i)
                    bk = []
                    for c in range(2):
                        b = mine.take()
                        s, t = bT[c]
                        bk.append((b, P(lambda e, b=b, s=s, k=k, u=u: e.matmul(b.ap[:, :], s.f[:, k * 128:(k + 1) * 128], u.f,
                                                                          start=True, stop=True), t, tu, b.free)))
                    (b0, p0), (b1, p1) = bk
                    gr, gi, w1, w2 = (pool.take() for _ in range(4))
                    t1 = V(lambda e, gr=gr, b0=b0, er=er: e.tensor_tensor(gr.f, b0.ap[:, :], er.f, MUL), p0, t_er, *gr.free)
                    t2 = V(lambda e, w1=w1, b1=b1, ei=ei: e.tensor_tensor(w1.f, b1.ap[:, :], ei.f, MUL), p1, t_ei, *w1.free)
                    t3 = V(lambda e, gi=gi, b1=b1, er=er: e.tensor_tensor(gi.f, b1.ap[:, :], er.f, MUL), *gi.free)
                    mine_give(b1, t3)
                    t4 = V(lambda e, w2=w2, b0=b0, ei=ei: e.tensor_tensor(w2.f, b0.ap[:, :], ei.f, MUL), *w2.free)
                    mine_give(b0, t4)
                    t1 = G(lambda e, gr=gr, w1=w1: e.tensor_tensor(gr.f, gr.f, w1.f, ADD), t1, t2)
                    t3 = G(lambda e, gi=gi, w2=w2: e.tensor_tensor(gi.f, gi.f, w2.f, SUB), t3, t4)
                    yield
                    if len(late_c) > LATE:
                        c_product(late_c.popleft(), cc, yb)
                    mg = mag[:, i:i + 1].to_broadcast([128, 512])
                    sr = V(lambda e, w1=w1, gr=gr, mg=mg: e.tensor_tensor_scan(w1.f, mg, gr.f, 0.0, MUL, ADD), t1, t_mag)
                    si = V(lambda e, w2=w2, gi=gi, mg=mg: e.tensor_tensor_scan(w2.f, mg, gi.f, 0.0, MUL, ADD), t3)
                    h2 = pool.take()
                    t1 = V(lambda e, gr=gr, w1=w1, er=er: e.tensor_tensor(gr.f, w1.f, er.f, MUL), sr)
                    t2 = V(lambda e, gi=gi, w2=w2, ei=ei: e.tensor_tensor(gi.f, w2.f, ei.f, MUL), si)
                    t1 = V(lambda e, gr=gr, gi=gi: e.tensor_tensor(gr.f, gr.f, gi.f, SUB), t1, t2)
                    t3 = V(lambda e, h2=h2, w1=w1, ei=ei: e.tensor_tensor(h2.f, w1.f, ei.f, MUL), *h2.free)
                    t4 = V(lambda e, gi=gi, w2=w2, er=er: e.tensor_tensor(gi.f, w2.f, er.f, MUL), t1)
                    t3 = V(lambda e, h2=h2, gi=gi: e.scalar_tensor_tensor(out=h2.f, in0=h2.f, scalar=-1.0, in1=gi.f,
                                                                          op0=MUL, op1=SUB), t3, t4)
                    pool.give(w1, t3)
                    pool.give(w2, t4)
                    pool.give(er, t4)
                    pool.give(ei, t3)
                    pool.give(gi, t3)
                    ahead = rotation(i + 1) if i < 15 else None
                    yield
                    if yb is None:
                        yb = mine.take()
                    late_c.append((k, gr, t1, h2, t3))
                    if k == 3:
                        yield
                        while late_c:
                            tok = c_product(late_c.popleft(), cc, yb)
                yt = pool.take()
                t = V(lambda e, yt=yt, u=u, yb=yb, j=j: e.scalar_tensor_tensor(
                    out=yt.f, in0=u.f, scalar=col("dskip", j), in1=yb.ap[:, :], op0=MUL, op1=ADD), tok, tu, *yt.free)
                mine_give(yb, t)
                pool.give(u, t)
                for s, _ in bT + cc:
                    pool.give(s, tok)
                t = A(lambda e, yt=yt: e.activation(yt.f, yt.f, ACT.Gelu_apprx_tanh), t)
                h, l, th, tl = split(yt.f, t)
                pool.give(yt, tl)
                ys.append(operand(h, l, th, tl) + (h, l))
                yield
            ssm_out.extend(ys)
            for s in (el_r, el_i, eh):
                pool.give(s, t_ei)
            pool.give(pp, t3)
            while mine.q:
                psum.q.append(mine.q.popleft())

        ssm_out = []
        bg = ssm()

        def step(n=1):
            for _ in range(n):
                try:
                    next(bg)
                except StopIteration:
                    return

        for _ in range(4):
            step()
        rc1, rs1, t_rc1, t_rs1 = rope_table(pos1, col("if1"), col("sg1"))

        DIL = (1, 4, 16)
        SCALE = 1.0 / math.sqrt(128.0)
        OT = [[None] * 4 for _ in range(3)]
        st_t = {}
        MO, DO = stat_cols(48), stat_cols(48)

        def perm(ap, d):
            if d == 1:
                return ap
            if len(ap.shape) == 2:
                return ap.rearrange("p (r l) -> p l r", r=d)

        def nat(ap, d):
            return ap if d == 1 else ap.rearrange("p (l r) -> p l r", r=d)

        def rope(b, dst, rows, tbl, d, tok_copy):
            c, s, tc_, ts_ = tbl
            w1, w2 = pool.take(), pool.take()
            mask = list(range(16, 32)) + list(range(16))
            t1 = V(lambda e: e.tensor_tensor(w1.f[rows, :], b.ap[rows, :], c.f[rows, :], MUL), tok_copy, tc_, *w1.free)
            t2 = V(lambda e: e.stream_shuffle(w2.f[rows, :], b.ap[rows, :], mask), *w2.free)
            psum.give(b, t2)
            q = G if rows.start == 0 else V
            q2 = V if d != 1 or rows.start else q
            t2 = q(lambda e: e.tensor_tensor(w2.f[rows, :], w2.f[rows, :], s.f[rows, :], MUL), t2, ts_)
            t = q2(lambda e: e.tensor_tensor(perm(dst.f[rows, :], d), nat(w1.f[rows, :], d), nat(w2.f[rows, :], d), ADD),
                  t1, t2, tok_copy)
            pool.give(w1, t)
            pool.give(w2, t)
            return t

        tbl1 = (rc1, rs1, t_rc1, t_rs1)

        def qkv(g, h):
            d = DIL[g]
            got = []
            for part in range(3):
                b, tok = yield from gproject("in", part * 12 + g * 4 + h, n1)
                s = pool.take()
                t = A(lambda e, b=b, s=s: e.activation(perm(s.f, d), nat(b.ap[:, :], d), ACT.Copy), tok, *s.free)
                if part < 2:
                    t = rope(b, s, slice(0, 32), tbl1, d, t)
                else:
                    psum.give(b, t)
                got.append((s, t))
                step(STEPS[(h * 3 + g) * 3 + part])
            return got

        def scores(g, h, got):
            (q, tq), (k, tk), (v, tv) = got
            vb = psum.take()
            for n in range(4):
                tok = P(lambda e, n=n: e.transpose(vb.ap[:, n * 128:(n + 1) * 128], v.f[:, n * 128:(n + 1) * 128], ident[:, :]),
                        tv, vb.free)
            vn = pool.take()
            t_vn = A(lambda e: e.activation(vn.f, vb.ap[:, :], ACT.Copy), tok, *vn.free)
            psum.give(vb, t_vn)
            pool.give(v, tok)
            yield
            if g == 0:
                parts = [[(0, 0, 128, m_diag, 128), (1, 128, 256, m_prev, 256)],
                         [(2, 0, 256, m_prev, 256), (3, 256, 256, m_prev, 256)]]
            else:
                parts = [[(n, n * 128, 128, m_diag if g == 1 else m_blk, 128) for n in range(4)]]
            probs = {}
            for part in parts:
                b = psum.take()
                for n, o, w, mo, mw in part:
                    k0 = (n - 1) * 128 if w == 256 else n * 128
                    P(lambda e, n=n, o=o, w=w, k0=k0, b=b: e.matmul(b.ap[:, o:o + w], q.f[:, n * 128:(n + 1) * 128],
                                                                    k.f[:, k0:k0 + w], start=True, stop=False),
                      tq, tk, b.free)
                    tok = P(lambda e, o=o, w=w, mo=mo, b=b: e.matmul(b.ap[:, o:o + w], identb[:, :], maskb[:, mo:mo + w],
                                                                     start=False, stop=True), t_idb, t_mb)
                mcol = lambda n: MO + g * 16 + n * 4 + h
                t = None
                if g == 0:
                    for n, o, w, *_ in part:
                        t = V(lambda e, n=n, o=o, w=w, b=b: e.tensor_reduce(stat[:, mcol(n):mcol(n) + 1], b.ap[:, o:o + w], AX, MAX), tok)
                else:
                    t = V(lambda e, b=b: e.tensor_reduce(stat[:, MO + g * 16 + h:MO + g * 16 + 16:4],
                                                         b.ap[:, :].rearrange("p (n c) -> p n c", n=4), AX, MAX), tok)
                n0, n1_ = part[0][0], part[-1][0]
                neg = scl[:, 4 * ((h * 3 + g) % 8) + n0:4 * ((h * 3 + g) % 8) + n1_ + 1]
                t_m = t
                t = V(lambda e, neg=neg, n0=n0, n1_=n1_: e.tensor_scalar(neg, stat[:, mcol(n0):mcol(n1_) + 1:4], -SCALE, None, MUL), t,
                      neg_free[(h * 3 + g) % 8])
                p = pool.take()
                for n, o, w, *_ in part:
                    te = A(lambda e, p=p, b=b, n=n, o=o, w=w, neg=neg, n0=n0: e.activation(
                        p.f[:, o:o + w], b.ap[:, o:o + w], ACT.Exp, bias=neg[:, n - n0:n - n0 + 1], scale=SCALE,
                        accum_out=stat[:, DO + g * 16 + n * 4 + h:DO + g * 16 + n * 4 + h + 1]), t, *p.free)
                    probs[n] = (p, o, w, te)
                psum.give(b, te)
                neg_free[(h * 3 + g) % 8] = te
                yield
            st_t[(g, h)] = (t_m, te)
            pool.give(q, tok)
            pool.give(k, tok)
            return vn, t_vn, probs, parts

        neg_free = [None] * 8

        def values(g, h, sc):
            vn, t_vn, probs, parts = sc
            ob = psum.take()
            pts = []
            for part in parts:
                p = probs[part[0][0]][0]
                b = psum.take()
                width = part[-1][1] + part[-1][2]
                te = probs[part[-1][0]][3]
                for c in range(width // 128):
                    tok = P(lambda e, c=c, b=b, p=p: e.transpose(b.ap[:, c * 128:(c + 1) * 128], p.f[:, c * 128:(c + 1) * 128],
                                                                 ident[:, :]), te, b.free)
                pool.give(p, tok)
                pt = pool.take()
                t = A(lambda e, b=b, pt=pt, width=width: e.activation(pt.f[:, 0:width], b.ap[:, 0:width], ACT.Copy), tok, *pt.free)
                psum.give(b, t)
                pts.append((part, pt, t))
                yield
            for part, pt, t in pts:
                for n, o, w, *_ in part:
                    keys = [n] if w == 128 else [n - 1, n]
                    for x, kb in enumerate(keys):
                        tok = P(lambda e, n=n, o=o, x=x, kb=kb, pt=pt, last=(x == len(keys) - 1), ff=(x == 0): e.matmul(
                            ob.ap[:, n * 128:(n + 1) * 128], vn.f[:, kb * 128:(kb + 1) * 128],
                            pt.f[:, o + x * 128:o + (x + 1) * 128], start=ff, stop=last), t, t_vn, ob.free)
                pool.give(pt, tok)
                if part is not parts[-1]:
                    yield
            pool.give(vn, tok)
            o_ = pool.take()
            d = DIL[g]
            src = ob.ap[:, :] if d == 1 else ob.ap[:, :].rearrange("p (r l) -> p l r", r=d)
            t = A(lambda e: e.activation(nat(o_.f, d), src, ACT.Copy), tok, *o_.free)
            psum.give(ob, t)
            OT[g][h] = (o_, t)

        def head(g, h, got):
            yield from values(g, h, (yield from scores(g, h, got)))

        def sigmoid_of(b, tok):
            s = pool.take()
            t = A(lambda e: e.activation(s.f, b.ap[:, :], ACT.Sigmoid), tok, *s.free)
            psum.give(b, t)
            return s, t

        gates = []

        def gate_tile(j):
            b, tok = yield from gproject("in", 40 + j, n1)
            gates.append(sigmoid_of(b, tok))

        lo_turn["mode"] = "VG"
        pieces, count = iter(()), 0
        for h in range(4):
            for g in range(3):
                got = beside(qkv(g, h), 24, pieces, count)
                pieces, count = head(g, h, got), (7 if g == 0 else 4)
        beside(gate_tile(0), 8, pieces, count)
        step()
        pool.give(rc1, t_rc1, G.last())
        pool.give(rs1, t_rs1, G.last())

        rows_m, rows_d = [], []
        for kind, base, lst in ((0, MO, rows_m), (1, DO, rows_d)):
            for g in range(3):
                b = psum.take()
                for n in range(4):
                    c0 = base + g * 16 + n * 4
                    tok = P(lambda e, b=b, n=n, c0=c0: e.transpose(b.ap[0:4, n * 128:(n + 1) * 128], stat[:, c0:c0 + 4], ident[:, :]),
                            *[st_t[(g, h)][kind] for h in range(4)], b.free)
                s = pool.take()
                d = DIL[g]
                src = b.ap[0:4, :] if d == 1 else b.ap[0:4, :].rearrange("p (r l) -> p l r", r=d)
                t = A(lambda e, s=s, src=src, d=d: e.activation(nat(s.f[0:4, :], d), src, ACT.Copy), tok, *s.free)
                psum.give(b, t)
                lst.append((s, t))
        for j in (1, 2):
            whole(gate_tile(j))
            step(1)
        mx = pool.take()
        (m0, a0), (m1, a1), (m2, a2) = rows_m
        t = V(lambda e: e.tensor_tensor(mx.f[0:4, :], m0.f[0:4, :], m1.f[0:4, :], MAX), a0, a1, *mx.free)
        t = V(lambda e: e.tensor_tensor(mx.f[0:4, :], mx.f[0:4, :], m2.f[0:4, :], MAX), t, a2)
        te = []
        for s, _ in rows_m:
            x = V(lambda e, s=s: e.tensor_tensor(s.f[0:4, :], s.f[0:4, :], mx.f[0:4, :], SUB), t)
            te.append(A(lambda e, s=s: e.activation(s.f[0:4, :], s.f[0:4, :], ACT.Exp, scale=SCALE), x))
        tz = None
        for g in range(3):
            (e_s, _), (d_s, td) = rows_m[g], rows_d[g]
            x = V(lambda e, e_s=e_s, d_s=d_s: e.tensor_tensor(d_s.f[0:4, :], d_s.f[0:4, :], e_s.f[0:4, :], MUL), te[g], td)
            if g == 0:
                tz = V(lambda e, d_s=d_s: e.tensor_copy(mx.f[0:4, :], d_s.f[0:4, :]), x)
            else:
                tz = V(lambda e, d_s=d_s: e.tensor_tensor(mx.f[0:4, :], mx.f[0:4, :], d_s.f[0:4, :], ADD), x, tz)
            pool.give(d_s, tz)
        tz = V(lambda e: e.reciprocal(mx.f[0:4, :], mx.f[0:4, :]), tz)
        tw = []
        for g in range(3):
            s = rows_m[g][0]
            tw.append(V(lambda e, s=s: e.tensor_tensor(s.f[0:4, :], s.f[0:4, :], mx.f[0:4, :], MUL), tz))
        pool.give(mx, tw[-1])
        for j in (3, 4):
            whole(gate_tile(j))
            step(1)
        attn = []
        selp = pool.take()
        t_sel = load(selp.f[0:4, :], consts[0:4, 640:1152], *selp.free)
        for h in range(4):
            acc = None
            for g in range(3):
                b = psum.take()
                s = rows_m[g][0]
                tok = P(lambda e, b=b, s=s, h=h: e.matmul(b.ap[:, :], selp.f[0:4, h * 128:(h + 1) * 128], s.f[0:4, :],
                                                          start=True, stop=True), tw[g], t_sel, b.free)
                o_, to = OT[g][h]
                t = V(lambda e, o_=o_, b=b: e.tensor_tensor(o_.f, o_.f, b.ap[:, :], MUL), to, tok)
                psum.give(b, t)
                if acc is None:
                    acc, ta = o_, t
                else:
                    ta = (V if h == 3 else G)(lambda e, acc=acc, o_=o_: e.tensor_tensor(acc.f, acc.f, o_.f, ADD), t, ta)
                    pool.give(o_, ta)
            hs, ls, th, tl = split(acc.f, ta)
            pool.give(acc, tl)
            attn.append(operand(hs, ls, th, tl) + (hs, ls))
            if h < 3:
                whole(gate_tile(5 + h))
            step(1)
        for s, _ in rows_m:
            pool.give(s, tok)
        pool.give(selp, tok)

        def free_ops(ops, tok):
            for x in ops:
                pool.give(x[3], tok)
                pool.give(x[4], tok)

        def three(ops):
            return [x[:3] for x in ops]

        at3 = three(attn)
        for m in range(8):
            if m == 0:
                two = project2("ap", 0, "ap", 1, at3)
            b, tok = two[m] if m < 2 else project("ap", m, at3)
            ga, tga = gates[m]
            t = V(lambda e, ga=ga, b=b: e.tensor_tensor(ga.f, ga.f, b.ap[:, :], MUL), tga, tok)
            psum.give(b, t)
            gates[m] = (ga, t)
            step(1)
        free_ops(attn, P.last())
        for m in range(8):
            whole(gate_tile(8 + m))
            step(1)
        free_ops(n1s, P.last())
        step(80)
        y3 = three(ssm_out)
        merged = []
        for m in range(8):
            (ga, t), (gs, tgs) = gates[m], gates[8 + m]
            sb_, tsb = sigmoid_of(*project("gb", m, y3))
            b, tok = project("ga", m, y3)
            t2 = V(lambda e, sb_=sb_, b=b: e.tensor_tensor(sb_.f, sb_.f, b.ap[:, :], MUL), tsb, tok)
            psum.give(b, t2)
            q = V if m == 7 else G
            t2 = q(lambda e, sb_=sb_, gs=gs: e.tensor_tensor(gs.f, gs.f, sb_.f, MUL), t2, tgs)
            pool.give(sb_, t2)
            t = q(lambda e, ga=ga, gs=gs: e.tensor_tensor(ga.f, ga.f, gs.f, ADD), t, t2)
            pool.give(gs, t)
            h, l, th, tl = split(ga.f, t)
            pool.give(ga, tl)
            merged.append(operand(h, l, th, tl) + (h, l))
        free_ops(ssm_out, P.last())
        lo_turn["mode"] = "VG"

        hs_ = []
        for k in range(8):
            s = pool.take()
            hs_.append([s, load(s.f, xT[k], *s.free)])
        mg3 = three(merged)
        nrm = Norm()

        def residual(name, ops, nrm=None, k0=0, gate=None, then=None):
            two = project2(name, 0, name, 1, ops, k0)
            for m in range(8):
                b, tok = two[m] if m < 2 else project(name, m, ops, k0)
                s, ts_ = hs_[m]
                if gate is None:
                    t = V(lambda e, s=s, b=b: e.tensor_tensor(s.f, s.f, b.ap[:, :], ADD), tok, ts_)
                else:
                    t = V(lambda e, s=s, b=b, m=m: e.scalar_tensor_tensor(out=s.f, in0=b.ap[:, :], scalar=gate(m), in1=s.f,
                                                                          op0=MUL, op1=ADD), tok, ts_)
                psum.give(b, t)
                hs_[m][1] = t
                if nrm is not None:
                    nrm.add(s.f, t)
                if then is not None:
                    then(m)

        pl = []
        for k in range(2):
            s = pool.take()
            t = load(s.f, pT[k], *s.free)
            h, l, th, tl = split(s.f, t)
            pool.give(s, tl)
            pl.append(operand(h, l, th, tl) + (h, l))
        residual("out", mg3, nrm)
        free_ops(merged, P.last())

        ple = []

        def ple_tile(m):
            b, tok = project("pp", m, three(pl))
            s = pool.take()
            t = A(lambda e: e.activation(s.f, b.ap[:, :], ACT.Copy), tok, *s.free)
            psum.give(b, t)
            ple.append((s, t))

        def normed(rb, trb, g, q2=None):
            for *_, ops in scaled(hs_, g, rb, trb):
                pass
            return ops

        ple_tile(0)
        ple_tile(1)
        dg = nrm.rstd(1024, stat_cols(4))
        ple_tile(2)
        ple_tile(3)
        n2 = normed(*broadcast(*dg), lambda k: col("g_ffn", k))
        for m in range(4, 8):
            ple_tile(m)
        free_ops(pl, P.last())

        def params2():
            nonlocal rc2, rs2, t_rc2, t_rs2, r_, rn_, t_sp, rst, keep_, t_keep, t_rst
            rc2, rs2, t_rc2, t_rs2 = yield from rope_steps(pos2, col("if2"), col("sg2"))
            sp = stat_cols(70)
            spv = [stat[:, sp + 10 * i:sp + 10 * i + 10] for i in range(7)]
            lru = col("lru", 0, 10)
            a_, z_, s_2, u_, acc_, r_, rn_ = spv
            t = V(lambda e: e.tensor_scalar(a_, lru, -1.0, None, MUL), t_sm)
            t = V(lambda e: e.tensor_tensor(a_, a_, lru, MIN), t)
            t = A(lambda e: e.activation(z_, a_, ACT.Exp), t)
            yield
            t = V(lambda e: e.tensor_scalar(u_, z_, 2.0, None, ADD), t)
            t = V(lambda e: e.reciprocal(u_, u_), t)
            t = V(lambda e: e.tensor_tensor(z_, z_, u_, MUL), t)
            t = V(lambda e: e.tensor_tensor(s_2, z_, z_, MUL), t)
            t = V(lambda e: e.tensor_scalar(acc_, s_2, 1.0 / 17, 1.0 / 15, MUL, ADD), t)
            yield
            for n in (13, 11, 9, 7, 5, 3, 1):
                t = V(lambda e: e.tensor_tensor(acc_, acc_, s_2, MUL), t)
                t = V(lambda e, n=n: e.tensor_scalar(acc_, acc_, 1.0 / n, None, ADD), t)
            t = V(lambda e: e.tensor_tensor(acc_, acc_, z_, MUL), t)
            t = V(lambda e: e.tensor_scalar(acc_, acc_, 8.0, None, MUL), t)
            t = V(lambda e: e.tensor_scalar(r_, lru, -4.0, 0.0, MUL, MAX), t)
            t = V(lambda e: e.tensor_tensor(r_, r_, acc_, ADD), t)
            t_sp = V(lambda e: e.tensor_scalar(rn_, r_, -2.0, None, MUL), t)
            yield
            rst = pool.take()
            pi = pool.take()
            tp = load(pi.f.bitcast(I32), pos2[:, :], *pi.free)
            yield
            t = V(lambda e: e.tensor_copy(rst.f, pi.f.bitcast(I32)), tp, *rst.free)
            pool.give(pi, t)
            keep_ = pool.take()
            t_keep = V(lambda e: e.tensor_scalar(keep_.f, rst.f, 0.0, None, ALU.not_equal), t, *keep_.free)
            t_rst = V(lambda e: e.tensor_scalar(rst.f, rst.f, 0.0, None, ALU.is_equal), t_keep)

        rc2 = rs2 = t_rc2 = t_rs2 = r_ = rn_ = t_sp = rst = keep_ = t_keep = t_rst = None

        def ada():
            yield from params2()
            cr = [pool.take() for _ in range(2)]
            tcs = []
            for i, s in enumerate(cr):
                t = load(s.f, cT[:, i * 512:(i + 1) * 512], *s.free)
                tcs.append(A(lambda e, s=s: e.activation(s.f, s.f, ACT.Silu), t))
            part = pool.take()
            for m in range(48):
                ws = [pool.take() for _ in range(2)]
                for i, s in enumerate(ws):
                    t = load(s.f, wadaT[m, :, i * 512:(i + 1) * 512], *s.free)
                    t = V(lambda e, s=s, i=i, m=m: e.tensor_tensor_reduce(
                        s.f, s.f, cr[i].f, 1.0, 0.0, MUL, ADD, part.f[:, 2 * m + i:2 * m + i + 1]), t, tcs[i], *part.free)
                    pool.give(s, t)
                yield
            t = V(lambda e: e.tensor_tensor(mod[:, :], part.f[:, 0:96:2], part.f[:, 1:96:2], ADD), t)
            t = V(lambda e: e.tensor_tensor(mod[:, :], mod[:, :], col("b_ada", 0, 48), ADD), t)
            V(lambda e: e.scalar_tensor_tensor(out=scl[:, 32:40], in0=mod[:, 8:16], scalar=1.0, in1=col("n1", 0, 8),
                                               op0=ADD, op1=MUL), t)
            t = V(lambda e: e.scalar_tensor_tensor(out=scl[:, 40:48], in0=mod[:, 32:40], scalar=1.0, in1=col("n2", 0, 8),
                                                   op0=ADD, op1=MUL))
            t_mod.append(t)
            for s in cr:
                pool.give(s, t)
            pool.give(part, t)

        t_mod = []
        bg = ada()

        def gated(name_g, name_u, m, ops):
            two = project2(name_g, m, name_u, m, ops) if m == 0 else (project(name_g, m, ops), None)
            b, tok = two[0]
            s = pool.take()
            t = A(lambda e: e.activation(s.f, b.ap[:, :], ACT.Silu), tok, *s.free)
            psum.give(b, t)
            b2, tok = two[1] or project(name_u, m, ops)
            t = V(lambda e: e.tensor_tensor(s.f, s.f, b2.ap[:, :], MUL), tok, t)
            psum.give(b2, t)
            h, l, th, tl = split(s.f, t)
            pool.give(s, tl)
            return operand(h, l, th, tl) + (h, l)

        h2 = []

        def split_h(k):
            s, t = hs_[k]
            h, l, th, tl = split(s.f, t, q=(V if k % 2 else G))
            h2.append(operand(h, l, th, tl) + (h, l))

        n23 = three(n2)
        for half in range(2):
            acts = []
            for m in range(11):
                acts.append(gated("fg", "fu", half * 11 + m, n23))
                step(2)
            if half == 1:
                free_ops(n2, P.last())
            residual("fd", three(acts), None, half * 11, then=split_h if half else None)
            free_ops(acts, P.last())
            step(8)
        for _ in range(50):
            step()

        nrm1, nrm2 = Norm(), Norm()
        late = deque()

        def two_sums():
            s, t, m = late.popleft()
            nrm1.add(s.f, t)
            nrm2.add(s.f, t, scale=col("g_final", m))

        t_g = V(lambda e: e.tensor_tensor(scl[:, 48:56], scl[:, 32:40], col("g_final", 0, 8), MUL), t_mod[0])
        h23 = three(h2)
        for mt in range(0, 8, 2):
            two = project2("pg", mt, "pg", mt + 1, h23) if mt == 0 else (project("pg", mt, h23), project("pg", mt + 1, h23))
            for m, (b, tok) in zip((mt, mt + 1), two):
                s_, t = sigmoid_of(b, tok)
                w, tw_ = ple[m]
                t = V(lambda e, s_=s_, w=w: e.tensor_tensor(s_.f, s_.f, w.f, MUL), t, tw_)
                pool.give(w, t)
                s, ts_ = hs_[m]
                t = V(lambda e, s=s, s_=s_: e.tensor_tensor(s.f, s.f, s_.f, ADD), t, ts_, h2[m][2][0], h2[m][2][1])
                pool.give(s_, t)
                hs_[m][1] = t
                late.append((s, t, m))
                if len(late) > 1:
                    two_sums()
        two_sums()
        free_ops(h2, P.last())

        so = stat_cols(12)
        r1, r12, v2 = (stat[:, so + 4 * i:so + 4 * i + 4] for i in range(3))
        half_ = scl[:, 94:95].to_broadcast([128, 4])
        (b1, t1), (b2, t2) = nrm1.total(), nrm2.total()
        t1 = V(lambda e, b1=b1: e.tensor_scalar(r1, b1.ap[:, 0:4], 1.0 / 1024, 1e-6, MUL, ADD), t1)
        t2 = V(lambda e, b2=b2: e.tensor_scalar(v2, b2.ap[:, 0:4], 1.0 / 1024, None, MUL), t2)
        psum.give(b1, t1)
        psum.give(b2, t2)
        t = V(lambda e: e.scalar_tensor_tensor(out=v2, in0=r1, scalar=1e-6, in1=v2, op0=MUL, op1=ADD), t1, t2)
        t = G(lambda e: e.tensor_tensor(r12, v2, half_, ALU.pow), t, t_half)
        t1 = G(lambda e: e.tensor_tensor(r1, r1, half_, ALU.pow), t1, t)
        rb, trb = broadcast(*diagonal(r12, t))
        rb1, trb1 = broadcast(*diagonal(r1, t1))

        def modulated(rb, trb, so, sh):
            ops, late = [], None

            def low(w, h, l, th, shift):
                tl = V(lambda e: e.scalar_tensor_tensor(out=l.r, in0=w.f, scalar=shift, in1=h.r.bitcast(F32),
                                                        op0=ADD, op1=SUB), th, *l.free)
                pool.give(w, th, tl)
                ops.append(operand(h, l, th, tl) + (h, l))

            for k in range(8):
                s, ts_ = hs_[k]
                w, h, l = pool.take(), pool.take(), pool.take()
                shift = mod[:, sh + k:sh + k + 1]
                t = V(lambda e, s=s, w=w, k=k: e.scalar_tensor_tensor(out=w.f, in0=s.f, scalar=scl[:, so + k:so + k + 1],
                                                                      in1=rb.ap[:, :], op0=MUL, op1=MUL),
                      ts_, trb, t_mod[0], *w.free)
                th = A(lambda e, w=w, h=h, shift=shift: e.activation(h.r, w.f, ACT.Identity, bias=shift), t, *h.free)
                if late:
                    low(*late)
                late = (w, h, l, th, shift)
            low(*late)
            psum.give(rb, t)
            return ops

        lo_turn["mode"] = "G"
        nn = modulated(rb, trb, 48, 0)
        nn3 = three(nn)

        gw = []
        for i in range(5):
            s = pool.take()
            gw.append((s, load(s.f, gblk[i], *s.free)))

        def x2_tile(k):
            s, ts_ = hs_[k]
            t = V(lambda e: e.scalar_tensor_tensor(out=s.f, in0=s.f, scalar=col("g_final", k), in1=rb1.ap[:, :],
                                                   op0=MUL, op1=MUL), ts_, trb1, nn[k][2][0])
            keep = load(spare[k], s.f, t)
            pool.give(s, keep)
            hs_[k] = keep
            return t

        def lru_conv(i, b, tok):
            xc = pool.take()
            t = V(lambda e: e.tensor_scalar(xc.f, b.ap[:, :], col("convw", 30 + i), col("convb", i), MUL, ADD), tok, *xc.free)
            for k in (1, 2, 3):
                t = V(lambda e, k=k: e.scalar_tensor_tensor(
                    out=xc.f[:, k:512], in0=b.ap[:, 0:512 - k], scalar=col("convw", (3 - k) * 10 + i), in1=xc.f[:, k:512],
                    op0=MUL, op1=ADD), t)
            psum.give(b, t)
            return i, xc, t

        def lru_work(convs):
            for part in range(2):
                group = range(5 * part, 5 * part + 5)
                for i in group:
                    lru_gate(*convs[i])
                    if i % 5:
                        lru_tanh(i - 1)
                    yield
                lru_tanh(group[-1])
                for i in group:
                    lru_exp(i)
                yield
                for i in group:
                    lru_input(i)
                yield
                late = None
                for i in group:
                    now = lru_scan(i)
                    if late:
                        lru_low(*late)
                    late = now
                    if i % 5 == 2:
                        yield
                lru_low(*late)

        lr_st = {}

        def lru_gate(i, xc, t):
            g_s, tg = gw[i // 2]
            o = (i % 2) * 256
            b1, b2 = psum.take(), psum.take()
            tk1 = P(lambda e: e.matmul(b1.ap[:, :], g_s.f[:, o:o + 128], xc.f, start=True, stop=True), t, tg, b1.free)
            tk2 = P(lambda e: e.matmul(b2.ap[:, :], g_s.f[:, o + 128:o + 256], xc.f, start=True, stop=True), b2.free)
            if i % 2:
                pool.give(g_s, tk2)
            r, x = pool.take(), pool.take()
            t1 = A(lambda e: e.activation(r.f, b1.ap[:, :], ACT.Sigmoid, bias=col("ba", i)), tk1, *r.free)
            psum.give(b1, t1)
            t2 = A(lambda e: e.activation(x.f, b2.ap[:, :], ACT.Sigmoid, bias=col("bx", i)), tk2, *x.free)
            psum.give(b2, t2)
            t2 = G(lambda e: e.tensor_tensor(x.f, x.f, xc.f, MUL), t2, tk2)
            lr_st[i] = (r, x, xc, t1, t2)

        def lru_tanh(i):
            r, x, xc, t1, t2 = lr_st[i]
            t3 = A(lambda e: e.activation(xc.f, r.f, ACT.Tanh, scale=r_[:, i:i + 1]), t1, t2, t_sp)
            t3 = V(lambda e: e.tensor_tensor(xc.f, xc.f, rst.f, MAX), t3, t_rst)
            lr_st[i] = (r, x, xc, t1, t2, t3)

        def lru_exp(i):
            r, x, xc, t1, t2, t3 = lr_st[i]
            t1 = A(lambda e: e.activation(r.f, r.f, ACT.Exp, scale=rn_[:, i:i + 1]), t3, t_sp)
            lr_st[i] = (r, x, xc, t1, t2, t3)

        def lru_input(i):
            r, x, xc, t1, t2, t3 = lr_st[i]
            t1 = V(lambda e: e.tensor_tensor(r.f, r.f, keep_.f, MUL), t1, t_keep)
            t2 = V(lambda e: e.scalar_tensor_tensor(out=x.f, in0=r.f, scalar=1.0, in1=x.f, op0=ADD, op1=MUL), t1, t2)
            t3 = A(lambda e: e.activation(xc.f, xc.f, ACT.Sqrt), t3)
            t2 = G(lambda e: e.tensor_tensor(x.f, x.f, xc.f, MUL), t3, t2)
            lr_st[i] = (r, x, xc, t1, t2, t3)

        def lru_scan(i):
            a, x, r, t1, t2, t3 = lr_st[i]
            t = V(lambda e: e.tensor_tensor_scan(r.f, a.f, x.f, 0.0, MUL, ADD), t2, t1)
            pool.give(x, t)
            pool.give(a, t)
            t_lru.append(t)
            h = pool.take()
            return r, h, A(lambda e: e.activation(h.r, r.f, ACT.Copy), t, *h.free)

        def lru_low(r, h, th):
            l = pool.take()
            tl = V(lambda e: e.tensor_tensor(l.r, r.f, h.r.bitcast(F32), SUB), th, *l.free)
            pool.give(r, tl)
            yr.append(operand(h, l, th, tl) + (h, l))

        yr, t_lru = [], []
        convs = []
        lo_turn["mode"] = "VG"
        two = project2("in2", 0, "in2", 1, nn3)
        convs.append(lru_conv(0, *two[0]))
        convs.append(lru_conv(1, *two[1]))
        bg = lru_work(convs)
        for i in range(2, 10):
            convs.append(lru_conv(i, *project("in2", i, nn3)))
            if i % 2:
                step()

        lat = []
        nq, nk = Norm(), Norm()
        pend = None
        for i in range(5):
            b, tok = project("in2", 10 + i, nn3)
            s = pool.take()
            t = A(lambda e, s=s, b=b: e.activation(s.f, b.ap[:, :], ACT.Copy), tok, *s.free)
            psum.give(b, t)
            (nq if i < 3 else nk).add(s.f, t)
            lat.append((s, t))
            step()
        b, tok = project("in2", 15, nn3)
        kr = pool.take()
        tkr = A(lambda e, b=b: e.activation(kr.f, b.ap[:, :], ACT.Copy), tok, *kr.free)
        tbl2 = (rc2, rs2, t_rc2, t_rs2)
        w1, w2 = pool.take(), pool.take()
        mask = list(range(16, 32)) + list(range(16))
        t1 = V(lambda e, b=b: e.tensor_tensor(w1.f, b.ap[:, :], rc2.f, MUL), tkr, t_rc2, *w1.free)
        t2 = V(lambda e, b=b: e.stream_shuffle(w2.f, b.ap[:, :], mask), *w2.free)
        psum.give(b, t2)
        t2 = G(lambda e: e.tensor_tensor(w2.f, w2.f, rs2.f, MUL), t2, t_rs2)
        tkr = G(lambda e: e.tensor_tensor(kr.f, w1.f, w2.f, ADD), t1, t2, tkr)
        pool.give(w1, tkr)
        pool.give(w2, tkr)

        def latent(nrm, tiles, gname):
            rb, trb = broadcast(*nrm)
            ops = []
            for k, (s, ts_) in enumerate(tiles):
                t = V(lambda e, s=s, k=k: e.scalar_tensor_tensor(out=s.f, in0=s.f, scalar=col(gname, k), in1=rb.ap[:, :],
                                                                 op0=MUL, op1=MUL), ts_, trb)
                h, l, th, tl = split(s.f, t)
                pool.give(s, tl)
                ops.append(operand(h, l, th, tl) + (h, l))
            psum.give(rb, t)
            return ops

        g_rnn, g_mla = [], []
        for m in range(8):
            b, tok = project("in2", 16 + m, nn3)
            s = pool.take()
            t = A(lambda e, b=b, s=s: e.activation(s.f, b.ap[:, :], ACT.Copy), tok, *s.free)
            psum.give(b, t)
            g_rnn.append((s, t))
            if m == 0:
                nk = nk.rstd(256, stat_cols(4))
                nq = nq.rstd(384, stat_cols(4))
            if m == 2:
                kl = latent(nk, lat[3:], "kg")
                ql = latent(nq, lat[:3], "qg")
            step()

        def fill():
            for m in range(8):
                b, tok = yield from gproject("in2", 24 + m, nn3)
                s = pool.take()
                t = A(lambda e, b=b, s=s: e.activation(s.f, b.ap[:, :], ACT.Copy), tok, *s.free)
                psum.give(b, t)
                g_mla.append((s, t))
            free_ops(nn, P.last())

        vs = {}
        align4()
        for half in range(2):
            bk = [psum.take() for _ in range(4)]
            for k in range(2):
                offs = [block("uv", k, half * 4 + i) for i in range(4)]
                o, wt = offs[0]
                hi, lo, toks = kl[k][:3]
                for j in range(4):
                    b = bk[j]
                    js = slice(j * 128, (j + 1) * 128)
                    rh, rl = whi[:, o:o + 512], wlo[:, o:o + 512]
                    P(lambda e, b=b, js=js, hi=hi, rh=rh, k=k: e.matmul(b.ap[:, :], hi[:, js], rh, start=(k == 0), stop=False),
                      *toks, *wt, b.free)
                    P(lambda e, b=b, js=js, lo=lo, rh=rh: e.matmul(b.ap[:, :], lo[:, js], rh, start=False, stop=False))
                    tok = P(lambda e, b=b, js=js, hi=hi, rl=rl, k=k: e.matmul(b.ap[:, :], hi[:, js], rl, start=False, stop=(k == 1)))
            for j in range(4):
                b, s = bk[j], pool.take()
                q = A if j % 2 else V
                if q is A:
                    t = A(lambda e, b=b, s=s: e.activation(s.f, b.ap[:, :], ACT.Copy), tok, *s.free)
                else:
                    t = V(lambda e, b=b, s=s: e.tensor_copy(s.f, b.ap[:, :]), tok, *s.free)
                psum.give(b, t)
                vs[(j, half)] = (s, t)

        step(30)
        for m in range(8):
            if m == 0:
                two = project2("pr", 0, "pr", 1, three(yr))
            b, tok = two[m] if m < 2 else project("pr", m, three(yr))
            s, t = g_rnn[m]
            t = A(lambda e, s=s: e.activation(s.f, s.f, ACT.Sigmoid), t)
            t = V(lambda e, s=s, b=b: e.tensor_tensor(s.f, s.f, b.ap[:, :], MUL), tok, t)
            psum.give(b, t)
            g_rnn[m] = (s, t)
            tx = x2_tile(m)
        psum.give(rb1, tx)
        free_ops(yr, P.last())
        pool.give(rst, t_lru[-1])
        pool.give(keep_, t_lru[-1])

        lo_turn["mode"] = "G"
        SC2 = 1.0 / math.sqrt(96.0)
        ql3, kl3 = three(ql), three(kl)
        MS, DS = stat_cols(16), stat_cols(16)
        st_free = [None] * 4
        kpair = {}

        def head_qk(h):
            if h % 2 == 0:
                b, tok = yield from gproject("uk", h // 2, kl3)
                for odd in range(2):
                    s = pool.take()
                    rows = slice(64 * odd, 64 * odd + 64)
                    t = A(lambda e, s=s, b=b, rows=rows: e.activation(s.f[rows, :], b.ap[rows, :], ACT.Copy, scale=SC2), tok, *s.free)
                    rr = slice(64, 96) if odd == 0 else slice(0, 32)
                    t2 = V(lambda e, s=s, rr=rr: e.tensor_scalar(s.f[rr, :], kr.f[rr, :], SC2, None, MUL), tkr, *s.free)
                    t3 = V(lambda e, s=s: e.memset(s.f[32:64, :], 0.0), *s.free) if odd else None
                    kpair[odd] = (s, t, t2, t3)
                psum.give(b, t)
            b, tok = yield from gproject("uq", h, ql3)
            q = pool.take()
            t = A(lambda e: e.activation(q.f, b.ap[:, :], ACT.Copy), tok, *q.free)
            rr = slice(64, 96) if h % 2 == 0 else slice(0, 32)
            t = rope(b, q, rr, tbl2, 1, t)
            return q, t, kpair[h % 2]

        def head_scores(h, qk):
            q, tq, (k, *tks) = qk
            K = slice(0, 96) if h % 2 == 0 else slice(0, 128)
            z = 4 * (h % 4)
            for n in (3, 2, 1, 0):
                b = psum.take()
                w = (n + 1) * 128
                P(lambda e, b=b, n=n, w=w: e.matmul(b.ap[:, 0:w], q.f[K, n * 128:(n + 1) * 128], k.f[K, 0:w],
                                                    start=True, stop=True, skip_group_check=True), tq, *tks, b.free)
                tok = P(lambda e, b=b, n=n, w=w: e.matmul(b.ap[:, n * 128:w], identb[:, :], maskb[:, m_diag:m_diag + 128],
                                                          start=False, stop=True, skip_group_check=True))
                mc, dc = stat[:, MS + z + n:MS + z + n + 1], stat[:, DS + z + n:DS + z + n + 1]
                t = V(lambda e, b=b, w=w, mc=mc: e.tensor_reduce(mc, b.ap[:, 0:w], AX, MAX, negate=True), tok, st_free[h % 4])
                p = pool.take()
                te = A(lambda e, p=p, b=b, w=w, mc=mc, dc=dc: e.activation(p.f[:, 0:w], b.ap[:, 0:w], ACT.Exp, bias=mc,
                                                                           accum_out=dc), t, *p.free, st_free[h % 4])
                psum.give(b, te)
                probs2[h][n] = (p, te)
                if n == 0:
                    pool.give(q, tok)
                    pool.give(k, tok)
                else:
                    yield
                if n < 3:
                    norm_row(h, n + 1)
            yield

        def norm_row(h, n):
            p, te = probs2[h][n]
            w = (n + 1) * 128
            dc = stat[:, DS + 4 * (h % 4) + n:DS + 4 * (h % 4) + n + 1]
            t = V(lambda e: e.reciprocal(dc, dc), te)
            t = V(lambda e: e.tensor_scalar(p.f[:, 0:w], p.f[:, 0:w], dc, None, MUL), t)
            probs2[h][n] = (p, t)

        def head_values(h, ob):
            norm_row(h, 0)
            res = probs2.pop(h)
            ps = [res[n] for n in range(4)]
            st_free[h % 4] = ps[0][1]
            rows = slice(64 * (h % 2), 64 * (h % 2) + 64)

            def turn(kb):
                b = psum.take()
                for n in range(kb, 4):
                    p, tp = ps[n]
                    tok = P(lambda e, b=b, p=p, n=n, kb=kb: e.transpose(b.ap[:, n * 128:(n + 1) * 128],
                                                                        p.f[:, kb * 128:(kb + 1) * 128], ident[:, :]), tp, b.free)
                if kb == 3:
                    for p, _ in ps:
                        pool.give(p, tok)
                pt = pool.take()
                c0 = kb * 128
                if kb == 1:
                    t = V(lambda e, b=b, pt=pt, c0=c0: e.tensor_copy(pt.f[:, c0:512], b.ap[:, c0:512]), tok, *pt.free)
                else:
                    t = A(lambda e, b=b, pt=pt, c0=c0: e.activation(pt.f[:, c0:512], b.ap[:, c0:512], ACT.Copy), tok, *pt.free)
                psum.give(b, t)
                return pt, t

            def times(kb, pt, t):
                v, tv = vs[(kb, h // 8)]
                vo = (h % 8) * 64
                c0 = kb * 128
                tok = P(lambda e: e.matmul(ob.ap[rows, c0:512], v.f[:, vo:vo + 64], pt.f[:, c0:512], start=(kb == 0), stop=True,
                                           skip_group_check=True), t, tv, ob.free)
                pool.give(pt, tok)
                return tok

            prev = None
            for kb in range(4):
                cur = turn(kb)
                yield
                if prev is not None:
                    times(kb - 1, *prev)
                    yield
                prev = cur
            t_head[h] = times(3, *prev)
            yield

        ym = []
        ob = None
        t_head = {}
        probs2 = {h: {} for h in range(16)}
        filler = fill()

        def side(h):
            n = 0
            if h < 16:
                gen = head_qk(h)
                while True:
                    try:
                        next(gen)
                    except StopIteration as e:
                        qks[h] = e.value
                        break
                    n += 1
                    yield
            for _ in range(NFILL - n):
                next(filler, None)
                yield

        pm_two = gproject2("pm", 0, "pm", 1, ym, 8)
        qks = {}
        whole(side(0))
        sc = head_scores(0, qks[0])
        for _ in side(1):
            next(sc, None)
        for _ in sc:
            pass
        for h in range(16):
            if h % 2 == 0:
                ob = psum.take()
            work = side(h + 2) if h < 15 else pm_two
            val = head_values(h, ob)
            sc = head_scores(h + 1, qks[h + 1]) if h < 15 else iter(())
            if h == 15:
                whole(filler)
            for c in ORDER if h < 15 else LAST_HEAD:
                next({"V": val, "S": sc, "F": work}[c], None)
            if h < 15:
                for _ in work:
                    pass
            for g_ in (val, sc):
                for _ in g_:
                    raise ValueError("a head's pieces are not done")
            if h % 2:
                h_, l_, th, tl = split(ob.ap[:, :], t_head[h])
                psum.give(ob, tl)
                ym.append(operand(h_, l_, th, tl) + (h_, l_))
        free_ops(ql, P.last())
        free_ops(kl, P.last())
        pool.give(kr, G.last())
        pool.give(rc2, V.last())
        pool.give(rs2, G.last())
        for s, _ in vs.values():
            pool.give(s, P.last())

        for k in range(8):
            s = pool.take()
            hs_[k] = [s, load(s.f, spare[k], hs_[k], *s.free)]
        merged = []
        for m in range(8):
            if m == 0:
                two = whole(pm_two)
            b, tok = two[m] if m < 2 else project("pm", m, three(ym))
            s, t = g_mla[m]
            t = A(lambda e, s=s: e.activation(s.f, s.f, ACT.Sigmoid), t)
            t = V(lambda e, s=s, b=b: e.tensor_tensor(s.f, s.f, b.ap[:, :], MUL), tok, t)
            psum.give(b, t)
            w, tw_ = g_rnn[m]
            t = (V if m == 7 else G)(lambda e, s=s, w=w: e.tensor_tensor(s.f, s.f, w.f, ADD), t, tw_)
            pool.give(w, t)
            h, l, th, tl = split(s.f, t)
            pool.give(s, tl)
            merged.append(operand(h, l, th, tl) + (h, l))
        free_ops(ym, P.last())
        nrm = Norm()
        residual("out2", three(merged), nrm, gate=lambda m: mod[:, 16 + m:17 + m])
        free_ops(merged, P.last())
        rb, trb = nrm.finish(1024, stat_cols(4))
        nn = modulated(rb, trb, 40, 24)
        nn3 = three(nn)


        def conv(mt, got=None):
            b, tok = got or project("up", mt, nn3)
            s = pool.take()
            t = A(lambda e: e.activation(s.f, b.ap[:, :], ACT.Identity, bias=col("fcb", mt), scale=col("fcw", 88 + mt)), tok, *s.free)
            for k in (1, 2):
                t = V(lambda e, k=k: e.scalar_tensor_tensor(out=s.f[:, k:512], in0=b.ap[:, 0:512 - k],
                                                            scalar=col("fcw", (2 - k) * 44 + mt), in1=s.f[:, k:512],
                                                            op0=MUL, op1=ADD), t)
            psum.give(b, t)
            return s, t

        nrm = Norm()
        for half in range(2):
            acts = []
            for m in range(11):
                mt = half * 11 + m
                two = project2("up", mt, "up", 22 + mt, nn3) if mt == 0 else (None, None)
                g_, tg = conv(mt, two[0])
                tg = A(lambda e, g_=g_: e.activation(g_.f, g_.f, ACT.Silu), tg)
                u_s, tu = conv(22 + mt, two[1])
                t = (V if m == 10 else G)(lambda e, g_=g_, u_s=u_s: e.tensor_tensor(g_.f, g_.f, u_s.f, MUL), tg, tu)
                pool.give(u_s, t)
                h, l, th, tl = split(g_.f, t)
                pool.give(g_, tl)
                acts.append(operand(h, l, th, tl) + (h, l))
            if half == 1:
                free_ops(nn, P.last())
            residual("dn", three(acts), nrm if half else None, half * 11, gate=lambda m: mod[:, 40 + m:41 + m])
            free_ops(acts, P.last())

        rb, trb = nrm.finish(1024, stat_cols(4))
        ends = []
        for k in range(8):
            s, ts_ = hs_[k]
            t = V(lambda e, s=s, k=k, rb=rb: e.scalar_tensor_tensor(out=s.f, in0=s.f, scalar=col("gf2", k), in1=rb.ap[:, :],
                                                             op0=MUL, op1=MUL), ts_, trb)
            ends.append(load(out[k], s.f, t))

        for q in (P, A, V, G, S):
            q.count()
        if (len(blocks) + CB - 1) // CB != NCHUNK:
            raise ValueError(f"NCHUNK should be {(len(blocks) + CB - 1) // CB}")
        with nc.Block() as block_:
            @block_.sync
            def _(e):
                S.emit(e)
                for s, n in ends:
                    e.wait_ge(s, n)

            @block_.tensor
            def _(e):
                P.emit(e)

            @block_.scalar
            def _(e):
                A.emit(e)

            @block_.vector
            def _(e):
                V.emit(e)

            @block_.gpsimd
            def _(e):
                G.emit(e)
    return nc


def columns(v, n):
    return np.asarray(v).reshape(n, 128).T


def lay_out(x):
    f = np.float32
    rs = np.concatenate
    invf1 = (np.float32(500000.0) ** (-np.arange(16, dtype=f) * f(2.0) / f(32))).astype(f)
    invf2 = (np.float32(10000.0) ** (-np.arange(16, dtype=f) / f(16))).astype(f)
    parts = dict(
        g_mix=columns(x["g_mix"], 8), g_ffn=columns(x["g_ffn"], 8), g_final=columns(x["g_final"], 8),
        n1=columns(x["norm1_g_2"], 8), n2=columns(x["norm2_g_2"], 8), gf2=columns(x["final_g_2"], 8),
        b_ada=columns(x["b_ada_2"], 48),
        convw=rs([columns(x["conv_w_2"][0, k], 10) for k in range(4)], axis=1), convb=columns(x["conv_b_2"], 10),
        ba=columns(x["b_gate_a_2"], 10), bx=columns(x["b_gate_x_2"], 10), lru=columns(x["lru_param_2"], 10),
        qg=columns(x["q_norm_g_2"], 3), kg=columns(x["kv_norm_g_2"], 2),
        fcw=rs([columns(x["ffn_conv_w_2"][0, k], 44) for k in range(3)], axis=1), fcb=columns(x["ffn_conv_b_2"], 44),
        dskip=columns(x["d_skip"], 4), are=columns(x["a_re"], 16), aim=columns(x["a_im"], 16),
        ldt=columns(np.repeat(x["log_dt"][0], 64), 16),
        if1=np.tile(invf1, 8)[:, None], sg1=np.tile(rs([-np.ones(16, f), np.ones(16, f)]), 4)[:, None],
        if2=np.tile(invf2, 8)[:, None], sg2=np.tile(rs([-np.ones(16, f), np.ones(16, f)]), 4)[:, None])
    small = np.empty((128, NSMALL), f)
    for n, w in SMALL:
        small[:, SOFF[n]:SOFF[n] + w] = parts[n]
    q, k = np.arange(128)[:, None], np.arange(128)[None, :]
    neg = f(-1e30)
    consts = np.zeros((128, 1152), f)
    consts[:, 0:128] = np.eye(128, dtype=f)
    consts[:, 128:256] = np.where(k >= q, f(0), neg)
    consts[:, 256:384] = np.where(k <= q, f(0), neg)
    consts[:, 384:512] = np.where((k <= q) & (k // 32 == q // 32), f(0), neg)
    consts[:, 512:640] = 1
    for h in range(4):
        consts[h, 640 + h * 128:640 + (h + 1) * 128] = 1
    bc = np.empty((128, 2, 16, 16), f)
    cp = np.zeros((2, 4, 128, 4, 128), f)
    for c, (bn, cn) in enumerate((("b_re", "c_re"), ("b_im", "c_im"))):
        for g in range(32):
            i, half = g // 2, g % 2
            bc[64 * half:64 * half + 64, c, i, :] = x[bn][0, g]
            o = (g % 8) * 16
            cp[c, i // 4, 64 * half:64 * half + 64, i % 4, o:o + 16] = np.asarray(x[cn][0, g]).T
    gb = np.zeros((5, 128, 2, 2, 128), f)
    for i in range(10):
        for c, n in enumerate(("w_gate_a_2", "w_gate_x_2")):
            for s in range(2):
                gb[i // 2, 64 * s:64 * s + 64, i % 2, c, 64 * s:64 * s + 64] = x[n][0, 2 * i + s]
    c_ = np.ascontiguousarray
    return dict(
        xT=c_(x["x"][0].T).reshape(8, 128, T), pT=c_(x["p"][0, 0].T).reshape(2, 128, T), small=small, consts=consts,
        pos1=c_(np.broadcast_to(x["positions"], (128, T))), pos2=c_(np.broadcast_to(x["positions_2"], (128, T))),
        cT=c_(np.broadcast_to(x["c_2"], (128, 1024))), wadaT=c_(x["w_ada_2"][0].T).reshape(48, 128, 1024),
        bcmp=bc.reshape(128, 512), cpad=cp.reshape(2, 4, 128, 512), gblk=gb.reshape(5, 128, 512))


def stream(x, blocks):
    f = np.float32
    w2 = x["w_in_2"][0]
    z = lambda r, c: np.zeros((r, c), f)
    kr = w2[:, 1920:1952]
    in2 = np.concatenate([w2[:, :1920], kr, z(1024, 32), kr, z(1024, 32), w2[:, 1952:]], axis=1)
    uq = x["w_uq_2"][0].reshape(384, 16, 96)
    uqp = np.zeros((384, 16, 128), f)
    uqp[:, 0::2, 0:96] = uq[:, 0::2]
    uqp[:, 1::2, 0:32] = uq[:, 1::2, 64:96]
    uqp[:, 1::2, 64:128] = uq[:, 1::2, 0:64]
    ukv = x["w_ukv_2"][0].reshape(256, 16, 128)
    ws = {"in": x["w_in"][0], "ap": x["w_attn_proj"][0], "ga": x["w_glu_a"][0], "gb": x["w_glu_b"][0],
          "out": x["w_out"][0], "fg": x["w_ffn_gate"][0], "fu": x["w_ffn_up"][0], "fd": x["w_ffn_down"][0],
          "pg": x["w_ple_gate"][0], "pp": x["w_ple_proj"][0], "in2": in2, "uq": uqp.reshape(384, 2048),
          "uk": ukv[:, :, :64].reshape(256, 1024), "uv": ukv[:, :, 64:].reshape(256, 1024),
          "pr": x["w_proj_rnn_2"][0], "pm": x["w_proj_mla_2"][0], "out2": x["w_out_2"][0],
          "up": x["w_up_2"][0], "dn": x["w_down_2"][0], "zero": z(128, 128)}
    out = np.zeros((NCHUNK, 128, CB * 128), f)
    for n, (name, k, m) in enumerate(blocks):
        out[n // CB, :, (n % CB) * 128:(n % CB + 1) * 128] = ws[name][k * 128:(k + 1) * 128, m * 128:(m + 1) * 128]
    return out


def kernel(**inputs):
    import concourse.bacc as bacc
    from concourse.bass_utils import run_bass_kernel_spmd

    x = {n: np.asarray(a) for n, a in inputs.items()}
    nc = bacc.Bacc("TRN2", target_bir_lowering=False, num_devices=1)
    arrays = lay_out(x)
    args = {n: nc.dram_tensor(n, a.shape, mybir.dt.from_np(a.dtype), kind="ExternalInput").ap() for n, a in arrays.items()}
    wst = nc.dram_tensor("wst", (NCHUNK, 128, CB * 128), F32, kind="ExternalInput").ap()
    out = nc.dram_tensor("out", (8, 128, T), F32, kind="ExternalOutput").ap()
    spare = nc.dram_tensor("spare", (8, 128, T), F32, kind="Internal").ap()
    blocks = []
    program(nc, blocks, wst, spare=spare, out=out, **args)
    arrays["wst"] = stream(x, blocks)
    r = run_bass_kernel_spmd(nc, [arrays], core_ids=[0])
    got = r.results[0]["out"]
    return np.ascontiguousarray(np.asarray(got).reshape(1024, T).T).reshape(1, T, 1024)
```
